# Optimizing a Trainium2 kernel written in Bass

```python
import math
import jax, jax.numpy as jnp
from jax import lax
import numpy as np

D_MODEL = 1024
BATCH = 1
SEQ = 1024
DEPTH = 2

CHUNK = 64
Q_BLOCK = 128
RMS_EPS = 1e-6
ROPE_BASE = 10000.0

RET_HEADS = 8
RET_QK_DIM = D_MODEL // RET_HEADS
RET_V_DIM = 2 * RET_QK_DIM
RET_QK_WIDTH = RET_HEADS * RET_QK_DIM
RET_WIDTH = RET_HEADS * RET_V_DIM
RET_IN = 2 * RET_QK_WIDTH + 2 * RET_WIDTH

MLA_HEADS = 8
MLA_NOPE = 128
MLA_ROPE = 64
MLA_V = 128
MLA_WIDTH = MLA_HEADS * MLA_V
Q_LORA = 384
KV_LORA = 256
MLA_IN = Q_LORA + MLA_WIDTH


def rmsnorm(x, g):
    xf = x.astype(jnp.float32)
    y = xf * lax.rsqrt(jnp.mean(xf * xf, axis=-1, keepdims=True) + RMS_EPS)
    return (y * g.astype(jnp.float32)).astype(x.dtype)

def rope(x, pos):
    half = x.shape[-1] // 2
    inv = ROPE_BASE ** (-jnp.arange(half, dtype=jnp.float32) / half)
    ang = pos.astype(jnp.float32)[:, None] * inv[None, :]
    cos = jnp.cos(ang)[None, :, None, :].astype(x.dtype)
    sin = jnp.sin(ang)[None, :, None, :].astype(x.dtype)
    x1, x2 = x[..., :half], x[..., half:]
    return jnp.concatenate([x1 * cos - x2 * sin, x1 * sin + x2 * cos], axis=-1)

def retention_decays(dtype):
    log_g = jnp.log(1.0 - jnp.exp2(-5.0 - jnp.arange(RET_HEADS, dtype=jnp.float32)))
    idx = jnp.arange(CHUNK, dtype=jnp.float32)
    dist = jnp.abs(idx[:, None] - idx[None, :])
    inner = jnp.exp(log_g[:, None, None] * dist[None])
    xi = jnp.exp(log_g[:, None] * (idx + 1.0)[None])
    zeta = jnp.exp(log_g[:, None] * (CHUNK - 1.0 - idx)[None])
    g_c = jnp.exp(log_g * CHUNK)
    return inner.astype(dtype), xi.astype(dtype), zeta.astype(dtype), g_c.astype(dtype)

def retention_layer(x, g_pre, w_in, gn_gain, w_out, g_post):
    b, s, _ = x.shape
    nc = s // CHUNK
    h = rmsnorm(x, g_pre)
    proj = h @ w_in
    q, k, v, gate = jnp.split(proj, [RET_QK_WIDTH, 2 * RET_QK_WIDTH, 2 * RET_QK_WIDTH + RET_WIDTH], axis=-1)
    pos = jnp.arange(s)
    q = rope(q.reshape(b, s, RET_HEADS, RET_QK_DIM), pos)
    k = rope(k.reshape(b, s, RET_HEADS, RET_QK_DIM), pos) * (RET_QK_DIM ** -0.5)
    v = v.reshape(b, s, RET_HEADS, RET_V_DIM)

    def to_chunks(t):
        return t.reshape(b, nc, CHUNK, RET_HEADS, t.shape[-1]).transpose(1, 0, 3, 2, 4)

    qc, kc, vc = to_chunks(q), to_chunks(k), to_chunks(v)
    inner_dec, xi, zeta, g_c = retention_decays(x.dtype)
    scores = jnp.einsum('nbhcd,nbhmd->nbhcm', qc, kc) * inner_dec[None, None]
    inner = jnp.einsum('nbhcm,nbhme->nbhce', scores, vc)

    def step(R, inp):
        q_i, k_i, v_i = inp
        cross = jnp.einsum('bhcd,bhde->bhce', q_i, R) * xi[None, :, :, None]
        R = R * g_c[None, :, None, None] + jnp.einsum('bhcd,bhce->bhde', k_i * zeta[None, :, :, None], v_i)
        return R, cross

    R0 = jnp.zeros((b, RET_HEADS, RET_QK_DIM, RET_V_DIM), x.dtype)
    _, cross = lax.scan(step, R0, (qc, kc, vc))
    o = (inner + cross).transpose(1, 0, 3, 2, 4).reshape(b, s, RET_HEADS, RET_V_DIM)
    of = o.astype(jnp.float32)
    mu = jnp.mean(of, axis=-1, keepdims=True)
    var = jnp.mean(jnp.square(of - mu), axis=-1, keepdims=True)
    o = ((of - mu) * lax.rsqrt(var + RMS_EPS)).reshape(b, s, RET_WIDTH) * gn_gain.astype(jnp.float32)
    y = (jax.nn.silu(gate) * o.astype(x.dtype)) @ w_out
    return x + rmsnorm(y, g_post)

def shared_latent_kv(h, g_kv, w_kv_a, g_kv_lat, w_uk, w_uv):
    b, s, _ = h.shape
    src = rmsnorm(h, g_kv)
    a = src @ w_kv_a
    c_kv, k_r = a[..., :KV_LORA], a[..., KV_LORA:]
    c_kv = rmsnorm(c_kv, g_kv_lat)
    k_nope = (c_kv @ w_uk).reshape(b, s, MLA_HEADS, MLA_NOPE)
    v = (c_kv @ w_uv).reshape(b, s, MLA_HEADS, MLA_V)
    k_rope = rope(k_r[:, :, None, :], jnp.arange(s))[:, :, 0, :]
    return k_nope, k_rope, v

def mla_attention(q_nope, q_rope, k_nope, k_rope, v):
    b, s = q_nope.shape[:2]
    nb = s // Q_BLOCK
    qn = q_nope.reshape(b, nb, Q_BLOCK, MLA_HEADS, MLA_NOPE).transpose(1, 0, 2, 3, 4)
    qr = q_rope.reshape(b, nb, Q_BLOCK, MLA_HEADS, MLA_ROPE).transpose(1, 0, 2, 3, 4)
    k_chunk = jnp.arange(s) // CHUNK
    scale = (MLA_NOPE + MLA_ROPE) ** -0.5

    def block(args):
        qn_i, qr_i, i = args
        sc = jnp.einsum('bqhd,bkhd->bhqk', qn_i, k_nope) + jnp.einsum('bqhr,bkr->bhqk', qr_i, k_rope)
        sc = sc.astype(jnp.float32) * scale
        q_chunk = (i * Q_BLOCK + jnp.arange(Q_BLOCK)) // CHUNK
        mask = k_chunk[None, :] <= q_chunk[:, None]
        sc = jnp.where(mask[None, None], sc, -jnp.inf)
        p = jax.nn.softmax(sc, axis=-1).astype(v.dtype)
        return jnp.einsum('bhqk,bkhd->bqhd', p, v)

    out = lax.map(block, (qn, qr, jnp.arange(nb)))
    return out.transpose(1, 0, 2, 3, 4).reshape(b, s, MLA_WIDTH)

def mla_layer(x, g_pre, w_in, g_q_lat, w_uq, w_out, g_post, k_nope, k_rope, v):
    b, s, _ = x.shape
    h = rmsnorm(x, g_pre)
    proj = h @ w_in
    c_q, gate = proj[..., :Q_LORA], proj[..., Q_LORA:]
    q = (rmsnorm(c_q, g_q_lat) @ w_uq).reshape(b, s, MLA_HEADS, MLA_NOPE + MLA_ROPE)
    q_nope = q[..., :MLA_NOPE]
    q_rope = rope(q[..., MLA_NOPE:], jnp.arange(s))
    o = mla_attention(q_nope, q_rope, k_nope, k_rope, v)
    y = (jax.nn.silu(gate) * o) @ w_out
    return x + rmsnorm(y, g_post)

def first_inputs(seed: int = 0) -> dict:
    key = jax.random.key(seed)
    ks = jax.random.split(key, 20)
    n_a = DEPTH // 2
    n_b = DEPTH - n_a
    f32 = jnp.float32

    def w(k, shape, fan_in):
        return jax.random.normal(k, shape, f32) * (fan_in ** -0.5)

    def gain(k, shape):
        return 1.0 + 0.02 * jax.random.normal(k, shape, f32)

    return {
        'x': jax.random.normal(ks[0], (BATCH, SEQ, D_MODEL), f32),
        'g_pre_a': gain(ks[1], (n_a, D_MODEL)),
        'w_in_a': w(ks[2], (n_a, D_MODEL, RET_IN), D_MODEL),
        'gn_gain_a': gain(ks[3], (n_a, RET_WIDTH)),
        'w_out_a': w(ks[4], (n_a, RET_WIDTH, D_MODEL), RET_WIDTH),
        'g_post_a': gain(ks[5], (n_a, D_MODEL)),
        'g_kv': gain(ks[6], (D_MODEL,)),
        'w_kv_a': w(ks[7], (D_MODEL, KV_LORA + MLA_ROPE), D_MODEL),
        'g_kv_lat': gain(ks[8], (KV_LORA,)),
        'w_uk': w(ks[9], (KV_LORA, MLA_HEADS * MLA_NOPE), KV_LORA),
        'w_uv': w(ks[10], (KV_LORA, MLA_WIDTH), KV_LORA),
        'g_pre_b': gain(ks[11], (n_b, D_MODEL)),
        'w_in_b': w(ks[12], (n_b, D_MODEL, MLA_IN), D_MODEL),
        'g_q_lat': gain(ks[13], (n_b, Q_LORA)),
        'w_uq': w(ks[14], (n_b, Q_LORA, MLA_HEADS * (MLA_NOPE + MLA_ROPE)), Q_LORA),
        'w_out_b': w(ks[15], (n_b, MLA_WIDTH, D_MODEL), MLA_WIDTH),
        'g_post_b': gain(ks[16], (n_b, D_MODEL)),
    }

def first_block(x, g_pre_a, w_in_a, gn_gain_a, w_out_a, g_post_a, g_kv, w_kv_a, g_kv_lat, w_uk, w_uv,
              g_pre_b, w_in_b, g_q_lat, w_uq, w_out_b, g_post_b):
    n_a = w_in_a.shape[0]
    h = x
    k_nope = k_rope = v = None
    for layer in range(DEPTH):
        if layer < n_a:
            h = retention_layer(h, g_pre_a[layer], w_in_a[layer], gn_gain_a[layer], w_out_a[layer], g_post_a[layer])
        else:
            if layer == n_a:
                k_nope, k_rope, v = shared_latent_kv(h, g_kv, w_kv_a, g_kv_lat, w_uk, w_uv)
            j = layer - n_a
            h = mla_layer(h, g_pre_b[j], w_in_b[j], g_q_lat[j], w_uq[j], w_out_b[j], g_post_b[j], k_nope, k_rope, v)
    return h


DEPTH_2 = 1

N_MIXERS = 2
D_FF = 4 * D_MODEL
EPS = 1e-6

GLA_HEADS = 4
GLA_DK = D_MODEL // 2
GLA_DV = D_MODEL
GLA_HEAD_K = GLA_DK // GLA_HEADS
GLA_HEAD_V = GLA_DV // GLA_HEADS
GLA_GATE_RANK = 16
GLA_GATE_NORM = 16.0
GLA_CHUNK = 64
GLA_IN = 2 * GLA_DK + 2 * GLA_DV + GLA_GATE_RANK

FOX_HEADS = 16
FOX_HEAD_DIM = D_MODEL // FOX_HEADS
FOX_BLOCK = 128
FOX_IN = 3 * D_MODEL + FOX_HEADS + D_MODEL


def rms_norm(x, g):
    xf = x.astype(jnp.float32)
    y = xf * lax.rsqrt(jnp.mean(xf * xf, axis=-1, keepdims=True) + EPS)
    return (y * g.astype(jnp.float32)).astype(x.dtype)

def sqrelu_mlp(h, w1, w2):
    return jnp.square(jax.nn.relu(h @ w1)) @ w2

def gla_mixer(h, w_in, w_gk_up, b_gk, g_onorm, w_out):
    B, S, _ = h.shape
    C = GLA_CHUNK
    N = S // C
    proj = h @ w_in
    q, k, v, r, gk_low = jnp.split(
        proj, [GLA_DK, 2 * GLA_DK, 2 * GLA_DK + GLA_DV, 2 * GLA_DK + 2 * GLA_DV], axis=-1)
    log_a = jax.nn.log_sigmoid((gk_low @ w_gk_up + b_gk).astype(jnp.float32)) / GLA_GATE_NORM

    def to_chunks(t, dh):
        return t.astype(jnp.float32).reshape(B, N, C, GLA_HEADS, dh).transpose(1, 0, 3, 2, 4)

    qc = to_chunks(q, GLA_HEAD_K) * (GLA_HEAD_K ** -0.5)
    kc = to_chunks(k, GLA_HEAD_K)
    vc = to_chunks(v, GLA_HEAD_V)
    gc = to_chunks(log_a, GLA_HEAD_K)
    causal = jnp.tril(jnp.ones((C, C), dtype=bool))

    def step(state, inp):
        qb, kb, vb, gb = inp
        b = jnp.cumsum(gb, axis=-2)
        o_inter = jnp.einsum('bhck,bhkv->bhcv', qb * jnp.exp(b), state)
        diff = b[:, :, :, None, :] - b[:, :, None, :, :]
        decay = jnp.exp(jnp.where(causal[:, :, None], diff, -jnp.inf))
        attn = jnp.einsum('bhik,bhjk,bhijk->bhij', qb, kb, decay)
        o_intra = jnp.einsum('bhij,bhjv->bhiv', attn, vb)
        b_last = b[:, :, -1:, :]
        k_dec = kb * jnp.exp(b_last - b)
        state = state * jnp.exp(b_last[:, :, 0, :])[..., None] + jnp.einsum('bhck,bhcv->bhkv', k_dec, vb)
        return state, o_inter + o_intra

    state0 = jnp.zeros((B, GLA_HEADS, GLA_HEAD_K, GLA_HEAD_V), jnp.float32)
    _, o = lax.scan(step, state0, (qc, kc, vc, gc))
    o = o.transpose(1, 0, 3, 2, 4).reshape(B, S, GLA_HEADS, GLA_HEAD_V).astype(h.dtype)
    o = rms_norm(o, g_onorm).reshape(B, S, GLA_DV)
    return (o * jax.nn.silu(r)) @ w_out

def fox_mixer(h, w_in, b_f, g_q, g_k, w_out):
    B, S, _ = h.shape
    H, Dh = FOX_HEADS, FOX_HEAD_DIM
    nb = S // FOX_BLOCK
    proj = h @ w_in
    q, k, v, f_logit, o_gate = jnp.split(
        proj, [D_MODEL, 2 * D_MODEL, 3 * D_MODEL, 3 * D_MODEL + H], axis=-1)
    q = rms_norm(q.reshape(B, S, H, Dh), g_q).transpose(0, 2, 1, 3)
    k = rms_norm(k.reshape(B, S, H, Dh), g_k).transpose(0, 2, 1, 3)
    v = v.reshape(B, S, H, Dh).transpose(0, 2, 1, 3)
    log_f = jax.nn.log_sigmoid((f_logit + b_f).astype(jnp.float32))
    c = jnp.cumsum(log_f, axis=1).transpose(0, 2, 1)
    scale = Dh ** -0.5
    key_pos = jnp.arange(S)
    q_blocks = q.reshape(B, H, nb, FOX_BLOCK, Dh).transpose(2, 0, 1, 3, 4)
    c_blocks = c.reshape(B, H, nb, FOX_BLOCK).transpose(2, 0, 1, 3)

    def attend(args):
        qb, cq, blk = args
        s = jnp.einsum('bhqd,bhkd->bhqk', qb, k).astype(jnp.float32) * scale
        s = s + cq[..., None] - c[:, :, None, :]
        q_pos = blk * FOX_BLOCK + jnp.arange(FOX_BLOCK)
        s = jnp.where(key_pos[None, :] <= q_pos[:, None], s, -jnp.inf)
        p = jax.nn.softmax(s, axis=-1)
        return jnp.einsum('bhqk,bhkd->bhqd', p.astype(v.dtype), v)

    o = lax.map(attend, (q_blocks, c_blocks, jnp.arange(nb)))
    o = o.transpose(1, 0, 3, 2, 4).reshape(B, S, D_MODEL)
    return (o * jax.nn.sigmoid(o_gate)) @ w_out

def second_inputs(seed: int = 0) -> dict:
    key = jax.random.key(seed)
    ks = jax.random.split(key, 24)
    f32 = jnp.float32
    nrm = lambda k, shape, fan_in: jax.random.normal(k, shape, f32) * (fan_in ** -0.5)
    gain = lambda k, n: 1.0 + 0.05 * jax.random.normal(k, (n,), f32)
    return {
        "x": jax.random.normal(ks[0], (BATCH, SEQ, D_MODEL), f32),
        "l0_norm_mix": gain(ks[1], D_MODEL),
        "l0_w_in": nrm(ks[2], (D_MODEL, GLA_IN), D_MODEL),
        "l0_w_gk_up": nrm(ks[3], (GLA_GATE_RANK, GLA_DK), GLA_GATE_RANK),
        "l0_b_gk": 0.1 * jax.random.normal(ks[4], (GLA_DK,), f32),
        "l0_g_onorm": gain(ks[5], GLA_HEAD_V),
        "l0_w_out": nrm(ks[6], (GLA_DV, D_MODEL), GLA_DV),
        "l0_norm_ffn": gain(ks[7], D_MODEL),
        "l0_w_ff1": nrm(ks[8], (D_MODEL, D_FF), D_MODEL),
        "l0_w_ff2": nrm(ks[9], (D_FF, D_MODEL), D_FF),
        "l1_norm_mix": gain(ks[10], D_MODEL),
        "l1_w_in": nrm(ks[11], (D_MODEL, FOX_IN), D_MODEL),
        "l1_b_f": jax.random.uniform(ks[12], (FOX_HEADS,), f32, 1.0, 5.0),
        "l1_g_q": gain(ks[13], FOX_HEAD_DIM),
        "l1_g_k": gain(ks[14], FOX_HEAD_DIM),
        "l1_w_out": nrm(ks[15], (D_MODEL, D_MODEL), D_MODEL),
        "l1_norm_ffn": gain(ks[16], D_MODEL),
        "l1_w_ff1": nrm(ks[17], (D_MODEL, D_FF), D_MODEL),
        "l1_w_ff2": nrm(ks[18], (D_FF, D_MODEL), D_FF),
        "final_norm": gain(ks[19], D_MODEL),
    }

def second_block(x, l0_norm_mix, l0_w_in, l0_w_gk_up, l0_b_gk, l0_g_onorm, l0_w_out,
              l0_norm_ffn, l0_w_ff1, l0_w_ff2,
              l1_norm_mix, l1_w_in, l1_b_f, l1_g_q, l1_g_k, l1_w_out,
              l1_norm_ffn, l1_w_ff1, l1_w_ff2, final_norm):
    layers = (
        (l0_norm_mix, (l0_w_in, l0_w_gk_up, l0_b_gk, l0_g_onorm, l0_w_out), l0_norm_ffn, l0_w_ff1, l0_w_ff2),
        (l1_norm_mix, (l1_w_in, l1_b_f, l1_g_q, l1_g_k, l1_w_out), l1_norm_ffn, l1_w_ff1, l1_w_ff2),
    )
    mixers = (gla_mixer, fox_mixer)
    for i in range(DEPTH_2):
        norm_mix, mix_params, norm_ffn, w1, w2 = layers[i]
        x = x + mixers[i % N_MIXERS](rms_norm(x, norm_mix), *mix_params)
        x = x + sqrelu_mlp(rms_norm(x, norm_ffn), w1, w2)
    return rms_norm(x, final_norm)


def setup_inputs(seed=0):
    out = dict(first_inputs(seed))
    for name, value in second_inputs(seed + 1).items():
        if name != "x":
            out[name + "_2"] = value
    return out


def reference(
    x, g_pre_a, w_in_a, gn_gain_a, w_out_a, g_post_a, g_kv, w_kv_a, g_kv_lat, w_uk, w_uv,
    g_pre_b, w_in_b, g_q_lat, w_uq, w_out_b, g_post_b, l0_norm_mix_2, l0_w_in_2, l0_w_gk_up_2,
    l0_b_gk_2, l0_g_onorm_2, l0_w_out_2, l0_norm_ffn_2, l0_w_ff1_2, l0_w_ff2_2, l1_norm_mix_2,
    l1_w_in_2, l1_b_f_2, l1_g_q_2, l1_g_k_2, l1_w_out_2, l1_norm_ffn_2, l1_w_ff1_2, l1_w_ff2_2,
    final_norm_2,
):
    x = first_block(
        x, g_pre_a, w_in_a, gn_gain_a, w_out_a, g_post_a, g_kv, w_kv_a, g_kv_lat, w_uk, w_uv,
        g_pre_b, w_in_b, g_q_lat, w_uq, w_out_b, g_post_b,
    )
    return second_block(
        x, l0_norm_mix_2, l0_w_in_2, l0_w_gk_up_2, l0_b_gk_2, l0_g_onorm_2, l0_w_out_2,
        l0_norm_ffn_2, l0_w_ff1_2, l0_w_ff2_2, l1_norm_mix_2, l1_w_in_2, l1_b_f_2, l1_g_q_2,
        l1_g_k_2, l1_w_out_2, l1_norm_ffn_2, l1_w_ff1_2, l1_w_ff2_2, final_norm_2,
    )


_drawn_inputs = setup_inputs


def setup_inputs(seed=0):
    import zlib

    import numpy as np

    out = dict(_drawn_inputs(seed))
    spreads = {}
    factors = {'g_kv': 3.085,
     'g_kv_lat': 2.745,
     'g_pre_b': 2.803,
     'g_q_lat': 4.146,
     'g_post_b': 4.077,
     'l0_b_gk_2': 3.667,
     'l0_g_onorm_2': 9.0,
     'l0_norm_ffn_2': 3.868}
    for name, (base, spread) in spreads.items():
        noise = np.random.default_rng([zlib.crc32(name.encode()), seed]).standard_normal(out[name].shape)
        drawn = base * np.exp(spread * noise) if base else spread * noise
        out[name] = __import__('jax').numpy.asarray(drawn.astype(out[name].dtype))
    for name, factor in factors.items():
        out[name] = (out[name] * factor).astype(out[name].dtype)
    return out
```

```python
from contextlib import ExitStack

import concourse.bass as bass
import numpy as np
from concourse import mybir

F32 = mybir.dt.float32
F32R = mybir.dt.float32r
BF16 = mybir.dt.bfloat16
U32 = mybir.dt.uint32
ALU = mybir.AluOpType
ACT = mybir.ActivationFunctionType
AX_X = mybir.AxisListType.X
ds = bass.ds

P = 128
SEQ = 1024
DM = 1024
NT = SEQ // P
KT = DM // P
HALF = 512
EPS = 1e-6

RET_HEADS = 8
RQK = DM // RET_HEADS
RV = 2 * RQK
RET_CHUNK = 64
RET_W = RET_HEADS * RV

MLA_HEADS = 8
NOPE, MROPE, MV = 128, 64, 128
Q_LORA, KV_LORA = 384, 256

GLA_HEADS = 4
GK = 128
GV = 256
GRANK = 16
GLA_LEVELS = 7
D_FF = 4 * DM


def shape_constants():
    f = np.float32
    out = {}
    out["identity"] = np.eye(P, dtype=f)

    def rotary(width):
        half = width // 2
        inv = (f(10000.0) ** (-np.arange(half, dtype=f) / f(half))).astype(f)
        ang = np.arange(SEQ, dtype=f)[:, None] * inv[None, :]
        lay = lambda a: np.ascontiguousarray(a.astype(f).reshape(NT, P, half).transpose(1, 0, 2))
        return lay(np.cos(ang)), lay(np.sin(ang))

    out["cos_ret"], out["sin_ret"] = rotary(RQK)
    out["cos_mla"], out["sin_mla"] = rotary(MROPE)
    log_g = np.log(1.0 - np.exp2(-5.0 - np.arange(RET_HEADS, dtype=np.float64)))
    pos = np.arange(P)
    m, c = pos[:, None], pos[None, :]
    sees = (m // RET_CHUNK) <= (c // RET_CHUNK)
    dec = np.where(sees[None], np.exp(log_g[:, None, None] * (np.abs(m - c) - (c + 1))[None]), 0.0) * RQK ** -0.5
    out["ret_decay"] = np.ascontiguousarray(dec.transpose(1, 0, 2).astype(f))
    out["ret_xi"] = np.exp(log_g[None, :] * (pos[:, None] + 1)).astype(f)
    out["ret_zeta"] = (np.exp(log_g[None, :] * (P - 1 - pos[:, None])) * RQK ** -0.5).astype(f)
    out["gla_masks"] = gla_masks()
    out["ret_carry"] = np.broadcast_to(np.exp(log_g * P)[None, :], (P, RET_HEADS)).astype(f).copy()
    return out


def columns(vector):
    return np.ascontiguousarray(vector.reshape(-1, P).T)


def retention_columns(w):
    w = w.reshape(KT, P, -1)
    parts = [w[:, :, 0:DM].reshape(KT, P, RET_HEADS, RQK), w[:, :, DM:2 * DM].reshape(KT, P, RET_HEADS, RQK),
             w[:, :, 2 * DM:2 * DM + RET_W].reshape(KT, P, RET_HEADS, RV),
             w[:, :, 2 * DM + RET_W:].reshape(KT, P, RET_HEADS, RV)]
    return np.ascontiguousarray(np.concatenate(parts, axis=3).transpose(2, 1, 0, 3))


def wait_alone(eng):
    eng.nop(nofuse=True)


def ff1_chunks(w):
    return np.ascontiguousarray(w.reshape(KT, P, D_FF // HALF, HALF).transpose(2, 1, 0, 3))


def row_tiles(w):
    return np.ascontiguousarray(w.reshape(-1, P, w.shape[1]).transpose(1, 0, 2))


def latent_columns(w_kv_a, w_in):
    return row_tiles(np.concatenate([w_kv_a, w_in[:, :Q_LORA]], axis=1))


def gate_units(w_in):
    return np.ascontiguousarray(w_in[:, Q_LORA:].reshape(KT, P, 2, HALF).transpose(2, 1, 0, 3))


def head_weights(w_uk, w_uq):
    uk = w_uk.reshape(2, P, MLA_HEADS, NOPE)
    uq = w_uq.reshape(3, P, MLA_HEADS, NOPE + MROPE)[:, :, :, :NOPE]
    return np.ascontiguousarray(np.concatenate([uk, uq], axis=0).transpose(2, 1, 0, 3))


def rotary_columns(w_uq):
    w = w_uq.reshape(Q_LORA, MLA_HEADS, NOPE + MROPE)[:, :, NOPE:]
    return row_tiles(np.ascontiguousarray(w).reshape(Q_LORA, MLA_HEADS * MROPE))


def clear_semaphores(nc, sems):
    numbers = sorted(s.num for s in sems)
    assert numbers == list(range(numbers[0], numbers[-1] + 1))
    with nc.Block() as block:
        @block.gpsimd
        def _(pool):
            pool.sem_clear(range(numbers[0], numbers[-1] + 1))


def retention_heads(nc, x, g_pre, w_in, con, ident, neghalf, gated):
    with ExitStack() as ctx:
        def sb(name, shape, dt=F32):
            return ctx.enter_context(nc.sbuf_tensor("ra_" + name, shape, dt))

        def bank(name):
            return ctx.enter_context(nc.psum_tensor("ra_" + name, [P, HALF], F32))

        sems = []

        def sem(name):
            sems.append(ctx.enter_context(nc.semaphore("ra_" + name)))
            return sems[-1]

        QKV = 2 * RQK + RV
        WC = QKV + RV
        xh = sb("xh", [P, KT, SEQ], F32R)
        xl = sb("xl", [P, KT, SEQ], F32R)
        wh = sb("wh", [P, 2, KT, WC], F32R)
        wl = sb("wl", [P, 2, KT, WC], F32R)
        raw = sb("raw", [P, 2, 2, WC])
        xin = sb("xin", [P, 2, DM])
        gain = sb("gain", [P, KT])
        cos = sb("cos", [P, NT, RQK // 2])
        sin = sb("sin", [P, NT, RQK // 2])
        decay = sb("decay", [P, RET_HEADS, P])
        xi = sb("xi", [P, RET_HEADS])
        zeta = sb("zeta", [P, RET_HEADS])
        carry = sb("carry", [P, RET_HEADS])
        qkv = sb("qkv", [P, 2, QKV])
        rot = sb("rot", [P, 2, 2, RQK])
        rtmp = sb("rtmp", [P, 2, RQK])
        kz = sb("kz", [P, 2, RQK])
        qkT = sb("qkT", [P, 2, 2, P])
        sT = sb("sT", [P, P])
        R = sb("R", [P, RV])
        sg = sb("sg", [P, 4, RV])
        oS = sb("oS", [P, 2, RV])
        bn = sb("bn", [P, 6])
        mv = sb("mv", [P, 2, 2])
        rstd = sb("rstd", [P, 2, 2])
        ss = sb("ss", [P, NT])
        rx = sb("rx", [P, 2, NT])

        qkv_ps = [bank("qkv_ps0"), bank("qkv_ps1")]
        x_ps, gate_ps, T_ps, s_ps, o_ps, k_ps = (
            bank(n) for n in ("x_ps", "gate_ps", "T_ps", "s_ps", "o_ps", "k_ps"))

        con_in = sem("con_in")
        x_in = [sem("x_in0"), sem("x_in1")]
        raw_in = [sem("raw_in0"), sem("raw_in1")]
        g_out = [sem(f"g_out{i}") for i in range(4)]
        (ss_done, rms_part, rms_done, xn_done, xT_mm, xh_done, xl_done, wh_done, wl_done, qkv_mm, qkv_copied,
         rot_part, rot_done, kz_done, T_mm, T_copied, s_mm, sT_done, attend_mm, R_done, o_copied, gate_mm,
         silu_done, bn_part, mv_done, rstd_part, rstd_done, norm_part, G_done) = (sem(n) for n in (
            "ss_done rms_part rms_done xn_done xT_mm xh_done xl_done wh_done wl_done qkv_mm qkv_copied "
            "rot_part rot_done kz_done T_mm T_copied s_mm sT_done attend_mm R_done o_copied gate_mm "
            "silu_done bn_part mv_done rstd_part rstd_done norm_part G_done").split())
        block = ctx.enter_context(nc.Block())
        LAST = RET_HEADS * NT
        N_CON = 7

        @block.sync
        def _(sp):
            def load_x(t):
                if t >= 2:
                    sp.wait_ge(xT_mm, 2 * (t - 1))
                sp.dma_start(xin[:, t % 2, :], x[t * P:(t + 1) * P, :]).then_inc(x_in[t % 2], 16)

            def load_raw(h, kt):
                slot = kt // 2 % 2
                sp.dma_start(raw[:, slot, :, :], w_in[ds(h, 1), :, kt:kt + 2, :].rearrange("a p k n -> p (a k) n"))\
                  .then_inc(raw_in[slot], 16)

            def store(s, h, t):
                sp.wait_ge(G_done, s + 1)
                sp.dma_start(gated[t * P:(t + 1) * P, ds(h * RV, RV)], sg[:, t % 4, :]).then_inc(g_out[t % 4], 16)

            def head(h, first, more):
                for t in range(NT):
                    if first and t + 2 < NT:
                        load_x(t + 2)
                    if more and t % 2 == 0:
                        sp.wait_ge(wl_done, KT * h + KT + t - 2)
                        load_raw(h + 1, t)
                    if t >= 3:
                        store(h * NT + t - 3, h, t - 3)
                    elif not first:
                        store(h * NT + t - 3, h - 1, NT + t - 3)

            load_x(0)
            sp.dma_start(gain[:], g_pre).then_inc(con_in, 16)
            for dst, name in ((cos, "cos_ret"), (sin, "sin_ret"), (decay, "ret_decay"), (xi, "ret_xi"),
                              (zeta, "ret_zeta"), (carry, "ret_carry")):
                sp.dma_start(dst[:], con[name]).then_inc(con_in, 16)
            load_x(1)
            for kt in range(0, KT, 2):
                if kt >= 4:
                    sp.wait_ge(wl_done, kt - 2)
                load_raw(0, kt)
            head(0, True, True)
            with sp.Fori(1, RET_HEADS - 1) as h:
                head(h, False, True)
            head(RET_HEADS - 1, False, False)
            for t in range(NT - 3, NT):
                store(LAST - NT + t, RET_HEADS - 1, t)
            for slot in range(4):
                sp.wait_ge(g_out[slot], 16 * LAST // 4)

        @block.scalar
        def _(act):
            def square_x(t):
                act.wait_ge(x_in[t % 2], 16 * (t // 2 + 1))
                act.activation(xl[:, :, t * P:(t + 1) * P], xin[:, t % 2, :].rearrange("p (k n) -> p k n", k=KT), ACT.Square, accum_out=ss[:, t:t + 1]).then_inc(ss_done, 1)

            def x_upper(t, half):
                act.wait_ge(xT_mm, 2 * t + half + 1)
                act.activation(xh[:, 4 * half:4 * half + 4, t * P:(t + 1) * P],
                               x_ps[:, :].rearrange("p (k n) -> p k n", k=4), ACT.Copy).then_inc(xh_done, 1)

            def w_upper(h, slot, kt):
                act.wait_ge(raw_in[kt // 2 % 2], 16 * (h * 2 + kt // 4 + 1))
                wait_alone(act)
                act.activation(wh[:, ds(slot, 1), kt, :].rearrange("p a n -> p (a n)"), raw[:, kt // 2 % 2, kt % 2, :],
                               ACT.Copy, scale=gain[:, kt:kt + 1]).then_inc(wh_done, 1)

            def step(s, h, t, older):
                hp = h if t >= 2 else h - 1
                if older >= 1:
                    act.wait_ge(T_mm, s)
                    act.activation(qkT[:, (t - 1) % 2, :, :], T_ps[:, 0:2 * P].rearrange("p (a n) -> p a n", a=2),
                                   ACT.Copy).then_inc(T_copied, 1)
                if older >= 2:
                    act.wait_ge(attend_mm, s - 1)
                act.wait_ge(qkv_mm, s + 1)
                act.activation(qkv[:, t % 2, :], qkv_ps[t % 2][:, :], ACT.Copy).then_inc(qkv_copied, 1)
                if older >= 2:
                    if older >= 4:
                        act.wait_ge(G_done, s - 3)
                    wait_alone(act)
                    act.activation(oS[:, t % 2, :], o_ps[:, 0:RV], ACT.Copy, scale=xi[:, ds(hp, 1)]).then_inc(o_copied, 1)

            def silu(s, h, t, older):
                act.wait_ge(gate_mm, s + 1)
                if older >= 4:
                    act.wait_ge(g_out[t % 4], 16 * (h * (NT // 4) + t // 4))
                act.activation(sg[:, t % 4, :], gate_ps[:, 0:RV], ACT.Silu).then_inc(silu_done, 1)

            act.wait_ge(con_in, 16 * N_CON)
            square_x(0)
            for kt in range(4):
                w_upper(0, 0, kt)
            x_upper(0, 0)
            x_upper(0, 1)
            square_x(1)
            for kt in range(4, KT):
                w_upper(0, 0, kt)
            for t in range(NT):
                if t + 1 < NT:
                    x_upper(t + 1, 0)
                step(t, 0, t, t)
                if t + 1 < NT:
                    x_upper(t + 1, 1)
                silu(t, 0, t, t)
                if t + 2 < NT:
                    square_x(t + 2)
                w_upper(1, 1, t)

            def head(h, more):
                for t in range(NT):
                    step(h * NT + t, h, t, 4)
                    silu(h * NT + t, h, t, 4)
                    if more:
                        if t == 0:
                            act.wait_ge(gate_mm, NT * h)
                        w_upper(h + 1, (h + 1) % 2, t)

            with act.Fori(1, RET_HEADS - 1) as h:
                head(h, True)
            head(RET_HEADS - 1, False)
            act.wait_ge(T_mm, LAST)
            act.activation(qkT[:, 1, :, :], T_ps[:, 0:2 * P].rearrange("p (a n) -> p a n", a=2),
                           ACT.Copy).then_inc(T_copied, 1)
            for s in (LAST, LAST + 1):
                act.wait_ge(attend_mm, s - 1)
                act.wait_ge(G_done, s - 3)
                act.activation(oS[:, s % 2, :], o_ps[:, 0:RV], ACT.Copy,
                               scale=xi[:, RET_HEADS - 1:RET_HEADS]).then_inc(o_copied, 1)

        @block.gpsimd
        def _(pool):
            def rms_x(t):
                pool.wait_ge(ss_done, t + 1)
                pool.tensor_scalar(rx[:, 0, t:t + 1], ss[:, t:t + 1], 1.0 / DM, EPS, ALU.mult, ALU.add).then_inc(rms_part, 1)
                pool.wait_ge(rms_part, t + 1)
                pool.tensor_tensor(rx[:, 1, t:t + 1], rx[:, 0, t:t + 1], neghalf[:], ALU.pow).then_inc(rms_done, 1)

            def rotate(s, h, t, older):
                pool.wait_ge(qkv_copied, s + 1)
                if older >= 2:
                    pool.wait_ge(T_mm, s - 1)
                x = qkv[:, t % 2, 0:2 * RQK].rearrange("p (a u n) -> p a u n", a=2, u=2)
                r = rot[:, t % 2, :, :].rearrange("p a (u n) -> p a u n", u=2)
                tmp = rtmp[:, :, :].rearrange("p a (u n) -> p a u n", u=2)
                c = cos[:, t:t + 1, :].broadcast_to([P, 2, RQK // 2])
                n = sin[:, t:t + 1, :].broadcast_to([P, 2, RQK // 2])
                pool.tensor_tensor(r[:, :, 0, :], x[:, :, 0, :], c, ALU.mult)
                pool.tensor_tensor(r[:, :, 1, :], x[:, :, 1, :], c, ALU.mult)
                pool.tensor_tensor(tmp[:, :, 0, :], x[:, :, 1, :], n, ALU.mult)
                pool.tensor_tensor(tmp[:, :, 1, :], x[:, :, 0, :], n, ALU.mult).then_inc(rot_part, 1)
                pool.wait_ge(rot_part, 2 * s + 1)
                pool.tensor_tensor(r[:, :, 0, :], r[:, :, 0, :], tmp[:, :, 0, :], ALU.subtract)
                pool.tensor_tensor(r[:, :, 1, :], r[:, :, 1, :], tmp[:, :, 1, :], ALU.add).then_inc(rot_part, 1)
                pool.wait_ge(rot_part, 2 * s + 2)
                wait_alone(pool)
                pool.tensor_tensor(kz[:, t % 2, :], rot[:, t % 2, 1, :], zeta[:, ds(h, 1)].broadcast_to([P, RQK]),
                                   ALU.mult).then_inc(kz_done, 1)

            def deviation(s, t):
                pool.wait_ge(mv_done, s + 1)
                wait_alone(pool)
                pool.tensor_scalar(rstd[:, t % 2, 0:1], mv[:, t % 2, 1:2], EPS, None, ALU.add).then_inc(rstd_part, 1)
                pool.wait_ge(rstd_part, s + 1)
                pool.tensor_tensor(rstd[:, t % 2, 1:2], rstd[:, t % 2, 0:1], neghalf[:], ALU.pow).then_inc(rstd_done, 1)

            pool.wait_ge(con_in, 16 * N_CON)
            rms_x(0)
            rms_x(1)
            for t in range(NT):
                rotate(t, 0, t, t)
                if t + 2 < NT:
                    rms_x(t + 2)
                if t >= 2:
                    deviation(t - 2, t)
            with pool.Fori(1, RET_HEADS) as h:
                for t in range(NT):
                    rotate(h * NT + t, h, t, 2)
                    deviation(h * NT + t - 2, t)
            deviation(LAST - 2, 0)
            deviation(LAST - 1, 1)

        @block.vector
        def _(dve):
            def scale_x(t):
                dve.wait_ge(rms_done, t + 1)
                dve.tensor_scalar(xin[:, t % 2, :], xin[:, t % 2, :], rx[:, 1, t:t + 1], None, ALU.mult).then_inc(xn_done, 1)

            def x_lower(t, half):
                dve.wait_ge(xh_done, 2 * t + half + 1)
                dve.tensor_tensor(xl[:, 4 * half:4 * half + 4, t * P:(t + 1) * P],
                                  x_ps[:, :].rearrange("p (k n) -> p k n", k=4),
                                  xh[:, 4 * half:4 * half + 4, t * P:(t + 1) * P].bitcast(F32),
                                  ALU.subtract).then_inc(xl_done, 1)

            def w_lower(h, slot, kt):
                dve.wait_ge(wh_done, KT * h + kt + 1)
                dve.scalar_tensor_tensor(wl[:, ds(slot, 1), kt, :].rearrange("p a n -> p (a n)"),
                                         raw[:, kt // 2 % 2, kt % 2, :], gain[:, kt:kt + 1],
                                         wh[:, ds(slot, 1), kt, :].rearrange("p a n -> p (a n)").bitcast(F32),
                                         ALU.mult, ALU.subtract).then_inc(wl_done, 1)

            def norm_and_gate(s, h, t):
                dve.wait_ge(rstd_done, s + 1)
                dve.tensor_scalar(oS[:, t % 2, :], oS[:, t % 2, :], mv[:, t % 2, 0:1], rstd[:, t % 2, 1:2],
                                  ALU.subtract, ALU.mult).then_inc(norm_part, 1)
                dve.wait_ge(norm_part, s + 1)
                dve.wait_ge(silu_done, s + 1)
                dve.tensor_tensor(sg[:, t % 4, :], oS[:, t % 2, :], sg[:, t % 4, :], ALU.mult).then_inc(G_done, 1)

            def carry_state(s, h, t):
                dve.wait_ge(attend_mm, s + 1)
                if t == 0:
                    dve.tensor_copy(R[:, :], k_ps[:, 0:RV]).then_inc(R_done, 1)
                else:
                    dve.wait_ge(R_done, s)
                    dve.scalar_tensor_tensor(R[:, :], R[:, :], carry[:, ds(h, 1)], k_ps[:, 0:RV],
                                             ALU.mult, ALU.add).then_inc(R_done, 1)

            def moments(s, t):
                dve.wait_ge(o_copied, s + 1)
                dve.bn_stats(bn[:, :], oS[:, t % 2, :]).then_inc(bn_part, 1)
                dve.wait_ge(bn_part, s + 1)
                wait_alone(dve)
                dve.bn_aggr(mv[:, t % 2, :], bn[:, :]).then_inc(mv_done, 1)

            def decay_scores(s, h):
                dve.wait_ge(s_mm, s + 1)
                dve.tensor_tensor(sT[:, :], s_ps[:, 0:P], decay[:, ds(h, 1), :].rearrange("p a n -> p (a n)"),
                                  ALU.mult).then_inc(sT_done, 1)

            dve.wait_ge(con_in, 16 * N_CON)
            scale_x(0)
            for kt in range(4):
                w_lower(0, 0, kt)
            x_lower(0, 0)
            x_lower(0, 1)
            scale_x(1)
            for kt in range(4, KT):
                w_lower(0, 0, kt)
            for t in range(NT):
                if t + 1 < NT:
                    x_lower(t + 1, 0)
                if t >= 3:
                    norm_and_gate(t - 3, 0, t - 3)
                if t >= 2:
                    carry_state(t - 2, 0, t - 2)
                    moments(t - 2, t - 2)
                if t + 1 < NT:
                    x_lower(t + 1, 1)
                if t + 2 < NT:
                    scale_x(t + 2)
                w_lower(1, 1, t)
                if t >= 1:
                    decay_scores(t - 1, 0)

            def head(h, more):
                for t in range(NT):
                    s = h * NT + t
                    h1, h2, h3 = (h if t >= n else h - 1 for n in (1, 2, 3))
                    norm_and_gate(s - 3, h3, (t - 3) % NT)
                    carry_state(s - 2, h2, (t - 2) % NT)
                    moments(s - 2, (t - 2) % NT)
                    if more:
                        w_lower(h + 1, (h + 1) % 2, t)
                    decay_scores(s - 1, h1)

            with dve.Fori(1, RET_HEADS - 1) as h:
                head(h, True)
            h = RET_HEADS - 1
            head(h, False)
            norm_and_gate(LAST - 3, h, NT - 3)
            moments(LAST - 2, NT - 2)
            carry_state(LAST - 2, h, NT - 2)
            decay_scores(LAST - 1, h)
            norm_and_gate(LAST - 2, h, NT - 2)
            moments(LAST - 1, NT - 1)
            norm_and_gate(LAST - 1, h, NT - 1)

        @block.tensor
        def _(pe):
            def transpose_x(t, half):
                if half == 0:
                    pe.wait_ge(xn_done, t + 1)
                if t or half:
                    pe.wait_ge(xl_done, 2 * t + half)
                for k in range(4):
                    last = pe.transpose(x_ps[:, k * P:(k + 1) * P],
                                        xin[:, t % 2, (4 * half + k) * P:(4 * half + k + 1) * P], ident[:])
                last.then_inc(xT_mm, 1)

            def project(out, t, slot, at, n, done):
                for kt in range(KT):
                    for i, (a, b) in enumerate(((xl, wh), (xh, wl), (xh, wh))):
                        last = pe.matmul(out, a[:, kt, t * P:(t + 1) * P],
                                         b[:, ds(slot, 1), kt, at:at + n].rearrange("p a n -> p (a n)"),
                                         start=(kt == 0 and i == 0), stop=(kt == KT - 1 and i == 2))
                last.then_inc(done, 1)

            def transpose_qk(s, t, older):
                pe.wait_ge(rot_part, 2 * s + 2)
                if older:
                    pe.wait_ge(T_copied, s)
                for a in range(2):
                    last = pe.transpose(T_ps[:, a * P:(a + 1) * P], rot[:, t % 2, a, :], ident[:])
                last.then_inc(T_mm, 1)

            def attend(s, t, older):
                pe.wait_ge(sT_done, s + 1)
                pe.wait_ge(kz_done, s + 1)
                if older:
                    pe.wait_ge(o_copied, s)
                    pe.wait_ge(R_done, s)
                v = qkv[:, t % 2, 2 * RQK:QKV]
                pe.matmul(o_ps[:, 0:RV], sT[:, :], v, start=True, stop=(t == 0))
                if t:
                    pe.matmul(o_ps[:, 0:RV], qkT[:, t % 2, 0, :], R[:, :], start=False, stop=True)
                pe.matmul(k_ps[:, 0:RV], kz[:, t % 2, :], v, start=True, stop=True).then_inc(attend_mm, 1)

            def scores(s, t):
                pe.wait_ge(T_copied, s + 1)
                if type(s) is not int or s > 0:
                    pe.wait_ge(sT_done, s)
                pe.matmul(s_ps[:, 0:P], qkT[:, t % 2, 1, :], qkT[:, t % 2, 0, :], start=True, stop=True).then_inc(s_mm, 1)

            def step(s, h, t, slot, older, between=lambda: None):
                if older >= 2:
                    pe.wait_ge(qkv_copied, s - 1)
                if t == 0:
                    pe.wait_ge(wl_done, KT * h + KT)
                project(qkv_ps[t % 2][:, :], t, slot, 0, QKV, qkv_mm)
                if older >= 1:
                    transpose_qk(s - 1, (t - 1) % NT, older >= 2)
                if older >= 2:
                    attend(s - 2, (t - 2) % NT, older >= 3)
                between()
                if older >= 1:
                    pe.wait_ge(silu_done, s)
                project(gate_ps[:, 0:RV], t, slot, QKV, RV, gate_mm)
                if older >= 1:
                    scores(s - 1, (t - 1) % NT)

            transpose_x(0, 0)
            transpose_x(0, 1)
            for t in range(NT):
                if t + 1 < NT:
                    transpose_x(t + 1, 0)
                pe.wait_ge(xl_done, 2 * t + 2)
                step(t, 0, t, 0, t, (lambda: transpose_x(t + 1, 1)) if t + 1 < NT else (lambda: None))
            with pe.Fori(1, RET_HEADS) as h:
                for t in range(NT):
                    step(h * NT + t, h, t, h % 2, 3)
            transpose_qk(LAST - 1, NT - 1, True)
            attend(LAST - 2, NT - 2, True)
            scores(LAST - 1, NT - 1)
            attend(LAST - 1, NT - 1, True)
    return sems


def close_mixer(nc, tag, gated, w, gain, x, g_post, ident, neghalf, x_next, feature_major=False, xT=None):
    with ExitStack() as ctx:
        def sb(name, shape, dt=F32):
            return ctx.enter_context(nc.sbuf_tensor(tag + name, shape, dt))

        sems = []

        def sem(name):
            sems.append(ctx.enter_context(nc.semaphore(tag + name)))
            return sems[-1]

        KW = w.shape[0] // P
        NQ = KW // 4
        n_gain = gain.shape[1] if gain is not None else 0
        wh = sb("wh", [P, KW, DM], F32R)
        wl = sb("wl", [P, KW, DM], F32R)
        raw = sb("raw", [P, 2, DM])
        gin = sb("gin", [P, KW, P])
        gh = sb("gh", [P, 2, KW, P], F32R)
        gl = sb("gl", [P, 2, KW, P], F32R)
        xin = sb("xin", [P, 2, DM])
        y = sb("y", [P, 2, DM])
        ss = sb("ss", [P, 2])
        ms = sb("ms", [P, 2])
        rms = sb("rms", [P, 2])
        if xT is not None:
            xh, xl = xT
            xn = sb("xn", [P, DM])
            sx = sb("sx", [P, 2])
            mx = sb("mx", [P, 2])
            rx = sb("rx", [P, 2])
        gain_sb = sb("gain", [P, max(n_gain, 1)])
        post = sb("post", [P, DM])
        y_ps = [ctx.enter_context(nc.psum_tensor(f"{tag}y_ps{i}", [P, 2, HALF], F32)) for i in range(2)]
        T_ps = [ctx.enter_context(nc.psum_tensor(f"{tag}T_ps{i}", [P, HALF], F32)) for i in range(4)]

        con_in = sem("con_in")
        raw_in = [sem("raw_in0"), sem("raw_in1")]
        x_in = [sem("x_in0"), sem("x_in1")]
        x_out = [sem("x_out0"), sem("x_out1")]
        (g_in, wh_done, wl_done, T_mm, gh_done, gl_done, y_mm, ss_done, ms_done, rms_done, scaled, y_done,
         sx_done, mx_done, rx_done, xn_done, xT_mm, xh_done, xl_done) = (sem(n) for n in (
            "g_in wh_done wl_done T_mm gh_done gl_done y_mm ss_done ms_done rms_done scaled y_done "
            "sx_done mx_done rx_done xn_done xT_mm xh_done xl_done").split())
        X_BANK = 2
        n_con = 16 * ((gain is not None) + (g_post is not None))
        block = ctx.enter_context(nc.Block())

        def group_of_gin(q):
            return gin[:, 4 * q:4 * q + 4, :]

        @block.sync
        def _(sp):
            def load_g(t, first):
                if not first:
                    sp.wait_ge(gl_done if feature_major else T_mm, t * NQ)
                src = (gated[:, ds(t * P, P)].rearrange("(k p) n -> p k n", p=P) if feature_major else
                       gated[ds(t * P, P), :].rearrange("p (k n) -> p k n", n=P))
                sp.dma_start(gin[:, :, :], src).then_inc(g_in, 16)

            def load_x(t, slot, first):
                if not first:
                    sp.wait_ge(y_done, t - 1)
                sp.dma_start(xin[:, slot, :], x[ds(t * P, P), :]).then_inc(x_in[slot], 16)

            def store(t, slot):
                sp.wait_ge(y_done, t + 1)
                sp.dma_start(x_next[ds(t * P, P), :], y[:, slot, :]).then_inc(x_out[slot], 16)

            def load_w(kt):
                if kt >= 2:
                    sp.wait_ge(wl_done, kt - 1)
                sp.dma_start(raw[:, kt % 2, :], w[kt * P:(kt + 1) * P, :]).then_inc(raw_in[kt % 2], 16)

            load_g(0, True)
            if gain is not None:
                sp.dma_start(gain_sb[:], gain).then_inc(con_in, 16)
            load_w(0)
            load_w(1)
            load_g(1, False)
            for kt in range(2, KW):
                load_w(kt)
            if g_post is not None:
                sp.dma_start(post[:], g_post.partition_broadcast(P)).then_inc(con_in, 16)
            load_x(0, 0, True)
            load_x(1, 1, True)
            load_g(2, False)
            with sp.Fori(1, NT // 2 - 1) as pair:
                for u in range(2):
                    t = 2 * pair + u
                    store(t - 2, u)
                    load_x(t, u, False)
                    load_g(t + 1, False)
            for t in (NT - 2, NT - 1):
                store(t - 2, t % 2)
                load_x(t, t % 2, False)
                if t + 1 < NT:
                    load_g(t + 1, False)
            for t in (NT - 2, NT - 1):
                store(t, t % 2)
            for slot in range(2):
                sp.wait_ge(x_out[slot], 16 * NT // 2)

        @block.scalar
        def _(act):
            def w_upper(kt):
                act.wait_ge(raw_in[kt % 2], 16 * (kt // 2 + 1))
                scale = gain_sb[:, kt % n_gain:kt % n_gain + 1] if n_gain else 1.0
                act.activation(wh[:, kt, :], raw[:, kt % 2, :], ACT.Copy, scale=scale).then_inc(wh_done, 1)

            def g_upper(t, slot, q, early):
                if feature_major:
                    act.wait_ge(g_in, 16 * t + 16)
                    src = group_of_gin(q)
                else:
                    act.wait_ge(T_mm, t * NQ + q + 1)
                    src = T_ps[q][:, :].rearrange("p (k n) -> p k n", k=4)
                if not early and q == 0:
                    act.wait_ge(y_mm, t - 1)
                act.activation(gh[:, slot, 4 * q:4 * q + 4, :], src, ACT.Copy).then_inc(gh_done, 1)

            def square_y(t, slot, stored):
                act.wait_ge(y_mm, t + 1)
                if type(stored) is not int or stored:
                    act.wait_ge(x_out[slot], 16 * stored)
                act.activation(y[:, slot, :], y_ps[slot][:, :, :].rearrange("p a n -> p (a n)"), ACT.Square,
                               accum_out=ss[:, slot:slot + 1]).then_inc(ss_done, 1)

            def square_x(t, slot):
                act.wait_ge(y_done, t + 1)
                wait_alone(act)
                act.activation(xl[:, :, ds(t * P, P)], y[:, slot, :].rearrange("p (k n) -> p k n", k=KT), ACT.Square,
                               accum_out=sx[:, slot:slot + 1]).then_inc(sx_done, 1)

            def x_upper(t, half):
                act.wait_ge(xT_mm, 2 * t + half + 1)
                wait_alone(act)
                act.activation(xh[:, 4 * half:4 * half + 4, ds(t * P, P)],
                               T_ps[X_BANK + half][:, :].rearrange("p (k n) -> p k n", k=4), ACT.Copy).then_inc(xh_done, 1)

            def round_of(t, slot, stored, old):
                if g_post is not None:
                    square_y(t - 2, slot, stored)
                if xT is None:
                    for q in range(NQ):
                        g_upper(t, slot, q, False)
                    return
                if old:
                    x_upper(t - 3, 0)
                g_upper(t, slot, 0, False)
                square_x(t - 2, slot)
                if old:
                    x_upper(t - 3, 1)
                g_upper(t, slot, 1, False)

            if gain is not None:
                act.wait_ge(con_in, 16)
            for q in range(NQ):
                g_upper(0, 0, q, True)
            w_upper(0)
            w_upper(1)
            for q in range(NQ):
                g_upper(1, 1, q, True)
            for kt in range(2, KW):
                w_upper(kt)
            round_of(2, 0, 0, False)
            round_of(3, 1, 0, True)
            with act.Fori(2, NT // 2) as pair:
                for u in range(2):
                    round_of(2 * pair + u, u, pair - 1, True)
            for t in (NT, NT + 1):
                if g_post is not None:
                    square_y(t - 2, t % 2, t // 2 - 1)
                if xT is not None:
                    x_upper(t - 3, 0)
                    x_upper(t - 3, 1)
                    square_x(t - 2, t % 2)
            if xT is not None:
                x_upper(NT - 1, 0)
                x_upper(NT - 1, 1)

        @block.gpsimd
        def _(pool):
            def one_over_rms(t, u, sums, mean, root, sums_done, mean_done, root_done):
                pool.wait_ge(sums_done, t + 1)
                wait_alone(pool)
                pool.tensor_scalar(mean[:, u:u + 1], sums[:, u:u + 1], 1.0 / DM, EPS, ALU.mult, ALU.add).then_inc(mean_done, 1)
                pool.wait_ge(mean_done, t + 1)
                pool.tensor_tensor(root[:, u:u + 1], mean[:, u:u + 1], neghalf[:], ALU.pow).then_inc(root_done, 1)

            with pool.Fori(0, NT // 2) as pair:
                for u in range(2):
                    if g_post is not None:
                        one_over_rms(2 * pair + u, u, ss, ms, rms, ss_done, ms_done, rms_done)
                    if xT is not None:
                        one_over_rms(2 * pair + u, u, sx, mx, rx, sx_done, mx_done, rx_done)

        @block.vector
        def _(dve):
            def w_lower(kt):
                dve.wait_ge(wh_done, kt + 1)
                if n_gain:
                    dve.scalar_tensor_tensor(wl[:, kt, :], raw[:, kt % 2, :], gain_sb[:, kt % n_gain:kt % n_gain + 1],
                                             wh[:, kt, :].bitcast(F32), ALU.mult, ALU.subtract).then_inc(wl_done, 1)
                else:
                    dve.tensor_tensor(wl[:, kt, :], raw[:, kt % 2, :], wh[:, kt, :].bitcast(F32),
                                      ALU.subtract).then_inc(wl_done, 1)

            def g_lower(t, slot, q):
                dve.wait_ge(gh_done, t * NQ + q + 1)
                src = group_of_gin(q) if feature_major else T_ps[q][:, :].rearrange("p (k n) -> p k n", k=4)
                dve.tensor_tensor(gl[:, slot, 4 * q:4 * q + 4, :], src, gh[:, slot, 4 * q:4 * q + 4, :].bitcast(F32),
                                  ALU.subtract).then_inc(gl_done, 1)

            def finish(t, slot, stored):
                ys = y_ps[slot][:, :, :].rearrange("p a n -> p (a n)")
                dve.wait_ge(x_in[slot], 16 * stored + 16)
                if g_post is None:
                    dve.wait_ge(y_mm, t + 1)
                    if type(stored) is not int or stored:
                        dve.wait_ge(x_out[slot], 16 * stored)
                    dve.tensor_tensor(y[:, slot, :], ys, xin[:, slot, :], ALU.add).then_inc(y_done, 1)
                else:
                    dve.wait_ge(rms_done, t + 1)
                    dve.scalar_tensor_tensor(y[:, slot, :], ys, rms[:, slot:slot + 1], post[:], ALU.mult, ALU.mult).then_inc(scaled, 1)
                    dve.wait_ge(scaled, t + 1)
                    dve.tensor_tensor(y[:, slot, :], y[:, slot, :], xin[:, slot, :], ALU.add).then_inc(y_done, 1)

            def scale_x(t, slot, old):
                dve.wait_ge(rx_done, t + 1)
                if old:
                    dve.wait_ge(xT_mm, 2 * t)
                dve.tensor_scalar(xn[:, :], y[:, slot, :], rx[:, slot:slot + 1], None, ALU.mult).then_inc(xn_done, 1)

            def x_lower(t, half):
                dve.wait_ge(xh_done, 2 * t + half + 1)
                wait_alone(dve)
                dve.tensor_tensor(xl[:, 4 * half:4 * half + 4, ds(t * P, P)],
                                  T_ps[X_BANK + half][:, :].rearrange("p (k n) -> p k n", k=4),
                                  xh[:, 4 * half:4 * half + 4, ds(t * P, P)].bitcast(F32),
                                  ALU.subtract).then_inc(xl_done, 1)

            def round_of(t, slot, stored, old):
                finish(t - 2, slot, stored)
                if xT is None:
                    for q in range(NQ):
                        g_lower(t, slot, q)
                    return
                if old:
                    x_lower(t - 3, 0)
                g_lower(t, slot, 0)
                if old:
                    x_lower(t - 3, 1)
                scale_x(t - 2, slot, old)
                g_lower(t, slot, 1)

            if gain is not None:
                dve.wait_ge(con_in, 16)
            for q in range(NQ):
                g_lower(0, 0, q)
            w_lower(0)
            w_lower(1)
            for q in range(NQ):
                g_lower(1, 1, q)
            for kt in range(2, KW):
                w_lower(kt)
            if n_con:
                dve.wait_ge(con_in, n_con)
            round_of(2, 0, 0, False)
            round_of(3, 1, 0, True)
            with dve.Fori(2, NT // 2) as pair:
                for u in range(2):
                    round_of(2 * pair + u, u, pair - 1, True)
            for t in (NT, NT + 1):
                finish(t - 2, t % 2, t // 2 - 1)
                if xT is not None:
                    x_lower(t - 3, 0)
                    x_lower(t - 3, 1)
                    scale_x(t - 2, t % 2, True)
            if xT is not None:
                x_lower(NT - 1, 0)
                x_lower(NT - 1, 1)

        @block.tensor
        def _(pe):
            def transpose_g(t, q, early):
                if feature_major:
                    return
                if q == 0:
                    pe.wait_ge(g_in, 16 * t + 16)
                if not early:
                    pe.wait_ge(gl_done, (t - 1) * NQ + q + 1)
                for k in range(4):
                    last = pe.transpose(T_ps[q][:, k * P:(k + 1) * P], gin[:, 4 * q + k, :], ident[:])
                last.then_inc(T_mm, 1)

            def multiply(slot, kt):
                for c in range(2):
                    for i, (a, b) in enumerate(((gl, wh), (gh, wl), (gh, wh))):
                        last = pe.matmul(y_ps[slot][:, c, :], a[:, slot, kt, :], b[:, kt, c * HALF:(c + 1) * HALF],
                                         start=(kt == 0 and i == 0), stop=(kt == KW - 1 and i == 2))
                return last

            for t in range(2):
                for q in range(NQ):
                    transpose_g(t, q, t == 0)
            for kt in range(KW):
                for t in range(2):
                    if kt % 4 == 0:
                        pe.wait_ge(gl_done, t * NQ + kt // 4 + 1)
                    if t == 0:
                        pe.wait_ge(wl_done, kt + 1)
                    last = multiply(t, kt)
                    if kt == KW - 1:
                        last.then_inc(y_mm, 1)
            for q in range(NQ):
                transpose_g(2, q, False)

            def transpose_x(t, half, old):
                if half == 0:
                    pe.wait_ge(xn_done, t + 1)
                if old:
                    pe.wait_ge(xl_done, 2 * t + half - 1)
                for k in range(4):
                    last = pe.transpose(T_ps[X_BANK + half][:, k * P:(k + 1) * P],
                                        xn[:, (4 * half + k) * P:(4 * half + k + 1) * P], ident[:])
                last.then_inc(xT_mm, 1)

            def tile(t, slot, more, old=True):
                pe.wait_ge(y_done, t - 1)
                for kt in range(KW):
                    if kt % 4 == 0:
                        pe.wait_ge(gl_done, t * NQ + kt // 4 + 1)
                    last = multiply(slot, kt)
                    if xT is not None and kt in (2, 5):
                        transpose_x(t - 2, kt // 5, old)
                    if kt % 4 == 3 and more:
                        transpose_g(t + 1, kt // 4, False)
                last.then_inc(y_mm, 1)

            tile(2, 0, True, False)
            tile(3, 1, True)
            with pe.Fori(2, NT // 2 - 1) as pair:
                for u in range(2):
                    tile(2 * pair + u, u, True)
            tile(NT - 2, 0, True)
            tile(NT - 1, 1, False)
            if xT is not None:
                for t in (NT - 2, NT - 1):
                    for half in range(2):
                        transpose_x(t, half, True)
    return sems


def latents(nc, x, g_kv, g_pre, w_lat, w_gate, con, ident, neghalf, kv, cq, silu_gate):
    kvh, kvl = kv
    cqh, cql = cq
    with ExitStack() as ctx:
        def sb(name, shape, dt=F32):
            return ctx.enter_context(nc.sbuf_tensor("la_" + name, shape, dt))

        def bank(name):
            return ctx.enter_context(nc.psum_tensor("la_" + name, [P, HALF], F32))

        sems = []

        def sem(name):
            sems.append(ctx.enter_context(nc.semaphore("la_" + name)))
            return sems[-1]

        KVW = KV_LORA + MROPE
        WL = KVW + Q_LORA
        xh = sb("xh", [P, KT, SEQ], F32R)
        xl = sb("xl", [P, KT, SEQ], F32R)
        wh = sb("wh", [P, KT, WL], F32R)
        wl = sb("wl", [P, KT, WL], F32R)
        gh = sb("gh", [P, KT, HALF], F32R)
        gl = sb("gl", [P, KT, HALF], F32R)
        raw = sb("raw", [P, 2, DM])
        xin = sb("xin", [P, 2, DM])
        lat = xin[:, 0, :]
        gains = sb("gains", [P, 2, KT])
        cos = sb("cos", [P, NT, MROPE // 2])
        sin = sb("sin", [P, NT, MROPE // 2])
        kr = xin[:, 1, 0:MROPE]
        krot = xin[:, 1, MROPE:3 * MROPE].rearrange("p (a n) -> p a n", a=2)
        ktmp = sb("ktmp", [P, MROPE])
        ss = sb("ss", [P, NT])
        ms = sb("ms", [P, NT])
        rms = sb("rms", [P, NT])
        ls = sb("ls", [P, NT, 2])
        lm = sb("lm", [P, NT, 2])
        lr = sb("lr", [P, NT, 2])
        kv_ps = [bank("kv_ps0"), bank("kv_ps1")]
        cq_ps = [bank("cq_ps0"), bank("cq_ps1")]
        T_ps = [bank("T_ps0"), bank("T_ps1")]
        x_ps = bank("x_ps")

        con_in = sem("con_in")
        x_in = [sem("x_in0"), sem("x_in1")]
        raw_in = [sem("raw_in0"), sem("raw_in1")]
        g_out = [sem("g_out0"), sem("g_out1")]
        (ss_done, ms_done, rms_done, xn_done, xT_mm, xh_done, xl_done, wh_done, wl_done, lat_mm, ls_done, lm_done,
         lr_done, kr_done, kr_part, krot_done, lat_done, T_mm, Th_done, Tl_done, gate_mm, silu_done) = (
            sem(n) for n in ("ss_done ms_done rms_done xn_done xT_mm xh_done xl_done wh_done wl_done lat_mm ls_done "
                             "lm_done lr_done kr_done kr_part krot_done lat_done T_mm Th_done Tl_done gate_mm "
                             "silu_done").split())
        block = ctx.enter_context(nc.Block())
        N_PIECES = KT + 2 * KT // 2
        GROUPS = 16

        @block.sync
        def _(sp):
            def load_x(t):
                if t >= 2:
                    sp.wait_ge(xT_mm, 2 * (t - 1))
                sp.dma_start(xin[:, t % 2, :], x[t * P:(t + 1) * P, :]).then_inc(x_in[t % 2], 16)

            def load_piece(n):
                if n >= 2:
                    sp.wait_ge(wl_done, n - 1)
                if n < KT:
                    sp.dma_start(raw[:, n % 2, 0:WL], w_lat[:, n, :]).then_inc(raw_in[n % 2], 16)
                else:
                    unit, k = divmod(n - KT, 4)
                    sp.dma_start(raw[:, n % 2, :], w_gate[unit, :, 2 * k:2 * k + 2, :].rearrange("p k n -> p (k n)"))\
                      .then_inc(raw_in[n % 2], 16)

            load_x(0)
            sp.dma_start(gains[:, 0, :], g_kv).then_inc(con_in, 16)
            sp.dma_start(gains[:, 1, :], g_pre).then_inc(con_in, 16)
            sp.dma_start(cos[:], con["cos_mla"]).then_inc(con_in, 16)
            sp.dma_start(sin[:], con["sin_mla"]).then_inc(con_in, 16)
            load_x(1)
            load_piece(0)
            load_piece(1)
            for t in range(2, NT):
                load_x(t)
                load_piece(t)
            for n in range(KT, N_PIECES):
                load_piece(n)
            for j in range(GROUPS):
                sp.wait_ge(silu_done, j + 1)
                f, half = divmod(j, 2)
                sp.dma_start(silu_gate[f * P:(f + 1) * P, half * HALF:(half + 1) * HALF], xin[:, j % 2, 0:HALF])\
                  .then_inc(g_out[j % 2], 16)
            for slot in range(2):
                sp.wait_ge(g_out[slot], 16 * GROUPS // 2)

        def piece_parts(n):
            if n < KT:
                return [(n, 0, (0, KVW), wh[:, n, 0:KVW], wl[:, n, 0:KVW]),
                        (n, 1, (KVW, WL), wh[:, n, KVW:WL], wl[:, n, KVW:WL])]
            unit, k = divmod(n - KT, 4)
            h, l = ((gh, gl), (wh, wl))[unit]
            return [(kt, 1, (i * HALF, (i + 1) * HALF), h[:, kt, 0:HALF], l[:, kt, 0:HALF])
                    for i, kt in enumerate((2 * k, 2 * k + 1))]

        @block.scalar
        def _(act):
            def square_x(t):
                act.wait_ge(x_in[t % 2], 16 * (t // 2 + 1))
                act.activation(xl[:, :, t * P:(t + 1) * P], xin[:, t % 2, :].rearrange("p (k n) -> p k n", k=KT),
                               ACT.Square, accum_out=ss[:, t:t + 1]).then_inc(ss_done, 1)

            def x_upper(t, half):
                act.wait_ge(xT_mm, 2 * t + half + 1)
                act.activation(xh[:, 4 * half:4 * half + 4, t * P:(t + 1) * P],
                               x_ps[:, :].rearrange("p (k n) -> p k n", k=4), ACT.Copy).then_inc(xh_done, 1)

            def w_upper(n):
                act.wait_ge(raw_in[n % 2], 16 * (n // 2 + 1))
                if n == KT + 4:
                    act.wait_ge(lat_mm, NT)
                for kt, g, (a, b), h, _ in piece_parts(n):
                    last = act.activation(h, raw[:, n % 2, a:b], ACT.Copy, scale=gains[:, g, kt:kt + 1])
                last.then_inc(wh_done, 1)

            def latent(t):
                act.wait_ge(lat_mm, t + 1)
                if t:
                    act.wait_ge(T_mm, 2 * t)
                    act.wait_ge(kr_part, 2 * t)
                act.activation(lat[:, 0:KV_LORA], kv_ps[t % 2][:, 0:KV_LORA], ACT.Square, accum_out=ls[:, t, 0:1])
                act.activation(lat[:, KV_LORA:KV_LORA + Q_LORA], cq_ps[t % 2][:, 0:Q_LORA], ACT.Square, accum_out=ls[:, t, 1:2]).then_inc(ls_done, 1)
                act.activation(kr[:, :], kv_ps[t % 2][:, KV_LORA:KVW], ACT.Copy).then_inc(kr_done, 1)

            def latent_upper(t):
                for i, dst in ((0, kvh), (1, cqh)):
                    act.wait_ge(T_mm, 2 * t + i + 1)
                    act.activation(dst[:, :, t * P:(t + 1) * P], T_ps[i][:, 0:3 * P].rearrange("p (k n) -> p k n", k=3),
                                   ACT.Copy).then_inc(Th_done, 1)

            act.wait_ge(con_in, 64)
            square_x(0)
            square_x(1)
            for t in range(NT):
                w_upper(t)
                for half in range(2):
                    x_upper(t, half)
                if t + 2 < NT:
                    square_x(t + 2)
            for t in range(NT):
                latent(t)
                if t:
                    latent_upper(t - 1)
                if t % 2:
                    w_upper(KT + t // 2)
            latent_upper(NT - 1)
            for j in range(GROUPS):
                if j < 4:
                    w_upper(KT + 4 + j)
                act.wait_ge(gate_mm, j + 1)
                if j >= 2:
                    act.wait_ge(g_out[j % 2], 16 * (j // 2))
                act.activation(xin[:, j % 2, 0:HALF], kv_ps[j % 2][:, :], ACT.Silu).then_inc(silu_done, 1)

        @block.gpsimd
        def _(pool):
            def rms_x(t):
                pool.wait_ge(ss_done, t + 1)
                pool.tensor_scalar(ms[:, t:t + 1], ss[:, t:t + 1], 1.0 / DM, EPS, ALU.mult, ALU.add).then_inc(ms_done, 1)
                pool.wait_ge(ms_done, t + 1)
                pool.tensor_tensor(rms[:, t:t + 1], ms[:, t:t + 1], neghalf[:], ALU.pow).then_inc(rms_done, 1)

            def rms_latent(t):
                pool.wait_ge(ls_done, t + 1)
                pool.tensor_scalar(lm[:, t, 0:1], ls[:, t, 0:1], 1.0 / KV_LORA, EPS, ALU.mult, ALU.add)
                pool.tensor_scalar(lm[:, t, 1:2], ls[:, t, 1:2], 1.0 / Q_LORA, EPS, ALU.mult, ALU.add).then_inc(lm_done, 1)
                pool.wait_ge(lm_done, t + 1)
                pool.tensor_tensor(lr[:, t, :], lm[:, t, :], neghalf[:].broadcast_to([P, 2]), ALU.pow).then_inc(lr_done, 1)

            def rotate_key(t):
                H = MROPE // 2
                pool.wait_ge(kr_done, t + 1)
                if t:
                    pool.wait_ge(T_mm, 2 * t)
                c, s = cos[:, t, :], sin[:, t, :]
                pool.tensor_tensor(krot[:, 0, 0:H], kr[:, 0:H], c, ALU.mult)
                pool.tensor_tensor(krot[:, 0, H:], kr[:, H:], c, ALU.mult)
                pool.tensor_tensor(ktmp[:, 0:H], kr[:, H:], s, ALU.mult)
                pool.tensor_tensor(ktmp[:, H:], kr[:, 0:H], s, ALU.mult).then_inc(kr_part, 1)
                pool.wait_ge(kr_part, 2 * t + 1)
                pool.tensor_tensor(krot[:, 0, 0:H], krot[:, 0, 0:H], ktmp[:, 0:H], ALU.subtract)
                pool.tensor_tensor(krot[:, 0, H:], krot[:, 0, H:], ktmp[:, H:], ALU.add).then_inc(kr_part, 1)
                pool.wait_ge(kr_part, 2 * t + 2)
                pool.tensor_copy(krot[:, 1, :], krot[:, 0, :]).then_inc(krot_done, 1)

            pool.wait_ge(con_in, 64)
            for t in range(NT):
                rms_x(t)
            for t in range(NT):
                rms_latent(t)
                rotate_key(t)

        @block.vector
        def _(dve):
            def scale_x(t):
                dve.wait_ge(rms_done, t + 1)
                dve.tensor_scalar(xin[:, t % 2, :], xin[:, t % 2, :], rms[:, t:t + 1], None, ALU.mult).then_inc(xn_done, 1)

            def x_lower(t, half):
                dve.wait_ge(xh_done, 2 * t + half + 1)
                dve.tensor_tensor(xl[:, 4 * half:4 * half + 4, t * P:(t + 1) * P],
                                  x_ps[:, :].rearrange("p (k n) -> p k n", k=4),
                                  xh[:, 4 * half:4 * half + 4, t * P:(t + 1) * P].bitcast(F32),
                                  ALU.subtract).then_inc(xl_done, 1)

            def w_lower(n):
                dve.wait_ge(wh_done, n + 1)
                for kt, g, (a, b), h, l in piece_parts(n):
                    last = dve.scalar_tensor_tensor(l, raw[:, n % 2, a:b], gains[:, g, kt:kt + 1], h.bitcast(F32),
                                                    ALU.mult, ALU.subtract)
                last.then_inc(wl_done, 1)

            def norm_latents(t):
                dve.wait_ge(lr_done, t + 1)
                dve.wait_ge(kr_done, t + 1)
                dve.tensor_scalar(lat[:, 0:KV_LORA], kv_ps[t % 2][:, 0:KV_LORA], lr[:, t, 0:1], None, ALU.mult)
                dve.tensor_scalar(lat[:, KV_LORA:KV_LORA + Q_LORA], cq_ps[t % 2][:, 0:Q_LORA], lr[:, t, 1:2], None, ALU.mult)\
                   .then_inc(lat_done, 1)

            def latent_lower(t):
                for i, h, l in ((0, kvh, kvl), (1, cqh, cql)):
                    dve.wait_ge(Th_done, 2 * t + i + 1)
                    dve.tensor_tensor(l[:, :, t * P:(t + 1) * P], T_ps[i][:, 0:3 * P].rearrange("p (k n) -> p k n", k=3),
                                      h[:, :, t * P:(t + 1) * P].bitcast(F32), ALU.subtract).then_inc(Tl_done, 1)

            dve.wait_ge(con_in, 64)
            scale_x(0)
            for t in range(NT):
                w_lower(t)
                if t + 1 < NT:
                    scale_x(t + 1)
                for half in range(2):
                    x_lower(t, half)
            for t in range(NT):
                norm_latents(t)
                if t:
                    latent_lower(t - 1)
                if t % 2:
                    w_lower(KT + t // 2)
            latent_lower(NT - 1)
            for j in range(4):
                w_lower(KT + 4 + j)

        @block.tensor
        def _(pe):
            def transpose_x(t):
                pe.wait_ge(xn_done, t + 1)
                for half in range(2):
                    if t or half:
                        pe.wait_ge(xl_done, 2 * t + half)
                    for k in range(4):
                        last = pe.transpose(x_ps[:, k * P:(k + 1) * P],
                                            xin[:, t % 2, (4 * half + k) * P:(4 * half + k + 1) * P], ident[:])
                    last.then_inc(xT_mm, 1)

            def project(t):
                pe.wait_ge(xl_done, 2 * t + 2)
                if t >= 2:
                    pe.wait_ge(lat_done, t - 1)
                for kt in range(KT):
                    if t == 0:
                        pe.wait_ge(wl_done, kt + 1)
                    for out, a, b in ((kv_ps[t % 2][:, 0:KVW], 0, KVW), (cq_ps[t % 2][:, 0:Q_LORA], KVW, WL)):
                        for i, (xx, ww) in enumerate(((xl, wh), (xh, wl), (xh, wh))):
                            last = pe.matmul(out, xx[:, kt, t * P:(t + 1) * P], ww[:, kt, a:b],
                                             start=(kt == 0 and i == 0), stop=(kt == KT - 1 and i == 2))
                last.then_inc(lat_mm, 1)

            def transpose_latents(t):
                pe.wait_ge(lat_done, t + 1)
                pe.wait_ge(krot_done, t + 1)
                if t:
                    pe.wait_ge(Tl_done, 2 * t)
                for k in range(2):
                    pe.transpose(T_ps[0][:, k * P:(k + 1) * P], lat[:, k * P:(k + 1) * P], ident[:])
                pe.transpose(T_ps[0][:, 2 * P:3 * P], xin[:, 1, MROPE:3 * MROPE], ident[:]).then_inc(T_mm, 1)
                for k in range(3):
                    last = pe.transpose(T_ps[1][:, k * P:(k + 1) * P], lat[:, (2 + k) * P:(3 + k) * P], ident[:])
                last.then_inc(T_mm, 1)

            for t in range(NT):
                transpose_x(t)
            for t in range(NT):
                project(t)
                if t:
                    transpose_latents(t - 1)
            for j in range(GROUPS):
                f, half = divmod(j, 2)
                h, l = ((gh, gl), (wh, wl))[f // 4]
                if j % 8 == 0:
                    pe.wait_ge(wl_done, KT + 4 * (f // 4) + 4)
                if j >= 2:
                    pe.wait_ge(silu_done, j - 1)
                else:
                    pe.wait_ge(lat_done, NT)
                for kt in range(KT):
                    for i, (a, b) in enumerate(((l, xh), (h, xl), (h, xh))):
                        last = pe.matmul(kv_ps[j % 2][:, :], a[:, kt, f % 4 * P:(f % 4 + 1) * P],
                                         b[:, kt, half * HALF:(half + 1) * HALF],
                                         start=(kt == 0 and i == 0), stop=(kt == KT - 1 and i == 2))
                last.then_inc(gate_mm, 1)
                if j == 0:
                    transpose_latents(NT - 1)
    return sems


def values_and_rotary(nc, kv, cq, g_lat, w_uv, w_rot, con, ident, v, qrT):
    kvh, kvl = kv
    cqh, cql = cq
    SCALE = (NOPE + MROPE) ** -0.5
    RW = MLA_HEADS * MROPE
    with ExitStack() as ctx:
        def sb(name, shape, dt=F32):
            return ctx.enter_context(nc.sbuf_tensor("vr_" + name, shape, dt))

        sems = []

        def sem(name):
            sems.append(ctx.enter_context(nc.semaphore("vr_" + name)))
            return sems[-1]

        raw_v = sb("raw_v", [P, 2, DM])
        raw_r = sb("raw_r", [P, 3, RW])
        wvh = sb("wvh", [P, 2, DM], F32R)
        wvl = sb("wvl", [P, 2, DM], F32R)
        wrh = sb("wrh", [P, 3, RW], F32R)
        wrl = sb("wrl", [P, 3, RW], F32R)
        gains = sb("gains", [P, 5])
        cos = sb("cos", [P, NT, MROPE // 2])
        sin = sb("sin", [P, NT, MROPE // 2])
        qr = sb("qr", [P, 2, RW])
        rot = sb("rot", [P, 2, RW])
        tmp = sb("tmp", [P, RW])
        v_ps = [ctx.enter_context(nc.psum_tensor(f"vr_v_ps{i}", [P, 2, HALF], F32)) for i in range(2)]
        r_ps = [ctx.enter_context(nc.psum_tensor(f"vr_r_ps{i}", [P, HALF], F32)) for i in range(2)]
        T_ps = [ctx.enter_context(nc.psum_tensor(f"vr_T_ps{i}", [P, HALF], F32)) for i in range(2)]
        con_in, rw_in, vw_in = sem("con_in"), sem("rw_in"), sem("vw_in")
        (wh_done, wl_done, v_mm, v_copied, r_mm, qr_done, rot_part, T_mm, T_copied) = (
            sem(n) for n in "wh_done wl_done v_mm v_copied r_mm qr_done rot_part T_mm T_copied".split())
        block = ctx.enter_context(nc.Block())

        @block.sync
        def _(sp):
            sp.dma_start(gains[:], g_lat).then_inc(con_in, 16)
            sp.dma_start(raw_r[:], w_rot).then_inc(rw_in, 16)
            sp.dma_start(cos[:], con["cos_mla"]).then_inc(con_in, 16)
            sp.dma_start(sin[:], con["sin_mla"]).then_inc(con_in, 16)
            sp.dma_start(raw_v[:], w_uv).then_inc(vw_in, 16)

        @block.scalar
        def _(act):
            act.wait_ge(con_in, 48)
            act.wait_ge(rw_in, 16)
            for k in range(3):
                act.activation(wrh[:, k, :], raw_r[:, k, :], ACT.Copy, scale=gains[:, 2 + k:3 + k]).then_inc(wh_done, 1)
            act.wait_ge(vw_in, 16)
            for k in range(2):
                act.activation(wvh[:, k, :], raw_v[:, k, :], ACT.Copy, scale=gains[:, k:k + 1]).then_inc(wh_done, 1)
            for t in range(NT):
                act.wait_ge(r_mm, t + 1)
                if t >= 2:
                    act.wait_ge(rot_part, 2 * t - 2)
                act.activation(qr[:, t % 2, :], r_ps[t % 2][:, :], ACT.Copy, scale=SCALE).then_inc(qr_done, 1)
                act.wait_ge(v_mm, t + 1)
                act.activation(v[:, t, :], v_ps[t % 2][:, :, :].rearrange("p a n -> p (a n)"), ACT.Copy).then_inc(v_copied, 1)
                if t:
                    act.wait_ge(T_mm, t)
                    act.activation(qrT[:, :, (t - 1) * P:t * P], T_ps[(t - 1) % 2][:, :].rearrange("p (a n) -> p a n", a=4),
                                   ACT.Copy).then_inc(T_copied, 1)
            act.wait_ge(T_mm, NT)
            act.activation(qrT[:, :, (NT - 1) * P:], T_ps[(NT - 1) % 2][:, :].rearrange("p (a n) -> p a n", a=4),
                           ACT.Copy).then_inc(T_copied, 1)

        @block.gpsimd
        def _(pool):
            pool.wait_ge(con_in, 48)
            H = MROPE // 2
            for t in range(NT):
                pool.wait_ge(qr_done, t + 1)
                if t >= 2:
                    pool.wait_ge(T_mm, t - 1)
                q = qr[:, t % 2, :].rearrange("p (a u n) -> p a u n", u=2, n=H)
                r = rot[:, t % 2, :].rearrange("p (a u n) -> p a u n", u=2, n=H)
                w = tmp[:, :].rearrange("p (a u n) -> p a u n", u=2, n=H)
                c = cos[:, t:t + 1, :].broadcast_to([P, MLA_HEADS, H])
                s = sin[:, t:t + 1, :].broadcast_to([P, MLA_HEADS, H])
                pool.tensor_tensor(r[:, :, 0, :], q[:, :, 0, :], c, ALU.mult)
                pool.tensor_tensor(r[:, :, 1, :], q[:, :, 1, :], c, ALU.mult)
                if t:
                    pool.wait_ge(rot_part, 2 * t)
                pool.tensor_tensor(w[:, :, 0, :], q[:, :, 1, :], s, ALU.mult)
                pool.tensor_tensor(w[:, :, 1, :], q[:, :, 0, :], s, ALU.mult).then_inc(rot_part, 1)
                pool.wait_ge(rot_part, 2 * t + 1)
                pool.tensor_tensor(r[:, :, 0, :], r[:, :, 0, :], w[:, :, 0, :], ALU.subtract)
                pool.tensor_tensor(r[:, :, 1, :], r[:, :, 1, :], w[:, :, 1, :], ALU.add).then_inc(rot_part, 1)

        @block.vector
        def _(dve):
            dve.wait_ge(con_in, 48)
            for i in range(5):
                dve.wait_ge(wh_done, i + 1)
                r, h, l, g = ((raw_r, wrh, wrl, 2 + i), (raw_v, wvh, wvl, i - 3))[i >= 3]
                k = i if i < 3 else i - 3
                dve.scalar_tensor_tensor(l[:, k, :], r[:, k, :], gains[:, g:g + 1], h[:, k, :].bitcast(F32),
                                         ALU.mult, ALU.subtract).then_inc(wl_done, 1)

        @block.tensor
        def _(pe):
            def transpose_q(t):
                pe.wait_ge(rot_part, 2 * t + 2)
                if t >= 2:
                    pe.wait_ge(T_copied, t - 1)
                for k in range(4):
                    last = pe.transpose(T_ps[t % 2][:, k * P:(k + 1) * P], rot[:, t % 2, k * P:(k + 1) * P], ident[:])
                last.then_inc(T_mm, 1)

            for t in range(NT):
                here = slice(t * P, (t + 1) * P)
                if t == 0:
                    pe.wait_ge(wl_done, 3)
                if t >= 2:
                    pe.wait_ge(qr_done, t - 1)
                for k in range(3):
                    for i, (a, b) in enumerate(((cql, wrh), (cqh, wrl), (cqh, wrh))):
                        last = pe.matmul(r_ps[t % 2][:, :], a[:, k, here], b[:, k, :],
                                         start=(k == 0 and i == 0), stop=(k == 2 and i == 2))
                last.then_inc(r_mm, 1)
                if t == 0:
                    pe.wait_ge(wl_done, 5)
                if t >= 2:
                    pe.wait_ge(v_copied, t - 1)
                for n in range(2):
                    for k in range(2):
                        for i, (a, b) in enumerate(((kvl, wvh), (kvh, wvl), (kvh, wvh))):
                            last = pe.matmul(v_ps[t % 2][:, n, :], a[:, k, here], b[:, k, n * HALF:(n + 1) * HALF],
                                             start=(k == 0 and i == 0), stop=(k == 1 and i == 2))
                last.then_inc(v_mm, 1)
                if t:
                    transpose_q(t - 1)
            transpose_q(NT - 1)
    return sems


def attention(nc, kv, cq, v, qrT, g_lat, w_head, silu_gate, ident, gated):
    kvh, kvl = kv
    cqh, cql = cq
    SCALE = (NOPE + MROPE) ** -0.5
    FAR = -1e30
    H = MLA_HEADS
    with ExitStack() as ctx:
        def sb(name, shape, dt=F32):
            return ctx.enter_context(nc.sbuf_tensor("at_" + name, shape, dt))

        sems = []

        def sem(name):
            sems.append(ctx.enter_context(nc.semaphore("at_" + name)))
            return sems[-1]

        raw = sb("raw", [P, 5, P])
        wh = sb("wh", [P, 2, 5, P], F32R)
        wl = sb("wl", [P, 2, 5, P], F32R)
        gains = sb("gains", [P, 5])
        qh = sb("qh", [P, SEQ], F32R)
        ql = sb("ql", [P, SEQ], F32R)
        kh = sb("kh", [P, SEQ], F32R)
        kl = sb("kl", [P, SEQ], F32R)
        rh = sb("rh", [P, SEQ], F32R)
        rl = sb("rl", [P, SEQ], F32R)
        vh = sb("vh", [P, 2, NT, P], F32R)
        vl = sb("vl", [P, 2, NT, P], F32R)
        prob = sb("prob", [P, 2, SEQ])
        pth = sb("pth", [P, NT, 2 * P], F32R)
        ptl = sb("ptl", [P, NT, 2 * P], F32R)
        sg = sb("sg", [P, 2, SEQ])
        early = sb("early", [1, P])
        late = sb("late", [1, P])
        nmax = sb("nmax", [P, 2])
        rsum = sb("rsum", [P, 2])
        rinv = sb("rinv", [P, 2])
        s_ps = [ctx.enter_context(nc.psum_tensor(f"at_s_ps{i}", [P, 2, HALF], F32)) for i in range(2)]
        T_ps = [ctx.enter_context(nc.psum_tensor(f"at_T_ps{i}", [P, HALF], F32)) for i in range(2)]
        j_ps = ctx.enter_context(nc.psum_tensor("at_j_ps", [P, HALF], F32))
        v_ps = ctx.enter_context(nc.psum_tensor("at_v_ps", [P, HALF], F32))
        gain_in, w_in = sem("gain_in"), sem("w_in")
        sg_in = [sem("sg_in0"), sem("sg_in1")]
        g_out = [sem("g_out0"), sem("g_out1")]
        (mask_done, wh_done, wl_done, vh_done, vl_done, rh_done, rl_done, j_mm, jh_done, jl_done, s_mm, max_done,
         exp_done, inv_done, prob_done, T_mm, Th_done, Tl_done, v_mm, g_done) = (
            sem(n) for n in ("mask_done wh_done wl_done vh_done vl_done rh_done rl_done j_mm jh_done jl_done s_mm max_done "
                             "exp_done inv_done prob_done T_mm Th_done Tl_done v_mm g_done").split())
        block = ctx.enter_context(nc.Block())

        TG = 12

        def groups(i):
            if i < 4:
                return [(i, 0, i + 1)]
            return [(4 + 2 * (i - 4), 0, 4), (5 + 2 * (i - 4), 4, i - 3)]

        def last_group(h, i):
            return TG * h + groups(i)[-1][0]

        def before(h, i, n):
            return (h, i - n) if i >= n else (h - 1, i - n + NT)

        def projections():
            for g, (ks, src) in enumerate((((2, 3, 4), 0), ((2, 3, 4), 0), ((0, 1), 1), ((0, 1), 1))):
                yield g, ks, ((cqh, cql), (kvh, kvl))[src], g % 2

        def heads(eng, head):
            head(0, 0, True, False)
            with eng.Fori(0, (H - 2) // 2) as pair:
                head(2 * pair + 1, 1, False, False)
                head(2 * pair + 2, 0, False, False)
            head(H - 1, 1, False, True)

        @block.sync
        def _(sp):
            def load_gate(h, slot):
                sp.dma_start(sg[:, slot, :], silu_gate[ds(h * P, P), :]).then_inc(sg_in[slot], 16)

            def store(h, slot):
                sp.wait_ge(g_done, 4 * h + 4)
                sp.dma_start(gated[ds(h * P, P), :], sg[:, slot, :]).then_inc(g_out[slot], 16)

            def head(h, u, first, last):
                if not last:
                    sp.wait_ge(wl_done, h + 1)
                    sp.dma_start(raw[:], w_head[ds(h + 1, 1), :, :, :].rearrange("a p k n -> p (a k) n")).then_inc(w_in, 16)
                if not first:
                    store(h - 1, 1 - u)
                    if not last:
                        sp.wait_ge(g_out[1 - u], 8 * (h + 1 - (1 - u)))
                if not last:
                    load_gate(h + 1, 1 - u)

            sp.dma_start(gains[:], g_lat).then_inc(gain_in, 16)
            sp.dma_start(raw[:], w_head[0, :, :, :]).then_inc(w_in, 16)
            load_gate(0, 0)
            heads(sp, head)
            store(H - 1, 1)
            for slot in range(2):
                sp.wait_ge(g_out[slot], 16 * H // 2)

        @block.scalar
        def _(act):
            def w_upper(h, slot):
                act.wait_ge(w_in, 16 * h + 16)
                for k in range(5):
                    last = act.activation(wh[:, slot, k, :], raw[:, k, :], ACT.Copy, scale=gains[:, k:k + 1])
                last.then_inc(wh_done, 1)

            def v_upper(h, slot):
                wait_alone(act)
                act.activation(vh[:, slot, :, :], v[:, :, ds(h * MV, MV)], ACT.Copy).then_inc(vh_done, 1)

            def r_upper(pair):
                wait_alone(act)
                act.activation(rh[:, :], qrT[:, ds(pair, 1), :].rearrange("p a n -> p (a n)"), ACT.Copy).then_inc(rh_done, 1)

            def project_upper(h):
                for g, _, _, half in projections():
                    act.wait_ge(j_mm, 4 * h + g + 1)
                    dst, scale = ((qh, SCALE), (kh, 1.0))[g // 2]
                    act.activation(dst[:, half * HALF:(half + 1) * HALF], (j_ps, v_ps)[g % 2][:, :], ACT.Copy,
                                   scale=scale).then_inc(jh_done, 1)

            def transposed_upper(h, i):
                for g, k0, nk in groups(i):
                    act.wait_ge(T_mm, TG * h + g + 1)
                    if g == groups(i)[0][0] and (i > 1 or type(h) is not int or h):
                        act.wait_ge(v_mm, 4 * h + i // 2)
                    act.activation(pth[:, k0:k0 + nk, i % 2 * P:(i % 2 + 1) * P],
                                   T_ps[g % 2][:, 0:nk * P].rearrange("p (k n) -> p k n", n=P), ACT.Copy).then_inc(Th_done, 1)

            def exponential(h, i, older):
                act.wait_ge(max_done, NT * h + i + 1)
                if older >= 2:
                    act.wait_ge(T_mm, last_group(*before(h, i, 2)) + 1)
                w = (i + 1) * P
                act.activation(prob[:, i % 2, 0:w], s_ps[i % 2][:, :, :].rearrange("p a n -> p (a n)")[:, 0:w], ACT.Exp,
                               bias=nmax[:, i % 2:i % 2 + 1], accum_out=rsum[:, i % 2:i % 2 + 1]).then_inc(exp_done, 1)

            def head(h, u, first, last):
                for i in range(NT):
                    if i or not first:
                        transposed_upper(*before(h, i, 1))
                    exponential(h, i, i if first else 2)
                    if i == 2 and not last:
                        act.wait_ge(v_mm, 4 * h) if not first else None
                        v_upper(h + 1, 1 - u)
                        w_upper(h + 1, 1 - u)
                if not last:
                    if u == 1:
                        act.wait_ge(s_mm, NT * h + NT)
                        r_upper((h + 1) // 2)
                    project_upper(h + 1)

            act.wait_ge(gain_in, 16)
            w_upper(0, 0)
            v_upper(0, 0)
            r_upper(0)
            project_upper(0)
            heads(act, head)
            transposed_upper(H - 1, NT - 1)

        @block.gpsimd
        def _(pool):
            pool.memset(early[:, 0:P // 2], 1.0)
            pool.memset(early[:, P // 2:], 0.0)
            pool.memset(late[:, 0:P // 2], 0.0)
            pool.memset(late[:, P // 2:], FAR).then_inc(mask_done, 1)

        @block.vector
        def _(dve):
            def w_lower(h, slot):
                dve.wait_ge(wh_done, h + 1)
                for k in range(5):
                    last = dve.scalar_tensor_tensor(wl[:, slot, k, :], raw[:, k, :], gains[:, k:k + 1],
                                                    wh[:, slot, k, :].bitcast(F32), ALU.mult, ALU.subtract)
                last.then_inc(wl_done, 1)

            def v_lower(h, slot):
                dve.wait_ge(vh_done, h + 1)
                dve.tensor_tensor(vl[:, slot, :, :], v[:, :, ds(h * MV, MV)], vh[:, slot, :, :].bitcast(F32),
                                  ALU.subtract).then_inc(vl_done, 1)

            def r_lower(pair):
                dve.wait_ge(rh_done, pair + 1)
                dve.tensor_tensor(rl[:, :], qrT[:, ds(pair, 1), :].rearrange("p a n -> p (a n)"), rh[:, :].bitcast(F32),
                                  ALU.subtract).then_inc(rl_done, 1)

            def project_lower(h):
                for g, _, _, half in projections():
                    dve.wait_ge(jh_done, 4 * h + g + 1)
                    at = slice(half * HALF, (half + 1) * HALF)
                    if g < 2:
                        dve.scalar_tensor_tensor(ql[:, at], (j_ps, v_ps)[g % 2][:, :], SCALE, qh[:, at].bitcast(F32),
                                                 ALU.mult, ALU.subtract).then_inc(jl_done, 1)
                    else:
                        dve.tensor_tensor(kl[:, at], (j_ps, v_ps)[g % 2][:, :], kh[:, at].bitcast(F32),
                                          ALU.subtract).then_inc(jl_done, 1)

            def maximum(h, i):
                dve.wait_ge(s_mm, NT * h + i + 1)
                w = (i + 1) * P
                dve.tensor_reduce(nmax[:, i % 2:i % 2 + 1], s_ps[i % 2][:, :, :].rearrange("p a n -> p (a n)")[:, 0:w],
                                  AX_X, ALU.max, negate=True).then_inc(max_done, 1)

            def transposed_lower(h, i):
                for g, k0, nk in groups(i):
                    dve.wait_ge(Th_done, TG * h + g + 1)
                    at = (slice(None), slice(k0, k0 + nk), slice(i % 2 * P, (i % 2 + 1) * P))
                    dve.tensor_tensor(ptl[at], T_ps[g % 2][:, 0:nk * P].rearrange("p (k n) -> p k n", n=P),
                                      pth[at].bitcast(F32), ALU.subtract).then_inc(Tl_done, 1)

            def normalise(h, i):
                n = NT * h + i
                dve.wait_ge(exp_done, n + 1)
                dve.reciprocal(rinv[:, i % 2:i % 2 + 1], rsum[:, i % 2:i % 2 + 1]).then_inc(inv_done, 1)
                dve.wait_ge(inv_done, n + 1)
                w = (i + 1) * P
                dve.tensor_scalar(prob[:, i % 2, 0:w], prob[:, i % 2, 0:w], rinv[:, i % 2:i % 2 + 1], None,
                                  ALU.mult).then_inc(prob_done, 1)

            def gate(h, j, slot):
                dve.wait_ge(v_mm, 4 * h + j + 1)
                if j == 0:
                    dve.wait_ge(sg_in[slot], 8 * (h - slot) + 16)
                at = slice(2 * j * P, (2 * j + 2) * P)
                dve.tensor_tensor(sg[:, slot, at], v_ps[:, 0:2 * P], sg[:, slot, at], ALU.mult).then_inc(g_done, 1)

            def head(h, u, first, last):
                for i in range(NT):
                    if i:
                        maximum(h, i)
                        if i >= 3 and i % 2:
                            gate(h, (i - 3) // 2, u)
                        if i == 1 and not first:
                            gate(h - 1, 3, 1 - u)
                        transposed_lower(h, i - 1)
                    else:
                        if not first:
                            transposed_lower(h - 1, NT - 1)
                        maximum(h, 0)
                    normalise(h, i)
                    if i == 2 and not last:
                        v_lower(h + 1, 1 - u)
                        w_lower(h + 1, 1 - u)
                if not last:
                    if u == 1:
                        r_lower((h + 1) // 2)
                    project_lower(h + 1)

            dve.wait_ge(gain_in, 16)
            w_lower(0, 0)
            v_lower(0, 0)
            r_lower(0)
            project_lower(0)
            heads(dve, head)
            transposed_lower(H - 1, NT - 1)
            gate(H - 1, 3, 1)

        @block.tensor
        def _(pe):
            def three(out, pairs, start, stop):
                (ah, al), (bh, bl) = pairs
                pe.matmul(out, al, bh, start=start, stop=False)
                pe.matmul(out, ah, bl, start=False, stop=False)
                return pe.matmul(out, ah, bh, start=False, stop=stop)

            def project(h, slot):
                pe.wait_ge(wl_done, h + 1)
                for g, ks, (sh, sl), half in projections():
                    out = (j_ps, v_ps)[g % 2]
                    if g == 1 and (type(h) is not int or h):
                        pe.wait_ge(g_done, 4 * h - 1)
                    if g >= 2:
                        pe.wait_ge(jl_done, 4 * h + g - 1)
                    at = slice(half * HALF, (half + 1) * HALF)
                    for k in ks:
                        src = k - 2 if g < 2 else k
                        last = three(out[:, :], ((wh[:, slot, k, :], wl[:, slot, k, :]), (sh[:, src, at], sl[:, src, at])),
                                     k == ks[0], k == ks[-1])
                    last.then_inc(j_mm, 1)

            def scores(h, i, u, older):
                if older >= 2:
                    pe.wait_ge(exp_done, NT * h + i - 1)
                if i == 0:
                    pe.wait_ge(jl_done, 4 * h + 4)
                    if u == 0:
                        pe.wait_ge(rl_done, h // 2 + 1)
                q, r = slice(i * P, (i + 1) * P), slice(u * MROPE, (u + 1) * MROPE)
                for c in range(i // 4 + 1):
                    n = min(HALF, (i + 1) * P - c * HALF)
                    ks = slice(c * HALF, c * HALF + n)
                    out = s_ps[i % 2][:, c, 0:n]
                    three(out, ((qh[:, q], ql[:, q]), (kh[:, ks], kl[:, ks])), True, False)
                    last = three(out, ((rh[r, q], rl[r, q]), (kvh[r, 2, ks], kvl[r, 2, ks])), False, c < i // 4)
                    if c == i // 4:
                        last = pe.matmul(s_ps[i % 2][:, c, n - P:n], early[:, :], late[:, :], start=False, stop=True)
                last.then_inc(s_mm, 1)

            def transposes(h, i, older):
                pe.wait_ge(prob_done, NT * h + i + 1)
                for g, k0, nk in groups(i):
                    if older >= 2 or g >= 2:
                        pe.wait_ge(Tl_done, TG * h + g - 1)
                    for k in range(nk):
                        last = pe.transpose(T_ps[g % 2][:, k * P:(k + 1) * P],
                                            prob[:, i % 2, (k0 + k) * P:(k0 + k + 1) * P], ident[:])
                    last.then_inc(T_mm, 1)

            def values(h, j, slot):
                pe.wait_ge(Tl_done, last_group(h, 2 * j + 1) + 1)
                if j == 0:
                    pe.wait_ge(vl_done, h + 1)
                else:
                    pe.wait_ge(g_done, 4 * h + j)
                for k in range(2 * j + 2):
                    a = P if k == 2 * j + 1 else 0
                    last = three(v_ps[:, a:2 * P], ((vh[:, slot, k, :], vl[:, slot, k, :]), (pth[:, k, a:], ptl[:, k, a:])),
                                 k == 0, k == 2 * j + 1)
                last.then_inc(v_mm, 1)

            def head(h, u, first, last):
                for i in range(NT):
                    if i == 0 and not first:
                        transposes(h - 1, NT - 1, 2)
                    scores(h, i, u, i if first else 2)
                    if i == 1 and not first:
                        values(h - 1, 3, 1 - u)
                    if i >= 3 and i % 2:
                        values(h, (i - 3) // 2, u)
                    if i:
                        transposes(h, i - 1, i - 1 if first else 2)
                if not last:
                    project(h + 1, 1 - u)

            pe.wait_ge(mask_done, 1)
            project(0, 0)
            heads(pe, head)
            transposes(H - 1, NT - 1, 2)
            values(H - 1, 3, 1)
    return sems


def gla_masks():
    out = np.zeros((P, GLA_LEVELS, P // 2), np.uint32)
    for level in range(GLA_LEVELS):
        size = 1 << level
        for block in range(P // (2 * size)):
            out[2 * block * size:(2 * block + 1) * size, level, block * size:(block + 1) * size] = 1
    return out


def gla_columns(w_in):
    w = w_in.reshape(KT, P, -1)
    k, v = GLA_HEADS * GK, GLA_HEADS * GV
    qk = [w[:, :, i * k:(i + 1) * k].reshape(KT, P, GLA_HEADS, GK) for i in range(2)]
    vr = [w[:, :, 2 * k + i * v:2 * k + (i + 1) * v].reshape(KT, P, GLA_HEADS, GV) for i in range(2)]
    lay = lambda parts: np.ascontiguousarray(np.concatenate(parts, axis=3).transpose(2, 1, 0, 3))
    return lay(qk), lay(vr), np.ascontiguousarray(w[:, :, 2 * k + 2 * v:].transpose(1, 0, 2))


def gla_heads(nc, xT, g_mix, w_qk, w_vr, w_low, w_up, b_gk, masks, ident, neghalf, gated):
    with ExitStack() as ctx:
        def sb(name, shape, dt=F32):
            return ctx.enter_context(nc.sbuf_tensor("gl_" + name, shape, dt))

        def bank(name, shape=(P, HALF)):
            return ctx.enter_context(nc.psum_tensor("gl_" + name, list(shape), F32))

        def sem(name):
            return ctx.enter_context(nc.semaphore("gl_" + name))

        NL = GLA_LEVELS
        KD, QD, QK = NL, NL + 1, NL + 2
        BT = NT // 2
        INV_NORM = 1.0 / 16.0
        xh, xl = xT
        qkh = sb("qkh", [P, KT, 2 * GK], F32R)
        qkl = sb("qkl", [P, KT, 2 * GK], F32R)
        vrh = sb("vrh", [P, KT, 2 * GV], F32R)
        vrl = sb("vrl", [P, KT, 2 * GV], F32R)
        lowh = sb("lowh", [P, KT, GRANK], F32R)
        lowl = sb("lowl", [P, KT, GRANK], F32R)
        raw_low = sb("raw_low", [P, KT, GRANK])
        raw = sb("raw", [P, 2, DM])
        gain = sb("gain", [P, KT])
        bias = sb("bias", [P, GLA_HEADS])
        up = sb("up", [GRANK, GK])
        low = sb("low", [GRANK, SEQ])
        mn = sb("mn", [P, 2, SEQ])
        b = sb("b", [P, SEQ])
        lv = sb("lv", [P, 2, NL + 3, HALF])
        last_decay = sb("last_decay", [P, NT])
        q = sb("q", [P, SEQ])
        k = sb("k", [P, SEQ])
        v = sb("v", [P, 4, GV])
        sr = sb("sr", [P, NT, GV])
        oS = sb("oS", [P, 2, GV])
        osq = sb("osq", [P, GV])
        aT = sb("aT", [P, P])
        kt_ = sb("kt_", [P, P])
        R = sb("R", [P, GV])
        ones = sb("ones", [P, P])
        mask = sb("mask", [P, NL, P // 2], U32)
        so = sb("so", [P, 8])
        mo = sb("mo", [P, 2])
        ro = sb("ro", [P, 2])

        j_ps = bank("j_ps", (P, 2, HALF))
        vr_ps = [bank("vr_ps0"), bank("vr_ps1")]
        l_ps, T_ps, o_ps, k_ps = (bank(n) for n in ("l_ps", "T_ps", "o_ps", "k_ps"))

        gain_in, con_in, low_in, up_in = sem("gain_in"), sem("con_in"), sem("low_in"), sem("up_in")
        raw_in = [sem("raw_in0"), sem("raw_in1")]
        g_out = [sem(f"g_out{t}") for t in range(NT)]
        (ones_set, lowh_done, lowl_done, low_mm,
         low_copied, wh_done, wl_done, z_mm, mn_done, d_done, e_done, ln_done, la_done, b_done, sub_done, exp_done,
         mul_done, qk_mm, qk_copied, vr_mm, v_copied, silu_done, score_mm, part_done, mask_done, attend_mm, R_done,
         o_copied, sq_done, mo_done, ro_done, G_done) = (sem(n) for n in (
            "ones_set lowh_done lowl_done low_mm "
            "low_copied wh_done wl_done z_mm mn_done d_done e_done ln_done la_done b_done sub_done exp_done "
            "mul_done qk_mm qk_copied vr_mm v_copied silu_done score_mm part_done mask_done attend_mm R_done "
            "o_copied sq_done mo_done ro_done G_done").split())
        block = ctx.enter_context(nc.Block())
        H = GLA_HEADS
        LAST = H * NT
        PIECES = 6

        def before(h, t, n):
            return (h, t - n) if t >= n else (h - 1, t - n + NT)

        def piece_rows(i):
            if i < 2:
                return qkh, qkl, range(4 * i, 4 * i + 4), 2 * GK
            return vrh, vrl, range(2 * (i - 2), 2 * (i - 2) + 2), 2 * GV

        def heads(eng, head):
            head(0, 0, True)
            with eng.Fori(1, H - 1) as h:
                head(h, 1, True)
            head(H - 1, 1, False)

        @block.sync
        def _(sp):
            def load_piece(h, i, first=False):
                if not (first and i < 2):
                    sp.wait_ge(wl_done, PIECES * h + i - 1)
                _, _, rows, _ = piece_rows(i)
                src = w_qk if i < 2 else w_vr
                sp.dma_start(raw[:, i % 2, :], src[ds(h, 1), :, rows[0]:rows[-1] + 1, :].rearrange("a p k n -> p (a k n)"))\
                  .then_inc(raw_in[i % 2], 16)

            def load_up(h):
                sp.dma_start(up[:], w_up[:, ds(h * GK, GK)]).then_inc(up_in, 16)

            def store(s, h, t):
                sp.wait_ge(G_done, s + 1)
                sp.dma_start(gated[t * P:(t + 1) * P, ds(h * GV, GV)], sr[:, t, :]).then_inc(g_out[t], 16)

            def head(h, older, more):
                for t in range(NT):
                    if older or t >= 4:
                        store(h * NT + t - 4, *before(h, t, 4))
                    if more:
                        if t == 0:
                            load_piece(h + 1, 0)
                            load_piece(h + 1, 1)
                        if t == 2:
                            load_piece(h + 1, 2)
                            load_piece(h + 1, 3)
                            sp.wait_ge(z_mm, h + 1)
                            load_up(h + 1)
                if more:
                    load_piece(h + 1, 4)
                    load_piece(h + 1, 5)

            sp.dma_start(raw_low[:], w_low).then_inc(low_in, 16)
            sp.dma_start(gain[:], g_mix).then_inc(gain_in, 16)
            load_piece(0, 0, True)
            load_piece(0, 1, True)
            load_up(0)
            sp.dma_start(bias[:], b_gk).then_inc(con_in, 16)
            sp.dma_start(mask[:], masks).then_inc(con_in, 16)
            for i in range(2, PIECES):
                load_piece(0, i)
            heads(sp, head)
            for t in range(4, NT):
                store(LAST - NT + t, H - 1, t)
            for t in range(NT):
                sp.wait_ge(g_out[t], 16 * H)

        @block.scalar
        def _(act):
            def w_upper(h, i):
                up_, _, rows, n = piece_rows(i)
                act.wait_ge(raw_in[i % 2], 16 * (PIECES // 2 * h + i // 2 + 1))
                for j, r in enumerate(rows):
                    last = act.activation(up_[:, r, :], raw[:, i % 2, j * n:(j + 1) * n], ACT.Copy, scale=gain[:, r:r + 1])
                last.then_inc(wh_done, 1)

            def log_gates(h):
                act.wait_ge(d_done, h + 1)
                act.activation(mn[:, 1, :], mn[:, 1, :], ACT.Exp).then_inc(e_done, 1)
                act.wait_ge(e_done, h + 1)
                act.activation(mn[:, 1, :], mn[:, 1, :], ACT.Ln, bias=1.0).then_inc(ln_done, 1)

            def exponentials(h, c):
                act.wait_ge(sub_done, 2 * h + c + 1)
                act.activation(lv[:, c, 0:QD, :], lv[:, c, 0:QD, :], ACT.Exp, scale=INV_NORM)
                act.activation(lv[:, c, QD, :], b[:, c * HALF:(c + 1) * HALF], ACT.Exp, scale=INV_NORM)
                act.activation(last_decay[:, BT * c:BT * (c + 1)],
                               b[:, c * HALF:(c + 1) * HALF].rearrange("p (t n) -> p t n", n=P)[:, :, P - 1],
                               ACT.Exp, scale=INV_NORM).then_inc(exp_done, 1)

            def qk_copy(h, g):
                act.wait_ge(qk_mm, 4 * h + g + 1)
                dst, scale = ((q, GK ** -0.5), (k, 1.0))[g % 2]
                act.activation(dst[:, g // 2 * HALF:(g // 2 + 1) * HALF], j_ps[:, g % 2, :], ACT.Copy,
                               scale=scale).then_inc(qk_copied, 1)

            def evacuate(s, h, t, older):
                act.wait_ge(vr_mm, s + 1)
                if older or t >= 4:
                    act.wait_ge(attend_mm, s - 3)
                act.activation(v[:, t % 4, :], vr_ps[t % 2][:, 0:GV], ACT.Copy).then_inc(v_copied, 1)
                if older:
                    act.wait_ge(g_out[t], 16 * h)
                act.activation(sr[:, t, :], vr_ps[t % 2][:, GV:], ACT.Silu).then_inc(silu_done, 1)

            def output(s, t, older):
                act.wait_ge(attend_mm, s + 1)
                if older or t >= 2:
                    act.wait_ge(G_done, s - 1)
                act.activation(oS[:, t % 2, :], o_ps[:, 0:GV], ACT.Copy).then_inc(o_copied, 1)
                act.wait_ge(o_copied, s + 1)
                act.activation(osq[:, :], oS[:, t % 2, :], ACT.Square, accum_out=so[:, t % 2:t % 2 + 1]).then_inc(sq_done, 1)

            def head(h, older, more):
                for t in range(NT):
                    s = h * NT + t
                    evacuate(s, h, t, older)
                    if older or t >= 3:
                        _, tt = before(h, t, 3)
                        output(s - 3, tt, older if t >= 3 else older)
                    if more and t < 2:
                        w_upper(h + 1, t)
                    if t == 3:
                        exponentials(h, 1)
                    if more and t == 5:
                        log_gates(h + 1)
                    if more and t == 7:
                        exponentials(h + 1, 0)
                if more:
                    for g in range(4):
                        w_upper(h + 1, 2 + g)
                        qk_copy(h + 1, g)

            act.wait_ge(gain_in, 16)
            act.wait_ge(low_in, 16)
            for r in range(KT):
                last = act.activation(lowh[:, r, :], raw_low[:, r, :], ACT.Copy, scale=gain[:, r:r + 1])
            last.then_inc(lowh_done, 1)
            w_upper(0, 0)
            w_upper(0, 1)
            for half in range(2):
                act.wait_ge(low_mm, half + 1)
                act.activation(low[:, half * HALF:(half + 1) * HALF], vr_ps[half][0:GRANK, :], ACT.Copy).then_inc(low_copied, 1)
            log_gates(0)
            for g in range(4):
                qk_copy(0, g)
                w_upper(0, 2 + g)
                if g == 0:
                    exponentials(0, 0)
            heads(act, head)
            for s in range(LAST - 3, LAST):
                output(s, s % NT, 1)

        @block.gpsimd
        def _(pool):
            def rms_o(s, t):
                pool.wait_ge(sq_done, s + 1)
                wait_alone(pool)
                pool.tensor_scalar(mo[:, t % 2:t % 2 + 1], so[:, t % 2:t % 2 + 1], 1.0 / GV, EPS, ALU.mult, ALU.add)\
                    .then_inc(mo_done, 1)
                pool.wait_ge(mo_done, s + 1)
                pool.tensor_tensor(ro[:, t % 2:t % 2 + 1], mo[:, t % 2:t % 2 + 1], neghalf[:], ALU.pow).then_inc(ro_done, 1)

            pool.memset(ones[:], 1.0).then_inc(ones_set, 1)
            with pool.Fori(0, H) as h:
                for t in range(NT):
                    rms_o(h * NT + t, t)

        @block.vector
        def _(dve):
            def w_lower(h, i):
                up_, lo_, rows, n = piece_rows(i)
                dve.wait_ge(wh_done, PIECES * h + i + 1)
                for j, r in enumerate(rows):
                    last = dve.scalar_tensor_tensor(lo_[:, r, :], raw[:, i % 2, j * n:(j + 1) * n], gain[:, r:r + 1],
                                                    up_[:, r, :].bitcast(F32), ALU.mult, ALU.subtract)
                last.then_inc(wl_done, 1)

            def split_gates(h):
                z = j_ps[:, :, :].rearrange("p a n -> p (a n)")
                dve.wait_ge(z_mm, h + 1)
                dve.tensor_scalar(mn[:, 0, :], z, bias[:, ds(h, 1)], 0.0, ALU.add, ALU.min)
                dve.tensor_scalar(mn[:, 1, :], z, bias[:, ds(h, 1)], 0.0, ALU.add, ALU.max).then_inc(mn_done, 1)
                dve.wait_ge(mn_done, h + 1)
                dve.tensor_tensor(mn[:, 1, :], mn[:, 0, :], mn[:, 1, :], ALU.subtract).then_inc(d_done, 1)

            def sum_gates(h):
                dve.wait_ge(ln_done, h + 1)
                dve.tensor_tensor(mn[:, 0, :], mn[:, 0, :], mn[:, 1, :], ALU.subtract).then_inc(la_done, 1)
                dve.wait_ge(la_done, h + 1)
                for t in range(NT):
                    at = slice(t * P, (t + 1) * P)
                    last = dve.tensor_tensor_scan(b[:, at], ones[:, :], mn[:, 0, at], 0.0, ALU.mult, ALU.add)
                last.then_inc(b_done, 1)

            def exponents(h, c, older):
                dve.wait_ge(b_done, h + 1)
                if older:
                    dve.wait_ge(attend_mm, (h - 1) * NT + BT * c + BT)
                at = slice(c * HALF, (c + 1) * HALF)
                for level in range(NL):
                    n = 1 << level
                    src = b[:, at].rearrange("p (g u n) -> p g u n", u=2, n=n)
                    dst = lv[:, c, level, :].rearrange("p (g u n) -> p g u n", u=2, n=n)
                    mid = src[:, :, 0, n - 1:n].broadcast_to([P, HALF // (2 * n), n])
                    dve.tensor_tensor(dst[:, :, 0, :], mid, src[:, :, 0, :], ALU.subtract)
                    dve.tensor_tensor(dst[:, :, 1, :], src[:, :, 1, :], mid, ALU.subtract)
                src = b[:, at].rearrange("p (t n) -> p t n", n=P)
                dve.tensor_tensor(lv[:, c, KD, :].rearrange("p (t n) -> p t n", n=P),
                                  src[:, :, P - 1:P].broadcast_to([P, BT, P]), src, ALU.subtract).then_inc(sub_done, 1)

            def products(h, c):
                dve.wait_ge(exp_done, 2 * h + c + 1)
                dve.wait_ge(qk_copied, 4 * h + 2 * c + 2)
                at = slice(c * HALF, (c + 1) * HALF)
                for level in range(NL):
                    n = 1 << level
                    dst = lv[:, c, level, :].rearrange("p (g u n) -> p g u n", u=2, n=n)
                    for u, src in enumerate((k, q)):
                        dve.tensor_tensor(dst[:, :, u, :], dst[:, :, u, :],
                                          src[:, at].rearrange("p (g u n) -> p g u n", u=2, n=n)[:, :, u, :], ALU.mult)
                dve.tensor_tensor(lv[:, c, KD, :], lv[:, c, KD, :], k[:, at], ALU.mult)
                dve.tensor_tensor(lv[:, c, QD, :], lv[:, c, QD, :], q[:, at], ALU.mult)
                dve.tensor_tensor(lv[:, c, QK, :], q[:, at], k[:, at], ALU.mult).then_inc(mul_done, 1)

            def carry_state(s, t, older):
                dve.wait_ge(attend_mm, s + 1)
                if t == 0:
                    dve.tensor_copy(R[:, :], k_ps[:, 0:GV]).then_inc(R_done, 1)
                else:
                    dve.wait_ge(R_done, s)
                    dve.scalar_tensor_tensor(R[:, :], R[:, :], last_decay[:, t:t + 1], k_ps[:, 0:GV],
                                             ALU.mult, ALU.add).then_inc(R_done, 1)

            def gate(s, t):
                dve.wait_ge(ro_done, s + 1)
                dve.wait_ge(silu_done, s + 1)
                dve.scalar_tensor_tensor(sr[:, t, :], oS[:, t % 2, :], ro[:, t % 2:t % 2 + 1], sr[:, t, :],
                                         ALU.mult, ALU.mult).then_inc(G_done, 1)

            def gather_weights(s, older):
                dve.wait_ge(score_mm, s + 1)
                if older:
                    dve.wait_ge(attend_mm, s)
                dve.tensor_copy(kt_[:, :], T_ps[:, P:2 * P])
                dve.tensor_tensor(aT[:, :], T_ps[:, 0:P], ident[:], ALU.mult).then_inc(part_done, 1)
                for level in range(NL):
                    n = 1 << level
                    dve.wait_ge(part_done, NL * s + level + 1)
                    wait_alone(dve)
                    dst = aT[:, :].rearrange("p (g u n) -> p g u n", u=2, n=n)[:, :, 1, :]
                    last = dve.copy_predicated(dst, mask[:, level, :].rearrange("p (g n) -> p g n", n=n),
                                               l_ps[:, level * (P // 2):(level + 1) * (P // 2)].rearrange("p (g n) -> p g n", n=n))
                    last.then_inc(part_done if level < NL - 1 else mask_done, 1)

            def step(s, h, t, older):
                if older or t >= 3:
                    carry_state(s - 3, (t - 3) % NT, older)
                if older or t >= 4:
                    gate(s - 4, (t - 4) % NT)
                if older or t >= 2:
                    gather_weights(s - 2, older or t >= 3)

            def head(h, older, more):
                for t in range(NT):
                    step(h * NT + t, h, t, older)
                    if more and t < 2:
                        w_lower(h + 1, t)
                    if t == 3:
                        exponents(h, 1, older)
                    if t == 4:
                        products(h, 1)
                    if more and t == 5:
                        split_gates(h + 1)
                    if more and t == 6:
                        dve.wait_ge(exp_done, 2 * h + 2)
                        sum_gates(h + 1)
                    if more and t == 7:
                        exponents(h + 1, 0, 1)
                if more:
                    for i in range(2, PIECES):
                        w_lower(h + 1, i)
                    products(h + 1, 0)

            dve.wait_ge(gain_in, 16)
            dve.wait_ge(lowh_done, 1)
            for r in range(KT):
                last = dve.scalar_tensor_tensor(lowl[:, r, :], raw_low[:, r, :], gain[:, r:r + 1],
                                                lowh[:, r, :].bitcast(F32), ALU.mult, ALU.subtract)
            last.then_inc(lowl_done, 1)
            w_lower(0, 0)
            w_lower(0, 1)
            dve.wait_ge(con_in, 32)
            dve.wait_ge(ones_set, 1)
            split_gates(0)
            sum_gates(0)
            exponents(0, 0, 0)
            for i in range(2, PIECES):
                w_lower(0, i)
            products(0, 0)
            heads(dve, head)
            for s in range(LAST, LAST + 4):
                if s < LAST + 3:
                    carry_state(s - 3, s % NT + NT - 3, 1)
                gate(s - 4, s % NT + NT - 4)
                if s < LAST + 2:
                    gather_weights(s - 2, 1)

        @block.tensor
        def _(pe):
            def transposed_product(out, wh_, wl_, cols, half):
                at = slice(half * HALF, (half + 1) * HALF)
                for r in range(KT):
                    for i, (w, xx) in enumerate(((wl_, xh), (wh_, xl), (wh_, xh))):
                        last = pe.matmul(out, w[:, r, cols], xx[:, r, at], start=(r == 0 and i == 0),
                                         stop=(r == KT - 1 and i == 2))
                return last

            def gates(h):
                pe.wait_ge(up_in, 16 * h + 16)
                for half in range(2):
                    last = pe.matmul(j_ps[:, half, :], up[:, :], low[:, half * HALF:(half + 1) * HALF], start=True, stop=True)
                last.then_inc(z_mm, 1)

            def project_qk(h, older):
                pe.wait_ge(wl_done, PIECES * h + 2)
                pe.wait_ge(mn_done, h + 1)
                for g in range(4):
                    if g >= 2:
                        pe.wait_ge(qk_copied, 4 * h + g - 1)
                    transposed_product(j_ps[:, g % 2, :], qkh, qkl, slice(g % 2 * GK, (g % 2 + 1) * GK),
                                       g // 2).then_inc(qk_mm, 1)

            def project_vr(s, h, t, older):
                if t == 0:
                    pe.wait_ge(wl_done, PIECES * h + PIECES)
                if older or t >= 2:
                    pe.wait_ge(silu_done, s - 1)
                for r in range(KT):
                    for i, (xx, w) in enumerate(((xl, vrh), (xh, vrl), (xh, vrh))):
                        last = pe.matmul(vr_ps[t % 2][:, :], xx[:, r, t * P:(t + 1) * P], w[:, r, :],
                                         start=(r == 0 and i == 0), stop=(r == KT - 1 and i == 2))
                last.then_inc(vr_mm, 1)

            def attend(s, t, older):
                c, at = t // BT, slice(t % BT * P, (t % BT + 1) * P)
                pe.wait_ge(mask_done, s + 1)
                if older:
                    pe.wait_ge(o_copied, s)
                    pe.wait_ge(R_done, s)
                pe.matmul(o_ps[:, 0:GV], aT[:, :], v[:, t % 4, :], start=True, stop=(t == 0))
                if t:
                    pe.matmul(o_ps[:, 0:GV], lv[:, c, QD, at], R[:, :], start=False, stop=True)
                pe.matmul(k_ps[:, 0:GV], kt_[:, :], v[:, t % 4, :], start=True, stop=True).then_inc(attend_mm, 1)

            def scores(s, h, t, older):
                c, at = t // BT, slice(t % BT * P, (t % BT + 1) * P)
                pe.wait_ge(mul_done, 2 * h + c + 1)
                if older:
                    pe.wait_ge(mask_done, s)
                pe.matmul(T_ps[:, 0:P], ones[:, :], lv[:, c, QK, at], start=True, stop=True)
                pe.transpose(T_ps[:, P:2 * P], lv[:, c, KD, at], ident[:])
                for level in range(NL):
                    n = 1 << level
                    last = pe.matmul(l_ps[:, level * (P // 2):(level + 1) * (P // 2)].rearrange("p (g n) -> p g n", n=n),
                                     lv[:, c, level, at],
                                     lv[:, c, level, at].rearrange("p (g u n) -> p g u n", u=2, n=n)[:, :, 1, :],
                                     start=True, stop=True)
                last.then_inc(score_mm, 1)

            def head(h, older, more):
                for t in range(NT):
                    s = h * NT + t
                    project_vr(s, h, t, older)
                    if older or t >= 3:
                        attend(s - 3, before(h, t, 3)[1], older or t >= 4)
                    if older or t >= 2:
                        hh, tt = before(h, t, 2)
                        scores(s - 2, hh, tt, older or t >= 3)
                    if more and t == 4:
                        pe.wait_ge(qk_copied, 4 * h + 4)
                        gates(h + 1)
                if more:
                    pe.wait_ge(mul_done, 2 * h + 2)
                    project_qk(h + 1, 1)

            pe.wait_ge(ones_set, 1)
            pe.wait_ge(lowl_done, 1)
            for half in range(2):
                transposed_product(vr_ps[half][0:GRANK, :], lowh, lowl, slice(0, GRANK), half).then_inc(low_mm, 1)
            pe.wait_ge(low_copied, 2)
            gates(0)
            project_qk(0, 0)
            heads(pe, head)
            for s in range(LAST, LAST + 3):
                attend(s - 3, s % NT + NT - 3, 1)
                if s < LAST + 2:
                    scores(s - 2, H - 1, s % NT + NT - 2, 1)


def feed_forward(nc, x, xT, g_pre, w1, w2, g_final, ident, neghalf, out):
    with ExitStack() as ctx:
        def sb(name, shape, dt=F32):
            return ctx.enter_context(nc.sbuf_tensor("ff_" + name, shape, dt))

        def sem(name):
            return ctx.enter_context(nc.semaphore("ff_" + name))

        NC = D_FF // HALF
        FT = HALF // P
        xh, xl = xT
        w1h = sb("w1h", [P, KT, HALF], F32R)
        w1l = sb("w1l", [P, KT, HALF], F32R)
        w2h = sb("w2h", [P, FT, DM], F32R)
        w2l = sb("w2l", [P, FT, DM], F32R)
        hh = sb("hh", [P, FT, SEQ], F32R)
        hl = sb("hl", [P, FT, SEQ], F32R)
        acc = sb("acc", [P, NT, DM])
        raw = sb("raw", [P, 2, DM])
        relu = sb("relu", [P, HALF])
        gain = sb("gain", [P, KT])
        ss = sb("ss", [P, NT])
        ms = sb("ms", [P, NT])
        rms = sb("rms", [P, NT])
        f_ps = [ctx.enter_context(nc.psum_tensor(f"ff_f_ps{i}", [P, HALF], F32)) for i in range(2)]
        y_ps = [ctx.enter_context(nc.psum_tensor(f"ff_y_ps{i}", [P, 2, HALF], F32)) for i in range(2)]

        raw_in = [sem("raw_in0"), sem("raw_in1")]
        x_in = [sem("x_in0"), sem("x_in1")]
        (gain_in, final_in, out_done, ss_done, ms_done, rms_done, wh_done,
         wl_done, f_mm, relu_done, sq_done, hh_done, hl_done, y_mm, y_added, fin_done) = (
            sem(n) for n in ("gain_in final_in out_done ss_done ms_done rms_done "
                             "wh_done wl_done f_mm relu_done sq_done hh_done hl_done y_mm y_added fin_done").split())
        block = ctx.enter_context(nc.Block())

        @block.sync
        def _(sp):
            def load_w(c, n):
                if n < 4:
                    src = w1[ds(c, 1), :, 2 * n:2 * n + 2, :].rearrange("a p k n -> p (a k n)")
                else:
                    src = w2[ds(c * HALF + (n - 4) * P, P), :]
                sp.dma_start(raw[:, n % 2, :], src).then_inc(raw_in[n % 2], 16)

            def load_x(i):
                sp.dma_start(acc[:, 4 * i:4 * i + 4, :], x[i * HALF:(i + 1) * HALF, :].rearrange("(t p) n -> p t n", p=P))\
                  .then_inc(x_in[i], 16)

            load_w(0, 0)
            sp.dma_start(gain[:], g_pre).then_inc(gain_in, 16)
            load_w(0, 1)
            for n in range(2, 8):
                sp.wait_ge(wl_done, n - 1)
                load_w(0, n)
                if n >= 6:
                    load_x(n - 6)
            with sp.Fori(1, NC) as c:
                for n in range(8):
                    sp.wait_ge(wl_done, 8 * c + n - 1)
                    load_w(c, n)
            sp.wait_ge(wl_done, 8 * NC)
            sp.dma_start(raw[:, 0, :], g_final.partition_broadcast(P)).then_inc(final_in, 16)
            for t in range(NT):
                sp.wait_ge(fin_done, t + 1)
                sp.dma_start(out[t * P:(t + 1) * P, :], acc[:, t, :]).then_inc(out_done, 16)
            sp.wait_ge(out_done, 16 * NT)

        @block.scalar
        def _(act):
            def square(t):
                act.activation(xl[:, :, t * P:(t + 1) * P], acc[:, t, :].rearrange("p (k n) -> p k n", k=KT), ACT.Square,
                               accum_out=ss[:, t:t + 1]).then_inc(ss_done, 1)

            def w_upper(c, n):
                act.wait_ge(raw_in[n % 2], 64 * c + 16 * (n // 2) + 16)
                if n < 4:
                    for k in range(2):
                        kt = 2 * n + k
                        last = act.activation(w1h[:, kt, :], raw[:, n % 2, k * HALF:(k + 1) * HALF], ACT.Copy,
                                              scale=gain[:, kt:kt + 1])
                else:
                    last = act.activation(w2h[:, n - 4, :], raw[:, n % 2, :], ACT.Copy)
                last.then_inc(wh_done, 1)

            def h_upper(c, j):
                act.wait_ge(sq_done, 8 * c + j + 1)
                act.activation(hh[:, j % 4, j // 4 * HALF:(j // 4 + 1) * HALF], f_ps[j % 2][:, :], ACT.Copy).then_inc(hh_done, 1)

            def groups(c):
                for j in range(8):
                    act.wait_ge(f_mm, 8 * c + j + 1)
                    act.activation(relu[:, :], f_ps[j % 2][:, :], ACT.Relu).then_inc(relu_done, 1)
                    h_upper(c, j)
                    if j % 2 == 0:
                        w_upper(c, 4 + j // 2)

            act.wait_ge(gain_in, 16)
            for n in range(4):
                w_upper(0, n)
            groups(0)
            with act.Fori(1, NC) as c:
                act.wait_ge(f_mm, 8 * c)
                for n in range(4):
                    w_upper(c, n)
                groups(c)
            for t in range(NT):
                act.wait_ge(y_added, NT * (NC - 1) + t + 1)
                square(t)

        @block.gpsimd
        def _(pool):
            for i in range(NT):
                pool.wait_ge(ss_done, i + 1)
                pool.tensor_scalar(ms[:, i:i + 1], ss[:, i:i + 1], 1.0 / DM, EPS, ALU.mult, ALU.add).then_inc(ms_done, 1)
                pool.wait_ge(ms_done, i + 1)
                pool.tensor_tensor(rms[:, i:i + 1], ms[:, i:i + 1], neghalf[:], ALU.pow).then_inc(rms_done, 1)

        @block.vector
        def _(dve):
            def w_lower(c, n):
                dve.wait_ge(wh_done, 8 * c + n + 1)
                if n < 4:
                    for k in range(2):
                        kt = 2 * n + k
                        last = dve.scalar_tensor_tensor(w1l[:, kt, :], raw[:, n % 2, k * HALF:(k + 1) * HALF],
                                                        gain[:, kt:kt + 1], w1h[:, kt, :].bitcast(F32),
                                                        ALU.mult, ALU.subtract)
                else:
                    last = dve.tensor_tensor(w2l[:, n - 4, :], raw[:, n % 2, :], w2h[:, n - 4, :].bitcast(F32), ALU.subtract)
                last.then_inc(wl_done, 1)

            def square_of(c, j):
                dve.wait_ge(relu_done, 8 * c + j + 1)
                dve.scalar_tensor_tensor(f_ps[j % 2][:, :], f_ps[j % 2][:, :], 0.0, relu[:, :], ALU.max,
                                         ALU.mult).then_inc(sq_done, 1)

            def h_lower(c, j):
                dve.wait_ge(hh_done, 8 * c + j + 1)
                at = (j % 4, slice(j // 4 * HALF, (j // 4 + 1) * HALF))
                dve.tensor_tensor(hl[:, at[0], at[1]], f_ps[j % 2][:, :], hh[:, at[0], at[1]].bitcast(F32),
                                  ALU.subtract).then_inc(hl_done, 1)

            def groups(c):
                for j in range(8):
                    square_of(c, j)
                    h_lower(c, j)
                    if j % 2 == 0:
                        w_lower(c, 4 + j // 2)

            def add(c, t):
                dve.wait_ge(y_mm, NT * c + t + 1)
                dve.tensor_tensor(acc[:, t, :], y_ps[t % 2][:, :, :].rearrange("p a n -> p (a n)"), acc[:, t, :],
                                  ALU.add).then_inc(y_added, 1)

            dve.wait_ge(gain_in, 16)
            for n in range(4):
                w_lower(0, n)
            groups(0)
            for i in range(2):
                dve.wait_ge(x_in[i], 16)
            with dve.Fori(1, NC) as c:
                for t in range(NT):
                    add(c - 1, t)
                    if t < 4:
                        w_lower(c, t)
                groups(c)
            dve.wait_ge(final_in, 16)
            for t in range(NT):
                add(NC - 1, t)
                if t:
                    dve.wait_ge(rms_done, t)
                    dve.scalar_tensor_tensor(acc[:, t - 1, :], acc[:, t - 1, :], rms[:, t - 1:t], raw[:, 0, :],
                                             ALU.mult, ALU.mult).then_inc(fin_done, 1)
            dve.wait_ge(rms_done, NT)
            dve.scalar_tensor_tensor(acc[:, NT - 1, :], acc[:, NT - 1, :], rms[:, NT - 1:NT], raw[:, 0, :],
                                     ALU.mult, ALU.mult).then_inc(fin_done, 1)

        @block.tensor
        def _(pe):
            def inner(c, j):
                first = type(c) is int and c == 0
                if j >= 2 or not first:
                    pe.wait_ge(hl_done, 8 * c + j - 1)
                f, half = j % 4, j // 4
                for kt in range(KT):
                    if first and j == 0 and kt % 2 == 0:
                        pe.wait_ge(wl_done, kt // 2 + 1)
                    for i, (a, b) in enumerate(((w1l, xh), (w1h, xl), (w1h, xh))):
                        last = pe.matmul(f_ps[j % 2][:, :], a[:, kt, f * P:(f + 1) * P], b[:, kt, half * HALF:(half + 1) * HALF],
                                         start=(kt == 0 and i == 0), stop=(kt == KT - 1 and i == 2))
                last.then_inc(f_mm, 1)

            def outer(c, t):
                if t % 4 == 0:
                    pe.wait_ge(hl_done, 8 * c + t + 4)
                if t >= 2 or type(c) is not int:
                    pe.wait_ge(y_added, NT * c + t - 1)
                for f in range(FT):
                    for n in range(2):
                        for i, (a, b) in enumerate(((hl, w2h), (hh, w2l), (hh, w2h))):
                            last = pe.matmul(y_ps[t % 2][:, n, :], a[:, f, t * P:(t + 1) * P], b[:, f, n * HALF:(n + 1) * HALF],
                                             start=(f == 0 and i == 0), stop=(f == FT - 1 and i == 2))
                last.then_inc(y_mm, 1)

            for j in range(8):
                inner(0, j)
            pe.wait_ge(wl_done, 8)
            for t in range(NT):
                outer(0, t)
            with pe.Fori(1, NC) as c:
                pe.wait_ge(wl_done, 8 * c + 4)
                for j in range(8):
                    inner(c, j)
                pe.wait_ge(wl_done, 8 * c + 8)
                for t in range(NT):
                    outer(c, t)


def latent_gains(g_kv_lat, g_q_lat):
    return np.ascontiguousarray(np.concatenate([columns(g_kv_lat), columns(g_q_lat)], axis=1))


def build(nc, t, out):
    def scratch(name, shape):
        return nc.dram_tensor(name, shape, F32).ap()

    gated_a = scratch("gated_a", (SEQ, RET_W))
    x1 = scratch("x1", (SEQ, DM))
    silu_gate = scratch("silu_gate", (DM, SEQ))
    gated_b = scratch("gated_b", (DM, SEQ))
    x2 = scratch("x2", (SEQ, DM))
    gated_c = scratch("gated_c", (SEQ, DM))
    x3 = scratch("x3", (SEQ, DM))
    con = {name[4:]: ap for name, ap in t.items() if name.startswith("con_")}

    with ExitStack() as whole:
        ident = whole.enter_context(nc.sbuf_tensor("ident", [P, P], F32))
        neghalf = whole.enter_context(nc.sbuf_tensor("neghalf", [P, 1], F32))
        ident_in = whole.enter_context(nc.semaphore("ident_in"))
        neghalf_set = whole.enter_context(nc.semaphore("neghalf_set"))
        with nc.Block() as block:
            @block.sync
            def _(sp):
                sp.dma_start(ident[:], con["identity"]).then_inc(ident_in, 16)
                sp.wait_ge(ident_in, 16)

            @block.vector
            def _(dve):
                dve.memset(neghalf[:], -0.5).then_inc(neghalf_set, 1)

        used = retention_heads(nc, t["x"], t["g_pre_a"], t["w_in_a"], con, ident, neghalf, gated_a)
        used += close_mixer(nc, "wa_", gated_a, t["w_out_a"], t["gn_gain_a"], t["x"], t["g_post_a"], ident, neghalf, x1)

        with ExitStack() as ctx:
            def sb(name, shape, dt=F32):
                return ctx.enter_context(nc.sbuf_tensor(name, shape, dt))

            kv = sb("kv_upper", [P, 3, SEQ], F32R), sb("kv_lower", [P, 3, SEQ], F32R)
            cq = sb("cq_upper", [P, 3, SEQ], F32R), sb("cq_lower", [P, 3, SEQ], F32R)
            used += latents(nc, x1, t["g_kv"], t["g_pre_b"], t["w_latents"], t["w_gate_b"], con, ident, neghalf, kv, cq, silu_gate)
            v = sb("values", [P, NT, DM])
            qrT = sb("rotary_queries", [P, 4, SEQ])
            used += values_and_rotary(nc, kv, cq, t["g_latents"], t["w_uv"], t["w_uq_rotary"], con, ident, v, qrT)
            used += attention(nc, kv, cq, v, qrT, t["g_latents"], t["w_heads_b"], silu_gate, ident, gated_b)

        clear_semaphores(nc, used)

        xT = tuple(whole.enter_context(nc.sbuf_tensor(name, [P, KT, SEQ], F32R)) for name in ("x_upper", "x_lower"))
        close_mixer(nc, "wb_", gated_b, t["w_out_b"], None, x1, t["g_post_b"], ident, neghalf, x2, feature_major=True, xT=xT)

        gla_heads(nc, xT, t["g_mix"], t["w_qk_c"], t["w_vr_c"], t["w_low_c"], t["w_gk_up"], t["b_gk"], con["gla_masks"],
                  ident, neghalf, gated_c)
        close_mixer(nc, "wc_", gated_c, t["w_out_c"], t["g_onorm"], x2, None, ident, neghalf, x3, xT=xT)
        feed_forward(nc, x3, xT, t["g_ffn"], t["w_ff1"], t["w_ff2"], t["g_final"], ident, neghalf, out)


def lay_out(i):
    w_qk, w_vr, w_low = gla_columns(i["l0_w_in_2"])
    arrays = {
        "x": i["x"][0], "g_pre_a": columns(i["g_pre_a"][0]), "w_in_a": retention_columns(i["w_in_a"][0]),
        "gn_gain_a": columns(i["gn_gain_a"][0]), "w_out_a": i["w_out_a"][0], "g_post_a": i["g_post_a"][0],
        "g_kv": columns(i["g_kv"]), "g_pre_b": columns(i["g_pre_b"][0]),
        "w_latents": latent_columns(i["w_kv_a"], i["w_in_b"][0]), "w_gate_b": gate_units(i["w_in_b"][0]),
        "g_latents": latent_gains(i["g_kv_lat"], i["g_q_lat"][0]), "w_uv": row_tiles(i["w_uv"]),
        "w_uq_rotary": rotary_columns(i["w_uq"][0]), "w_heads_b": head_weights(i["w_uk"], i["w_uq"][0]),
        "w_out_b": i["w_out_b"][0], "g_post_b": i["g_post_b"][0],
        "g_mix": columns(i["l0_norm_mix_2"]), "w_qk_c": w_qk, "w_vr_c": w_vr, "w_low_c": w_low,
        "w_gk_up": i["l0_w_gk_up_2"], "b_gk": columns(i["l0_b_gk_2"]), "g_onorm": columns(i["l0_g_onorm_2"]),
        "w_out_c": i["l0_w_out_2"], "g_ffn": columns(i["l0_norm_ffn_2"]), "w_ff1": ff1_chunks(i["l0_w_ff1_2"]),
        "w_ff2": i["l0_w_ff2_2"], "g_final": i["final_norm_2"],
    }
    for name, value in shape_constants().items():
        arrays["con_" + name] = value
    return {name: np.ascontiguousarray(a) for name, a in arrays.items()}


def kernel(**inputs):
    import numpy as _np
    import concourse.bacc as _bacc
    from concourse.bass_utils import run_bass_kernel_spmd as _run

    nc = _bacc.Bacc("TRN2", target_bir_lowering=False, num_devices=1)
    laid = lay_out({name: _np.asarray(a) for name, a in inputs.items()})
    arrays = {"in_" + name: a for name, a in laid.items()}
    tensors = {name: nc.dram_tensor("in_" + name, a.shape, mybir.dt.from_np(a.dtype), kind="ExternalInput").ap()
               for name, a in laid.items()}
    out = nc.dram_tensor("out_0", (SEQ, DM), F32, kind="ExternalOutput").ap()
    build(nc, tensors, out)
    r = _run(nc, [arrays], core_ids=[0])
    return r.results[0]["out_0"].reshape(1, SEQ, DM)
```

```python
from contextlib import ExitStack

import concourse.bass as bass
import numpy as np
from concourse import mybir

F32 = mybir.dt.float32
F32R = mybir.dt.float32r
BF16 = mybir.dt.bfloat16
U32 = mybir.dt.uint32
ALU = mybir.AluOpType
ACT = mybir.ActivationFunctionType
AX_X = mybir.AxisListType.X
ds = bass.ds

P = 128
SEQ = 1024
DM = 1024
NT = SEQ // P
KT = DM // P
HALF = 512
EPS = 1e-6

RET_HEADS = 8
RQK = DM // RET_HEADS
RV = 2 * RQK
RET_CHUNK = 64
RET_W = RET_HEADS * RV

MLA_HEADS = 8
NOPE, MROPE, MV = 128, 64, 128
Q_LORA, KV_LORA = 384, 256

GLA_HEADS = 4
GK = 128
GV = 256
GRANK = 16
GLA_LEVELS = 7
D_FF = 4 * DM


def shape_constants():
    f = np.float32
    out = {}
    out["identity"] = np.eye(P, dtype=f)

    def rotary(width):
        half = width // 2
        inv = (f(10000.0) ** (-np.arange(half, dtype=f) / f(half))).astype(f)
        ang = np.arange(SEQ, dtype=f)[:, None] * inv[None, :]
        lay = lambda a: np.ascontiguousarray(a.astype(f).reshape(NT, P, half).transpose(1, 0, 2))
        return lay(np.cos(ang)), lay(np.sin(ang))

    out["cos_ret"], out["sin_ret"] = rotary(RQK)
    out["cos_mla"], out["sin_mla"] = rotary(MROPE)
    log_g = np.log(1.0 - np.exp2(-5.0 - np.arange(RET_HEADS, dtype=np.float64)))
    pos = np.arange(P)
    m, c = pos[:, None], pos[None, :]
    sees = (m // RET_CHUNK) <= (c // RET_CHUNK)
    dec = np.where(sees[None], np.exp(log_g[:, None, None] * (np.abs(m - c) - (c + 1))[None]), 0.0) * RQK ** -0.5
    out["ret_decay"] = np.ascontiguousarray(dec.transpose(1, 0, 2).astype(f))
    out["ret_xi"] = np.exp(log_g[None, :] * (pos[:, None] + 1)).astype(f)
    out["ret_zeta"] = (np.exp(log_g[None, :] * (P - 1 - pos[:, None])) * RQK ** -0.5).astype(f)
    out["gla_masks"] = gla_masks()
    out["ret_carry"] = np.broadcast_to(np.exp(log_g * P)[None, :], (P, RET_HEADS)).astype(f).copy()
    return out


def columns(vector):
    return np.ascontiguousarray(vector.reshape(-1, P).T)


def retention_columns(w):
    w = w.reshape(KT, P, -1)
    parts = [w[:, :, 0:DM].reshape(KT, P, RET_HEADS, RQK), w[:, :, DM:2 * DM].reshape(KT, P, RET_HEADS, RQK),
             w[:, :, 2 * DM:2 * DM + RET_W].reshape(KT, P, RET_HEADS, RV),
             w[:, :, 2 * DM + RET_W:].reshape(KT, P, RET_HEADS, RV)]
    return np.ascontiguousarray(np.concatenate(parts, axis=3).transpose(2, 1, 0, 3))


def wait_alone(eng):
    eng.nop(nofuse=True)


def ff1_chunks(w):
    return np.ascontiguousarray(w.reshape(KT, P, D_FF // HALF, HALF).transpose(2, 1, 0, 3))


def row_tiles(w):
    return np.ascontiguousarray(w.reshape(-1, P, w.shape[1]).transpose(1, 0, 2))


def latent_columns(w_kv_a, w_in):
    return row_tiles(np.concatenate([w_kv_a, w_in[:, :Q_LORA]], axis=1))


def gate_units(w_in):
    return np.ascontiguousarray(w_in[:, Q_LORA:].reshape(KT, P, 2, HALF).transpose(2, 1, 0, 3))


def head_weights(w_uk, w_uq):
    uk = w_uk.reshape(2, P, MLA_HEADS, NOPE)
    uq = w_uq.reshape(3, P, MLA_HEADS, NOPE + MROPE)[:, :, :, :NOPE]
    return np.ascontiguousarray(np.concatenate([uk, uq], axis=0).transpose(2, 1, 0, 3))


def rotary_columns(w_uq):
    w = w_uq.reshape(Q_LORA, MLA_HEADS, NOPE + MROPE)[:, :, NOPE:]
    return row_tiles(np.ascontiguousarray(w).reshape(Q_LORA, MLA_HEADS * MROPE))


def clear_semaphores(nc, sems):
    numbers = sorted(s.num for s in sems)
    assert numbers == list(range(numbers[0], numbers[-1] + 1))
    with nc.Block() as block:
        @block.gpsimd
        def _(pool):
            pool.sem_clear(range(numbers[0], numbers[-1] + 1))


def values_and_rotary_units(w_uv, w_uq):
    return np.ascontiguousarray(np.concatenate([row_tiles(w_uv).reshape(P, 4, HALF), rotary_columns(w_uq)], axis=1))


def retention_heads(nc, x, gain, w_in, con, ident, neghalf, staging, ahead, gated):
    with ExitStack() as ctx:
        def sb(name, shape, dt=F32):
            return ctx.enter_context(nc.sbuf_tensor("ra_" + name, shape, dt))

        def bank(name):
            return ctx.enter_context(nc.psum_tensor("ra_" + name, [P, HALF], F32))

        sems = []

        def sem(name):
            sems.append(ctx.enter_context(nc.semaphore("ra_" + name)))
            return sems[-1]

        QKV = 2 * RQK + RV
        WC = QKV + RV
        xh = sb("xh", [P, KT, SEQ], F32R)
        xl = sb("xl", [P, KT, SEQ], F32R)
        wh = sb("wh", [P, 2, KT, WC], F32R)
        wl = sb("wl", [P, 2, KT, WC], F32R)
        raw = sb("raw", [P, 2, 2, WC])
        xin = staging
        cos = sb("cos", [P, NT, RQK // 2])
        sin = sb("sin", [P, NT, RQK // 2])
        decay = sb("decay", [P, RET_HEADS, P])
        xi = sb("xi", [P, RET_HEADS])
        zeta = sb("zeta", [P, RET_HEADS])
        carry = sb("carry", [P, RET_HEADS])
        qkv = sb("qkv", [P, 2, QKV])
        rot = sb("rot", [P, 2, 2, RQK])
        rtmp = sb("rtmp", [P, 2, RQK])
        kz = sb("kz", [P, 2, RQK])
        qkT = sb("qkT", [P, 2, 2, P])
        sT = sb("sT", [P, P])
        R = sb("R", [P, RV])
        sg = sb("sg", [P, 4, RV])
        oS = sb("oS", [P, 2, RV])
        bn = sb("bn", [P, 6])
        mv = sb("mv", [P, 2, 2])
        rstd = sb("rstd", [P, 2, 2])
        ss = sb("ss", [P, NT])
        rx = sb("rx", [P, 2, NT])

        qkv_ps = [bank("qkv_ps0"), bank("qkv_ps1")]
        x_ps, gate_ps, T_ps, s_ps, o_ps, k_ps = (
            bank(n) for n in ("x_ps", "gate_ps", "T_ps", "s_ps", "o_ps", "k_ps"))

        con_in = sem("con_in")
        x_in = [sem("x_in0"), sem("x_in1")]
        raw_in = [sem("raw_in0"), sem("raw_in1")]
        g_out = [sem(f"g_out{i}") for i in range(4)]
        (ss_done, rms_part, rms_done, xn_done, xT_mm, xh_done, xl_done, wh_done, wl_done, qkv_mm, qkv_copied,
         rot_part, rot_done, kz_done, T_mm, T_copied, s_mm, sT_done, attend_mm, R_done, o_copied, gate_mm,
         silu_done, bn_part, mv_done, rstd_part, rstd_done, norm_part, G_done) = (sem(n) for n in (
            "ss_done rms_part rms_done xn_done xT_mm xh_done xl_done wh_done wl_done qkv_mm qkv_copied "
            "rot_part rot_done kz_done T_mm T_copied s_mm sT_done attend_mm R_done o_copied gate_mm "
            "silu_done bn_part mv_done rstd_part rstd_done norm_part G_done").split())
        block = ctx.enter_context(nc.Block())
        LAST = RET_HEADS * NT
        N_CON = 6

        @block.sync
        def _(sp):
            def load_x(t):
                if t >= 2:
                    sp.wait_ge(xT_mm, 2 * (t - 1))
                sp.dma_start(xin[:, t % 2, :], x[t * P:(t + 1) * P, :]).then_inc(x_in[t % 2], 16)

            def load_raw(h, kt):
                slot = kt // 2 % 2
                sp.dma_start(raw[:, slot, :, :], w_in[ds(h, 1), :, kt:kt + 2, :].rearrange("a p k n -> p (a k) n"))\
                  .then_inc(raw_in[slot], 16)

            def store(s, h, t):
                sp.wait_ge(G_done, s + 1)
                sp.dma_start(gated[t * P:(t + 1) * P, ds(h * RV, RV)], sg[:, t % 4, :]).then_inc(g_out[t % 4], 16)

            def head(h, first, more):
                for t in range(NT):
                    if first and t + 2 < NT:
                        load_x(t + 2)
                    if more and t % 2 == 0:
                        sp.wait_ge(wl_done, KT * h + KT + t - 2)
                        load_raw(h + 1, t)
                    if t >= 3:
                        store(h * NT + t - 3, h, t - 3)
                    elif not first:
                        store(h * NT + t - 3, h - 1, NT + t - 3)

            load_x(0)
            load_raw(0, 0)
            load_x(1)
            load_raw(0, 2)
            for dst, name in ((cos, "cos_ret"), (sin, "sin_ret"), (decay, "ret_decay"), (xi, "ret_xi"),
                              (zeta, "ret_zeta"), (carry, "ret_carry")):
                sp.dma_start(dst[:], con[name]).then_inc(con_in, 16)
            for kt in range(4, KT, 2):
                sp.wait_ge(wl_done, kt - 2)
                load_raw(0, kt)
            head(0, True, True)
            sp.wait_ge(xT_mm, 2 * NT)
            ahead(sp)
            with sp.Fori(1, RET_HEADS - 1) as h:
                head(h, False, True)
            head(RET_HEADS - 1, False, False)
            for t in range(NT - 3, NT):
                store(LAST - NT + t, RET_HEADS - 1, t)
            for slot in range(4):
                sp.wait_ge(g_out[slot], 16 * LAST // 4)

        @block.scalar
        def _(act):
            def square_x(t):
                act.wait_ge(x_in[t % 2], 16 * (t // 2 + 1))
                act.activation(xl[:, :, t * P:(t + 1) * P], xin[:, t % 2, :].rearrange("p (k n) -> p k n", k=KT), ACT.Square, accum_out=ss[:, t:t + 1]).then_inc(ss_done, 1)

            def x_upper(t, half):
                act.wait_ge(xT_mm, 2 * t + half + 1)
                act.activation(xh[:, 4 * half:4 * half + 4, t * P:(t + 1) * P],
                               x_ps[:, :].rearrange("p (k n) -> p k n", k=4), ACT.Copy).then_inc(xh_done, 1)

            def w_upper(h, slot, kt):
                act.wait_ge(raw_in[kt // 2 % 2], 16 * (h * 2 + kt // 4 + 1))
                wait_alone(act)
                act.activation(wh[:, ds(slot, 1), kt, :].rearrange("p a n -> p (a n)"), raw[:, kt // 2 % 2, kt % 2, :],
                               ACT.Copy, scale=gain[:, kt:kt + 1]).then_inc(wh_done, 1)

            def step(s, h, t, older):
                hp = h if t >= 2 else h - 1
                if older >= 1:
                    act.wait_ge(T_mm, s)
                    act.activation(qkT[:, (t - 1) % 2, :, :], T_ps[:, 0:2 * P].rearrange("p (a n) -> p a n", a=2),
                                   ACT.Copy).then_inc(T_copied, 1)
                if older >= 2:
                    act.wait_ge(attend_mm, s - 1)
                act.wait_ge(qkv_mm, s + 1)
                act.activation(qkv[:, t % 2, :], qkv_ps[t % 2][:, :], ACT.Copy).then_inc(qkv_copied, 1)
                if older >= 2:
                    if older >= 4:
                        act.wait_ge(G_done, s - 3)
                    wait_alone(act)
                    act.activation(oS[:, t % 2, :], o_ps[:, 0:RV], ACT.Copy, scale=xi[:, ds(hp, 1)]).then_inc(o_copied, 1)

            def silu(s, h, t, older):
                act.wait_ge(gate_mm, s + 1)
                if older >= 4:
                    act.wait_ge(g_out[t % 4], 16 * (h * (NT // 4) + t // 4))
                act.activation(sg[:, t % 4, :], gate_ps[:, 0:RV], ACT.Silu).then_inc(silu_done, 1)

            square_x(0)
            w_upper(0, 0, 0)
            x_upper(0, 0)
            w_upper(0, 0, 1)
            x_upper(0, 1)
            w_upper(0, 0, 2)
            w_upper(0, 0, 3)
            square_x(1)
            for kt in range(4, KT):
                w_upper(0, 0, kt)
            act.wait_ge(con_in, 16 * N_CON)
            for t in range(NT):
                if t + 1 < NT:
                    x_upper(t + 1, 0)
                if t + 2 < NT:
                    square_x(t + 2)
                w_upper(1, 1, t)
                step(t, 0, t, t)
                if t + 1 < NT:
                    x_upper(t + 1, 1)
                silu(t, 0, t, t)

            def head(h, more):
                for t in range(NT):
                    if more:
                        if t == 0:
                            act.wait_ge(gate_mm, NT * h)
                        w_upper(h + 1, (h + 1) % 2, t)
                    step(h * NT + t, h, t, 4)
                    silu(h * NT + t, h, t, 4)

            with act.Fori(1, RET_HEADS - 1) as h:
                head(h, True)
            head(RET_HEADS - 1, False)
            act.wait_ge(T_mm, LAST)
            act.activation(qkT[:, 1, :, :], T_ps[:, 0:2 * P].rearrange("p (a n) -> p a n", a=2),
                           ACT.Copy).then_inc(T_copied, 1)
            for s in (LAST, LAST + 1):
                act.wait_ge(attend_mm, s - 1)
                act.wait_ge(G_done, s - 3)
                act.activation(oS[:, s % 2, :], o_ps[:, 0:RV], ACT.Copy,
                               scale=xi[:, RET_HEADS - 1:RET_HEADS]).then_inc(o_copied, 1)

        @block.gpsimd
        def _(pool):
            def rms_x(t):
                pool.wait_ge(ss_done, t + 1)
                pool.tensor_scalar(rx[:, 0, t:t + 1], ss[:, t:t + 1], 1.0 / DM, EPS, ALU.mult, ALU.add).then_inc(rms_part, 1)
                pool.wait_ge(rms_part, t + 1)
                pool.tensor_tensor(rx[:, 1, t:t + 1], rx[:, 0, t:t + 1], neghalf[:], ALU.pow).then_inc(rms_done, 1)

            def rotate(s, h, t, older):
                pool.wait_ge(qkv_copied, s + 1)
                if older >= 2:
                    pool.wait_ge(T_mm, s - 1)
                x = qkv[:, t % 2, 0:2 * RQK].rearrange("p (a u n) -> p a u n", a=2, u=2)
                r = rot[:, t % 2, :, :].rearrange("p a (u n) -> p a u n", u=2)
                tmp = rtmp[:, :, :].rearrange("p a (u n) -> p a u n", u=2)
                c = cos[:, t:t + 1, :].broadcast_to([P, 2, RQK // 2])
                n = sin[:, t:t + 1, :].broadcast_to([P, 2, RQK // 2])
                pool.tensor_tensor(r[:, :, 0, :], x[:, :, 0, :], c, ALU.mult)
                pool.tensor_tensor(r[:, :, 1, :], x[:, :, 1, :], c, ALU.mult)
                pool.tensor_tensor(tmp[:, :, 0, :], x[:, :, 1, :], n, ALU.mult)
                pool.tensor_tensor(tmp[:, :, 1, :], x[:, :, 0, :], n, ALU.mult).then_inc(rot_part, 1)
                pool.wait_ge(rot_part, 2 * s + 1)
                pool.tensor_tensor(r[:, :, 0, :], r[:, :, 0, :], tmp[:, :, 0, :], ALU.subtract)
                pool.tensor_tensor(r[:, :, 1, :], r[:, :, 1, :], tmp[:, :, 1, :], ALU.add).then_inc(rot_part, 1)
                pool.wait_ge(rot_part, 2 * s + 2)
                wait_alone(pool)
                pool.tensor_tensor(kz[:, t % 2, :], rot[:, t % 2, 1, :], zeta[:, ds(h, 1)].broadcast_to([P, RQK]),
                                   ALU.mult).then_inc(kz_done, 1)

            def deviation(s, t):
                pool.wait_ge(mv_done, s + 1)
                wait_alone(pool)
                pool.tensor_scalar(rstd[:, t % 2, 0:1], mv[:, t % 2, 1:2], EPS, None, ALU.add).then_inc(rstd_part, 1)
                pool.wait_ge(rstd_part, s + 1)
                pool.tensor_tensor(rstd[:, t % 2, 1:2], rstd[:, t % 2, 0:1], neghalf[:], ALU.pow).then_inc(rstd_done, 1)

            rms_x(0)
            rms_x(1)
            pool.wait_ge(con_in, 16 * N_CON)
            for t in range(NT):
                if t + 2 < NT:
                    rms_x(t + 2)
                rotate(t, 0, t, t)
                if t >= 2:
                    deviation(t - 2, t)
            with pool.Fori(1, RET_HEADS) as h:
                for t in range(NT):
                    rotate(h * NT + t, h, t, 2)
                    deviation(h * NT + t - 2, t)
            deviation(LAST - 2, 0)
            deviation(LAST - 1, 1)

        @block.vector
        def _(dve):
            def scale_x(t):
                dve.wait_ge(rms_done, t + 1)
                dve.tensor_scalar(xin[:, t % 2, :], xin[:, t % 2, :], rx[:, 1, t:t + 1], None, ALU.mult).then_inc(xn_done, 1)

            def x_lower(t, half):
                dve.wait_ge(xh_done, 2 * t + half + 1)
                dve.tensor_tensor(xl[:, 4 * half:4 * half + 4, t * P:(t + 1) * P],
                                  x_ps[:, :].rearrange("p (k n) -> p k n", k=4),
                                  xh[:, 4 * half:4 * half + 4, t * P:(t + 1) * P].bitcast(F32),
                                  ALU.subtract).then_inc(xl_done, 1)

            def w_lower(h, slot, kt):
                dve.wait_ge(wh_done, KT * h + kt + 1)
                dve.scalar_tensor_tensor(wl[:, ds(slot, 1), kt, :].rearrange("p a n -> p (a n)"),
                                         raw[:, kt // 2 % 2, kt % 2, :], gain[:, kt:kt + 1],
                                         wh[:, ds(slot, 1), kt, :].rearrange("p a n -> p (a n)").bitcast(F32),
                                         ALU.mult, ALU.subtract).then_inc(wl_done, 1)

            def norm_and_gate(s, h, t):
                dve.wait_ge(rstd_done, s + 1)
                dve.tensor_scalar(oS[:, t % 2, :], oS[:, t % 2, :], mv[:, t % 2, 0:1], rstd[:, t % 2, 1:2],
                                  ALU.subtract, ALU.mult).then_inc(norm_part, 1)
                dve.wait_ge(norm_part, s + 1)
                dve.wait_ge(silu_done, s + 1)
                dve.tensor_tensor(sg[:, t % 4, :], oS[:, t % 2, :], sg[:, t % 4, :], ALU.mult).then_inc(G_done, 1)

            def carry_state(s, h, t):
                dve.wait_ge(attend_mm, s + 1)
                if t == 0:
                    dve.tensor_copy(R[:, :], k_ps[:, 0:RV]).then_inc(R_done, 1)
                else:
                    dve.wait_ge(R_done, s)
                    dve.scalar_tensor_tensor(R[:, :], R[:, :], carry[:, ds(h, 1)], k_ps[:, 0:RV],
                                             ALU.mult, ALU.add).then_inc(R_done, 1)

            def moments(s, t):
                dve.wait_ge(o_copied, s + 1)
                dve.bn_stats(bn[:, :], oS[:, t % 2, :]).then_inc(bn_part, 1)
                dve.wait_ge(bn_part, s + 1)
                wait_alone(dve)
                dve.bn_aggr(mv[:, t % 2, :], bn[:, :]).then_inc(mv_done, 1)

            def decay_scores(s, h):
                dve.wait_ge(s_mm, s + 1)
                dve.tensor_tensor(sT[:, :], s_ps[:, 0:P], decay[:, ds(h, 1), :].rearrange("p a n -> p (a n)"),
                                  ALU.mult).then_inc(sT_done, 1)

            scale_x(0)
            w_lower(0, 0, 0)
            x_lower(0, 0)
            w_lower(0, 0, 1)
            x_lower(0, 1)
            w_lower(0, 0, 2)
            w_lower(0, 0, 3)
            scale_x(1)
            for kt in range(4, KT):
                w_lower(0, 0, kt)
            dve.wait_ge(con_in, 16 * N_CON)
            for t in range(NT):
                if t + 1 < NT:
                    x_lower(t + 1, 0)
                if t >= 3:
                    norm_and_gate(t - 3, 0, t - 3)
                if t >= 2:
                    carry_state(t - 2, 0, t - 2)
                    moments(t - 2, t - 2)
                if t + 1 < NT:
                    x_lower(t + 1, 1)
                if t + 2 < NT:
                    scale_x(t + 2)
                w_lower(1, 1, t)
                if t >= 1:
                    decay_scores(t - 1, 0)

            def head(h, more):
                for t in range(NT):
                    s = h * NT + t
                    h1, h2, h3 = (h if t >= n else h - 1 for n in (1, 2, 3))
                    if more:
                        w_lower(h + 1, (h + 1) % 2, t)
                    norm_and_gate(s - 3, h3, (t - 3) % NT)
                    carry_state(s - 2, h2, (t - 2) % NT)
                    moments(s - 2, (t - 2) % NT)
                    decay_scores(s - 1, h1)

            with dve.Fori(1, RET_HEADS - 1) as h:
                head(h, True)
            h = RET_HEADS - 1
            head(h, False)
            norm_and_gate(LAST - 3, h, NT - 3)
            moments(LAST - 2, NT - 2)
            carry_state(LAST - 2, h, NT - 2)
            decay_scores(LAST - 1, h)
            norm_and_gate(LAST - 2, h, NT - 2)
            moments(LAST - 1, NT - 1)
            norm_and_gate(LAST - 1, h, NT - 1)

        @block.tensor
        def _(pe):
            def transpose_x(t, half):
                if half == 0:
                    pe.wait_ge(xn_done, t + 1)
                if t or half:
                    pe.wait_ge(xl_done, 2 * t + half)
                for k in range(4):
                    last = pe.transpose(x_ps[:, k * P:(k + 1) * P],
                                        xin[:, t % 2, (4 * half + k) * P:(4 * half + k + 1) * P], ident[:])
                last.then_inc(xT_mm, 1)

            def project(out, t, slot, at, n, done, as_they_come=False):
                for kt in range(KT):
                    if as_they_come:
                        pe.wait_ge(wl_done, kt + 1)
                        if kt % 4 == 0:
                            pe.wait_ge(xl_done, kt // 4 + 1)
                    for i, (a, b) in enumerate(((xl, wh), (xh, wl), (xh, wh))):
                        last = pe.matmul(out, a[:, kt, t * P:(t + 1) * P],
                                         b[:, ds(slot, 1), kt, at:at + n].rearrange("p a n -> p (a n)"),
                                         start=(kt == 0 and i == 0), stop=(kt == KT - 1 and i == 2))
                last.then_inc(done, 1)

            def transpose_qk(s, t, older):
                pe.wait_ge(rot_part, 2 * s + 2)
                if older:
                    pe.wait_ge(T_copied, s)
                for a in range(2):
                    last = pe.transpose(T_ps[:, a * P:(a + 1) * P], rot[:, t % 2, a, :], ident[:])
                last.then_inc(T_mm, 1)

            def attend(s, t, older):
                pe.wait_ge(sT_done, s + 1)
                pe.wait_ge(kz_done, s + 1)
                if older:
                    pe.wait_ge(o_copied, s)
                    pe.wait_ge(R_done, s)
                v = qkv[:, t % 2, 2 * RQK:QKV]
                pe.matmul(o_ps[:, 0:RV], sT[:, :], v, start=True, stop=(t == 0))
                if t:
                    pe.matmul(o_ps[:, 0:RV], qkT[:, t % 2, 0, :], R[:, :], start=False, stop=True)
                pe.matmul(k_ps[:, 0:RV], kz[:, t % 2, :], v, start=True, stop=True).then_inc(attend_mm, 1)

            def scores(s, t):
                pe.wait_ge(T_copied, s + 1)
                if type(s) is not int or s > 0:
                    pe.wait_ge(sT_done, s)
                pe.matmul(s_ps[:, 0:P], qkT[:, t % 2, 1, :], qkT[:, t % 2, 0, :], start=True, stop=True).then_inc(s_mm, 1)

            def step(s, h, t, slot, older, between=lambda: None):
                if older >= 2:
                    pe.wait_ge(qkv_copied, s - 1)
                if t == 0 and older:
                    pe.wait_ge(wl_done, KT * h + KT)
                project(qkv_ps[t % 2][:, :], t, slot, 0, QKV, qkv_mm, not older)
                if older >= 1:
                    transpose_qk(s - 1, (t - 1) % NT, older >= 2)
                if older >= 2:
                    attend(s - 2, (t - 2) % NT, older >= 3)
                between()
                if older >= 1:
                    pe.wait_ge(silu_done, s)
                project(gate_ps[:, 0:RV], t, slot, QKV, RV, gate_mm)
                if older >= 1:
                    scores(s - 1, (t - 1) % NT)

            def rest_of_x(t):
                if t == 1:
                    transpose_x(t, 0)
                if t < NT:
                    transpose_x(t, 1)

            transpose_x(0, 0)
            transpose_x(0, 1)
            for t in range(NT):
                if t + 1 < NT and t:
                    transpose_x(t + 1, 0)
                if t:
                    pe.wait_ge(xl_done, 2 * t + 2)
                step(t, 0, t, 0, t, lambda: rest_of_x(t + 1))
            with pe.Fori(1, RET_HEADS) as h:
                for t in range(NT):
                    step(h * NT + t, h, t, h % 2, 3)
            transpose_qk(LAST - 1, NT - 1, True)
            attend(LAST - 2, NT - 2, True)
            scores(LAST - 1, NT - 1)
            attend(LAST - 1, NT - 1, True)
    return sems


def close_mixer(nc, tag, gated, w, gain, x, g_post, ident, neghalf, staging, arrived, ahead, x_next,
                feature_major=False, xT=None):
    with ExitStack() as ctx:
        def sb(name, shape, dt=F32):
            return ctx.enter_context(nc.sbuf_tensor(tag + name, shape, dt))

        sems = []

        def sem(name):
            sems.append(ctx.enter_context(nc.semaphore(tag + name)))
            return sems[-1]

        KW = w.shape[0] // P
        NQ = KW // 4
        n_gain = gain.shape[1] if gain is not None else 0
        wh = sb("wh", [P, KW, DM], F32R)
        wl = sb("wl", [P, KW, DM], F32R)
        raw = staging
        gin = sb("gin", [P, KW, P])
        gh = sb("gh", [P, 2, KW, P], F32R)
        gl = sb("gl", [P, 2, KW, P], F32R)
        xin = sb("xin", [P, 2, DM])
        y = sb("y", [P, 2, DM])
        ss = sb("ss", [P, 2])
        ms = sb("ms", [P, 2])
        rms = sb("rms", [P, 2])
        if xT is not None:
            xh, xl = xT
            xn = sb("xn", [P, DM])
            sx = sb("sx", [P, 2])
            mx = sb("mx", [P, 2])
            rx = sb("rx", [P, 2])
        post = sb("post", [P, DM])
        y_ps = [ctx.enter_context(nc.psum_tensor(f"{tag}y_ps{i}", [P, 2, HALF], F32)) for i in range(2)]
        T_ps = [ctx.enter_context(nc.psum_tensor(f"{tag}T_ps{i}", [P, HALF], F32)) for i in range(4)]

        con_in, g1_in = sem("con_in"), sem("g1_in")
        g0_in = [sem(f"g0_in{q}") for q in range(NQ)]
        raw_in = arrived
        x_in = [sem("x_in0"), sem("x_in1")]
        x_out = [sem("x_out0"), sem("x_out1")]
        (g_in, wh_done, wl_done, T_mm, gh_done, gl_done, y_mm, ss_done, ms_done, rms_done, scaled, y_done,
         sx_done, mx_done, rx_done, xn_done, xT_mm, xh_done, xl_done) = (sem(n) for n in (
            "g_in wh_done wl_done T_mm gh_done gl_done y_mm ss_done ms_done rms_done scaled y_done "
            "sx_done mx_done rx_done xn_done xT_mm xh_done xl_done").split())
        X_BANK = 2
        n_con = 16 * (g_post is not None)
        block = ctx.enter_context(nc.Block())

        gin1 = xin[:, :, :].rearrange("p a n -> p (a n)")[:, 0:KW * P].rearrange("p (k n) -> p k n", n=P)

        def source(t):
            return gin1 if type(t) is int and t == 1 else gin

        def wait_for_g(eng, t, q):
            if type(t) is int and t == 0:
                eng.wait_ge(g0_in[q], 16)
            elif type(t) is int and t == 1:
                eng.wait_ge(g1_in, 16)
            else:
                eng.wait_ge(g_in, 16 * (t - 1))

        @block.sync
        def _(sp):
            out_of_gin = gl_done if feature_major else T_mm

            def g_tile(t):
                return (gated[:, ds(t * P, P)].rearrange("(k p) n -> p k n", p=P) if feature_major else
                        gated[ds(t * P, P), :].rearrange("p (k n) -> p k n", n=P))

            def load_g(t, through):
                sp.wait_ge(out_of_gin, through * NQ)
                sp.dma_start(gin[:, :, :], g_tile(t)).then_inc(g_in, 16)

            def load_x(t, slot, first):
                if not first:
                    sp.wait_ge(y_done, t - 1)
                sp.dma_start(xin[:, slot, :], x[ds(t * P, P), :]).then_inc(x_in[slot], 16)

            def store(t, slot):
                sp.wait_ge(y_done, t + 1)
                sp.dma_start(x_next[ds(t * P, P), :], y[:, slot, :]).then_inc(x_out[slot], 16)

            def load_w(kt):
                sp.wait_ge(wl_done, kt - 1)
                sp.dma_start(raw[:, kt % 2, :], w[kt * P:(kt + 1) * P, :]).then_inc(raw_in[kt % 2], 16)

            for q in range(NQ):
                sp.dma_start(gin[:, 4 * q:4 * q + 4, :], g_tile(0)[:, 4 * q:4 * q + 4, :]).then_inc(g0_in[q], 16)
            sp.dma_start(gin1, g_tile(1)).then_inc(g1_in, 16)
            for kt in range(2, KW):
                load_w(kt)
                if kt == 3:
                    load_g(2, 1)
            sp.wait_ge(out_of_gin, 2 * NQ)
            if g_post is not None:
                sp.dma_start(post[:], g_post.partition_broadcast(P)).then_inc(con_in, 16)
            load_x(0, 0, True)
            load_x(1, 1, True)
            with sp.Fori(1, NT // 2 - 1) as pair:
                for u in range(2):
                    t = 2 * pair + u
                    store(t - 2, u)
                    load_x(t, u, False)
                    load_g(t + 1, t + 1)
            sp.wait_ge(wl_done, KW)
            for slot in range(2):
                sp.wait_ge(x_out[slot], 32)
            ahead(sp)
            for t in (NT - 2, NT - 1):
                store(t - 2, t % 2)
                load_x(t, t % 2, False)
                if t + 1 < NT:
                    load_g(t + 1, t + 1)
            for t in (NT - 2, NT - 1):
                store(t, t % 2)
            for slot in range(2):
                sp.wait_ge(x_out[slot], 16 * NT // 2)

        @block.scalar
        def _(act):
            def w_upper(kt):
                act.wait_ge(raw_in[kt % 2], 16 * (kt // 2 + 1))
                scale = gain[:, kt % n_gain:kt % n_gain + 1] if n_gain else 1.0
                act.activation(wh[:, kt, :], raw[:, kt % 2, :], ACT.Copy, scale=scale).then_inc(wh_done, 1)

            def g_upper(t, slot, q, early):
                if feature_major:
                    wait_for_g(act, t, q)
                    src = source(t)[:, 4 * q:4 * q + 4, :]
                else:
                    act.wait_ge(T_mm, t * NQ + q + 1)
                    src = T_ps[q][:, :].rearrange("p (k n) -> p k n", k=4)
                if not early and q == 0:
                    act.wait_ge(y_mm, t - 1)
                act.activation(gh[:, slot, 4 * q:4 * q + 4, :], src, ACT.Copy).then_inc(gh_done, 1)

            def square_y(t, slot, stored):
                act.wait_ge(y_mm, t + 1)
                if type(stored) is not int or stored:
                    act.wait_ge(x_out[slot], 16 * stored)
                act.activation(y[:, slot, :], y_ps[slot][:, :, :].rearrange("p a n -> p (a n)"), ACT.Square,
                               accum_out=ss[:, slot:slot + 1]).then_inc(ss_done, 1)

            def square_x(t, slot):
                act.wait_ge(y_done, t + 1)
                wait_alone(act)
                act.activation(xl[:, :, ds(t * P, P)], y[:, slot, :].rearrange("p (k n) -> p k n", k=KT), ACT.Square,
                               accum_out=sx[:, slot:slot + 1]).then_inc(sx_done, 1)

            def x_upper(t, half):
                act.wait_ge(xT_mm, 2 * t + half + 1)
                wait_alone(act)
                act.activation(xh[:, 4 * half:4 * half + 4, ds(t * P, P)],
                               T_ps[X_BANK + half][:, :].rearrange("p (k n) -> p k n", k=4), ACT.Copy).then_inc(xh_done, 1)

            def round_of(t, slot, stored, old):
                if g_post is not None:
                    square_y(t - 2, slot, stored)
                if xT is None:
                    for q in range(NQ):
                        g_upper(t, slot, q, False)
                    return
                if old:
                    x_upper(t - 3, 0)
                g_upper(t, slot, 0, False)
                square_x(t - 2, slot)
                if old:
                    x_upper(t - 3, 1)
                g_upper(t, slot, 1, False)

            for q in range(NQ):
                g_upper(0, 0, q, True)
            w_upper(0)
            w_upper(1)
            for q in range(NQ):
                g_upper(1, 1, q, True)
            for kt in range(2, KW):
                w_upper(kt)
            round_of(2, 0, 0, False)
            round_of(3, 1, 0, True)
            with act.Fori(2, NT // 2) as pair:
                for u in range(2):
                    round_of(2 * pair + u, u, pair - 1, True)
            for t in (NT, NT + 1):
                if g_post is not None:
                    square_y(t - 2, t % 2, t // 2 - 1)
                if xT is not None:
                    x_upper(t - 3, 0)
                    x_upper(t - 3, 1)
                    square_x(t - 2, t % 2)
            if xT is not None:
                x_upper(NT - 1, 0)
                x_upper(NT - 1, 1)

        @block.gpsimd
        def _(pool):
            def one_over_rms(t, u, sums, mean, root, sums_done, mean_done, root_done):
                pool.wait_ge(sums_done, t + 1)
                wait_alone(pool)
                pool.tensor_scalar(mean[:, u:u + 1], sums[:, u:u + 1], 1.0 / DM, EPS, ALU.mult, ALU.add).then_inc(mean_done, 1)
                pool.wait_ge(mean_done, t + 1)
                pool.tensor_tensor(root[:, u:u + 1], mean[:, u:u + 1], neghalf[:], ALU.pow).then_inc(root_done, 1)

            with pool.Fori(0, NT // 2) as pair:
                for u in range(2):
                    if g_post is not None:
                        one_over_rms(2 * pair + u, u, ss, ms, rms, ss_done, ms_done, rms_done)
                    if xT is not None:
                        one_over_rms(2 * pair + u, u, sx, mx, rx, sx_done, mx_done, rx_done)

        @block.vector
        def _(dve):
            def w_lower(kt):
                dve.wait_ge(wh_done, kt + 1)
                if n_gain:
                    dve.scalar_tensor_tensor(wl[:, kt, :], raw[:, kt % 2, :], gain[:, kt % n_gain:kt % n_gain + 1],
                                             wh[:, kt, :].bitcast(F32), ALU.mult, ALU.subtract).then_inc(wl_done, 1)
                else:
                    dve.tensor_tensor(wl[:, kt, :], raw[:, kt % 2, :], wh[:, kt, :].bitcast(F32),
                                      ALU.subtract).then_inc(wl_done, 1)

            def g_lower(t, slot, q):
                dve.wait_ge(gh_done, t * NQ + q + 1)
                src = source(t)[:, 4 * q:4 * q + 4, :] if feature_major else T_ps[q][:, :].rearrange("p (k n) -> p k n", k=4)
                dve.tensor_tensor(gl[:, slot, 4 * q:4 * q + 4, :], src, gh[:, slot, 4 * q:4 * q + 4, :].bitcast(F32),
                                  ALU.subtract).then_inc(gl_done, 1)

            def finish(t, slot, stored):
                ys = y_ps[slot][:, :, :].rearrange("p a n -> p (a n)")
                dve.wait_ge(x_in[slot], 16 * stored + 16)
                if g_post is None:
                    dve.wait_ge(y_mm, t + 1)
                    if type(stored) is not int or stored:
                        dve.wait_ge(x_out[slot], 16 * stored)
                    dve.tensor_tensor(y[:, slot, :], ys, xin[:, slot, :], ALU.add).then_inc(y_done, 1)
                else:
                    dve.wait_ge(rms_done, t + 1)
                    dve.scalar_tensor_tensor(y[:, slot, :], ys, rms[:, slot:slot + 1], post[:], ALU.mult, ALU.mult).then_inc(scaled, 1)
                    dve.wait_ge(scaled, t + 1)
                    dve.tensor_tensor(y[:, slot, :], y[:, slot, :], xin[:, slot, :], ALU.add).then_inc(y_done, 1)

            def scale_x(t, slot, old):
                dve.wait_ge(rx_done, t + 1)
                if old:
                    dve.wait_ge(xT_mm, 2 * t)
                dve.tensor_scalar(xn[:, :], y[:, slot, :], rx[:, slot:slot + 1], None, ALU.mult).then_inc(xn_done, 1)

            def x_lower(t, half):
                dve.wait_ge(xh_done, 2 * t + half + 1)
                wait_alone(dve)
                dve.tensor_tensor(xl[:, 4 * half:4 * half + 4, ds(t * P, P)],
                                  T_ps[X_BANK + half][:, :].rearrange("p (k n) -> p k n", k=4),
                                  xh[:, 4 * half:4 * half + 4, ds(t * P, P)].bitcast(F32),
                                  ALU.subtract).then_inc(xl_done, 1)

            def round_of(t, slot, stored, old):
                finish(t - 2, slot, stored)
                if xT is None:
                    for q in range(NQ):
                        g_lower(t, slot, q)
                    return
                if old:
                    x_lower(t - 3, 0)
                g_lower(t, slot, 0)
                if old:
                    x_lower(t - 3, 1)
                scale_x(t - 2, slot, old)
                g_lower(t, slot, 1)

            for q in range(NQ):
                g_lower(0, 0, q)
            w_lower(0)
            w_lower(1)
            for q in range(NQ):
                g_lower(1, 1, q)
            for kt in range(2, KW):
                w_lower(kt)
            if n_con:
                dve.wait_ge(con_in, n_con)
            round_of(2, 0, 0, False)
            round_of(3, 1, 0, True)
            with dve.Fori(2, NT // 2) as pair:
                for u in range(2):
                    round_of(2 * pair + u, u, pair - 1, True)
            for t in (NT, NT + 1):
                finish(t - 2, t % 2, t // 2 - 1)
                if xT is not None:
                    x_lower(t - 3, 0)
                    x_lower(t - 3, 1)
                    scale_x(t - 2, t % 2, True)
            if xT is not None:
                x_lower(NT - 1, 0)
                x_lower(NT - 1, 1)

        @block.tensor
        def _(pe):
            def transpose_g(t, q, early):
                if feature_major:
                    return
                if q == 0 or early:
                    wait_for_g(pe, t, q)
                if not early:
                    pe.wait_ge(gl_done, (t - 1) * NQ + q + 1)
                for k in range(4):
                    last = pe.transpose(T_ps[q][:, k * P:(k + 1) * P], source(t)[:, 4 * q + k, :], ident[:])
                last.then_inc(T_mm, 1)

            def multiply(slot, kt):
                for c in range(2):
                    for i, (a, b) in enumerate(((gl, wh), (gh, wl), (gh, wh))):
                        last = pe.matmul(y_ps[slot][:, c, :], a[:, slot, kt, :], b[:, kt, c * HALF:(c + 1) * HALF],
                                         start=(kt == 0 and i == 0), stop=(kt == KW - 1 and i == 2))
                return last

            for t in range(2):
                for q in range(NQ):
                    transpose_g(t, q, t == 0)
            for kt in range(KW):
                for t in range(2):
                    if kt % 4 == 0:
                        pe.wait_ge(gl_done, t * NQ + kt // 4 + 1)
                    if t == 0:
                        pe.wait_ge(wl_done, kt + 1)
                    last = multiply(t, kt)
                    if kt == KW - 1:
                        last.then_inc(y_mm, 1)
            for q in range(NQ):
                transpose_g(2, q, False)

            def transpose_x(t, half, old):
                if half == 0:
                    pe.wait_ge(xn_done, t + 1)
                if old:
                    pe.wait_ge(xl_done, 2 * t + half - 1)
                for k in range(4):
                    last = pe.transpose(T_ps[X_BANK + half][:, k * P:(k + 1) * P],
                                        xn[:, (4 * half + k) * P:(4 * half + k + 1) * P], ident[:])
                last.then_inc(xT_mm, 1)

            def tile(t, slot, more, old=True):
                pe.wait_ge(y_done, t - 1)
                for kt in range(KW):
                    if kt % 4 == 0:
                        pe.wait_ge(gl_done, t * NQ + kt // 4 + 1)
                    last = multiply(slot, kt)
                    if xT is not None and kt in (2, 5):
                        transpose_x(t - 2, kt // 5, old)
                    if kt % 4 == 3 and more:
                        transpose_g(t + 1, kt // 4, False)
                last.then_inc(y_mm, 1)

            tile(2, 0, True, False)
            tile(3, 1, True)
            with pe.Fori(2, NT // 2 - 1) as pair:
                for u in range(2):
                    tile(2 * pair + u, u, True)
            tile(NT - 2, 0, True)
            tile(NT - 1, 1, False)
            if xT is not None:
                for t in (NT - 2, NT - 1):
                    for half in range(2):
                        transpose_x(t, half, True)
    return sems


def latents(nc, x, g_kv, g_pre, w_lat, w_gate, g_lat, w_next, con, ident, neghalf, kv, cq, spare, staging, arrived,
            silu_gate):
    kvh, kvl = kv
    cqh, cql = cq
    with ExitStack() as ctx:
        def sb(name, shape, dt=F32):
            return ctx.enter_context(nc.sbuf_tensor("la_" + name, shape, dt))

        def bank(name):
            return ctx.enter_context(nc.psum_tensor("la_" + name, [P, HALF], F32))

        sems = []

        def sem(name):
            sems.append(ctx.enter_context(nc.semaphore("la_" + name)))
            return sems[-1]

        KVW = KV_LORA + MROPE
        WL = KVW + Q_LORA
        xh = sb("xh", [P, KT, SEQ], F32R)
        xl = sb("xl", [P, KT, SEQ], F32R)
        wh = sb("wh", [P, KT, WL], F32R)
        wl = sb("wl", [P, KT, WL], F32R)
        gh, gl = spare
        raw = sb("raw", [P, 2, WL])
        xin = staging
        lat = sb("lat", [P, KV_LORA + Q_LORA])
        cos = sb("cos", [P, NT, MROPE // 2])
        sin = sb("sin", [P, NT, MROPE // 2])
        kr = sb("kr", [P, MROPE])
        krot = sb("krot", [P, 2, MROPE])
        ktmp = sb("ktmp", [P, MROPE])
        ss = sb("ss", [P, NT])
        ls = sb("ls", [P, 2, 2])
        kv_ps = [bank("kv_ps0"), bank("kv_ps1")]
        cq_ps = [bank("cq_ps0"), bank("cq_ps1")]
        T_ps = [bank("T_ps0"), bank("T_ps1")]
        x_ps = [bank("x_ps0"), bank("x_ps1")]

        key_in = sem("key_in")
        x_in = arrived
        raw_in = [sem("raw_in0"), sem("raw_in1")]
        g_out = [sem("g_out0"), sem("g_out1")]
        (ss_done, ms_done, rms_done, xn_done, xT_mm, xh_done, xl_done, wh_done, wl_done, lat_mm, ls_done, lm_done,
         lr_done, kr_done, kr_part, krot_done, lat_done, T_mm, Th_done, Tl_done, gate_mm, silu_done) = (
            sem(n) for n in ("ss_done ms_done rms_done xn_done xT_mm xh_done xl_done wh_done wl_done lat_mm ls_done "
                             "lm_done lr_done kr_done kr_part krot_done lat_done T_mm Th_done Tl_done gate_mm "
                             "silu_done").split())
        block = ctx.enter_context(nc.Block())
        NEXT = w_next.shape[1]
        GROUPS = 16

        @block.sync
        def _(sp):
            def load_x(t):
                sp.wait_ge(xT_mm, 2 * (t - 1))
                sp.dma_start(xin[:, t % 2, :], x[t * P:(t + 1) * P, :]).then_inc(x_in[t % 2], 16)

            def load_piece(n):
                if n >= 2:
                    sp.wait_ge(wl_done, n - 1)
                if n < KT:
                    sp.dma_start(raw[:, n % 2, 0:WL], w_lat[:, n, :]).then_inc(raw_in[n % 2], 16)
                elif n >= 3 * KT:
                    sp.dma_start(raw[:, n % 2, 0:HALF], w_next[:, n - 3 * KT, :]).then_inc(raw_in[n % 2], 16)
                else:
                    sp.dma_start(raw[:, n % 2, 0:HALF], w_gate[n // KT - 1, :, n % KT, :]).then_inc(raw_in[n % 2], 16)

            load_piece(0)
            load_piece(1)
            sp.dma_start(cos[:], con["cos_mla"]).then_inc(key_in, 16)
            sp.dma_start(sin[:], con["sin_mla"]).then_inc(key_in, 16)
            for n in range(2, KT):
                load_piece(n)
                if n == 3:
                    load_x(2)
            for t in range(NT):
                load_piece(KT + t)
                if 3 <= t + 2 < NT:
                    load_x(t + 2)
            load_piece(2 * KT)
            load_piece(2 * KT + 1)
            for j in range(GROUPS):
                if j + 2 < KT + NEXT:
                    load_piece(2 * KT + 2 + j)
                sp.wait_ge(silu_done, j + 1)
                f, half = divmod(j, 2)
                sp.dma_start(silu_gate[f * P:(f + 1) * P, half * HALF:(half + 1) * HALF], xin[:, j % 2, 0:HALF])\
                  .then_inc(g_out[j % 2], 16)
            for slot in range(2):
                sp.wait_ge(g_out[slot], 16 * GROUPS // 2)

        def piece_parts(n):
            if n < KT:
                return [(g_kv[:, n:n + 1], (0, KVW), wh[:, n, 0:KVW], wl[:, n, 0:KVW]),
                        (g_pre[:, n:n + 1], (KVW, WL), wh[:, n, KVW:WL], wl[:, n, KVW:WL])]
            if n >= 3 * KT:
                u = n - 3 * KT
                g = u // 2 if u < 4 else u - 2
                return [(g_lat[:, g:g + 1], (0, HALF), gh[:, u, :], gl[:, u, :])]
            h, l = ((gh, gl), (wh, wl))[n // KT - 1]
            return [(g_pre[:, n % KT:n % KT + 1], (0, HALF), h[:, n % KT, 0:HALF], l[:, n % KT, 0:HALF])]

        @block.scalar
        def _(act):
            def square_x(t):
                act.wait_ge(x_in[t % 2], 16 * (t // 2 + 1))
                act.activation(xl[:, :, t * P:(t + 1) * P], xin[:, t % 2, :].rearrange("p (k n) -> p k n", k=KT),
                               ACT.Square, accum_out=ss[:, t:t + 1]).then_inc(ss_done, 1)

            def x_upper(t, half):
                act.wait_ge(xT_mm, 2 * t + half + 1)
                act.activation(xh[:, 4 * half:4 * half + 4, t * P:(t + 1) * P],
                               x_ps[half][:, :].rearrange("p (k n) -> p k n", k=4), ACT.Copy).then_inc(xh_done, 1)

            def w_upper(n):
                act.wait_ge(raw_in[n % 2], 16 * (n // 2 + 1))
                if n == 2 * KT:
                    act.wait_ge(lat_mm, NT)
                for gain, (a, b), h, _ in piece_parts(n):
                    last = act.activation(h, raw[:, n % 2, a:b], ACT.Copy, scale=gain)
                last.then_inc(wh_done, 1)

            def latent(t):
                act.wait_ge(lat_mm, t + 1)
                if t:
                    act.wait_ge(T_mm, 2 * t)
                    act.wait_ge(kr_part, 2 * t)
                act.activation(lat[:, 0:KV_LORA], kv_ps[t % 2][:, 0:KV_LORA], ACT.Square, accum_out=ls[:, t % 2, 0:1])
                act.activation(lat[:, KV_LORA:KV_LORA + Q_LORA], cq_ps[t % 2][:, 0:Q_LORA], ACT.Square, accum_out=ls[:, t % 2, 1:2]).then_inc(ls_done, 1)
                act.activation(kr[:, :], kv_ps[t % 2][:, KV_LORA:KVW], ACT.Copy).then_inc(kr_done, 1)

            def latent_upper(t):
                for i, dst in ((0, kvh), (1, cqh)):
                    act.wait_ge(T_mm, 2 * t + i + 1)
                    act.activation(dst[:, :, t * P:(t + 1) * P], T_ps[i][:, 0:3 * P].rearrange("p (k n) -> p k n", k=3),
                                   ACT.Copy).then_inc(Th_done, 1)

            for t in range(2):
                square_x(t)
                w_upper(2 * t)
                w_upper(2 * t + 1)
                for half in range(2):
                    x_upper(t, half)
            for n in range(4, KT):
                w_upper(n)
            for t in range(NT):
                if t + 2 < NT:
                    square_x(t + 2)
                w_upper(KT + t)
                latent(t)
                if t + 2 < NT:
                    for half in range(2):
                        x_upper(t + 2, half)
                if t:
                    latent_upper(t - 1)
            latent_upper(NT - 1)
            for j in range(GROUPS):
                if j < KT + NEXT:
                    w_upper(2 * KT + j)
                act.wait_ge(gate_mm, j + 1)
                if j >= 2:
                    act.wait_ge(g_out[j % 2], 16 * (j // 2))
                act.activation(xin[:, j % 2, 0:HALF], x_ps[j % 2][:, :], ACT.Silu).then_inc(silu_done, 1)

        @block.gpsimd
        def _(pool):
            def rms_x(t):
                pool.wait_ge(ss_done, t + 1)
                pool.tensor_scalar(ss[:, t:t + 1], ss[:, t:t + 1], 1.0 / DM, EPS, ALU.mult, ALU.add).then_inc(ms_done, 1)
                pool.wait_ge(ms_done, t + 1)
                pool.tensor_tensor(ss[:, t:t + 1], ss[:, t:t + 1], neghalf[:], ALU.pow).then_inc(rms_done, 1)

            def rms_latent(t):
                pool.wait_ge(ls_done, t + 1)
                pool.tensor_scalar(ls[:, t % 2, 0:1], ls[:, t % 2, 0:1], 1.0 / KV_LORA, EPS, ALU.mult, ALU.add)
                pool.tensor_scalar(ls[:, t % 2, 1:2], ls[:, t % 2, 1:2], 1.0 / Q_LORA, EPS, ALU.mult, ALU.add).then_inc(lm_done, 1)
                pool.wait_ge(lm_done, t + 1)
                pool.tensor_tensor(ls[:, t % 2, :], ls[:, t % 2, :], neghalf[:].broadcast_to([P, 2]), ALU.pow).then_inc(lr_done, 1)

            def rotate_key(t):
                H = MROPE // 2
                pool.wait_ge(kr_done, t + 1)
                if t:
                    pool.wait_ge(T_mm, 2 * t)
                c, s = cos[:, t, :], sin[:, t, :]
                pool.tensor_tensor(krot[:, 0, 0:H], kr[:, 0:H], c, ALU.mult)
                pool.tensor_tensor(krot[:, 0, H:], kr[:, H:], c, ALU.mult)
                pool.tensor_tensor(ktmp[:, 0:H], kr[:, H:], s, ALU.mult)
                pool.tensor_tensor(ktmp[:, H:], kr[:, 0:H], s, ALU.mult).then_inc(kr_part, 1)
                pool.wait_ge(kr_part, 2 * t + 1)
                pool.tensor_tensor(krot[:, 0, 0:H], krot[:, 0, 0:H], ktmp[:, 0:H], ALU.subtract)
                pool.tensor_tensor(krot[:, 0, H:], krot[:, 0, H:], ktmp[:, H:], ALU.add).then_inc(kr_part, 1)
                pool.wait_ge(kr_part, 2 * t + 2)
                pool.tensor_copy(krot[:, 1, :], krot[:, 0, :]).then_inc(krot_done, 1)

            rms_x(0)
            rms_x(1)
            pool.wait_ge(key_in, 32)
            for t in range(NT):
                if t + 2 < NT:
                    rms_x(t + 2)
                rms_latent(t)
                rotate_key(t)

        @block.vector
        def _(dve):
            def scale_x(t):
                dve.wait_ge(rms_done, t + 1)
                dve.tensor_scalar(xin[:, t % 2, :], xin[:, t % 2, :], ss[:, t:t + 1], None, ALU.mult).then_inc(xn_done, 1)

            def x_lower(t, half):
                dve.wait_ge(xh_done, 2 * t + half + 1)
                dve.tensor_tensor(xl[:, 4 * half:4 * half + 4, t * P:(t + 1) * P],
                                  x_ps[half][:, :].rearrange("p (k n) -> p k n", k=4),
                                  xh[:, 4 * half:4 * half + 4, t * P:(t + 1) * P].bitcast(F32),
                                  ALU.subtract).then_inc(xl_done, 1)

            def w_lower(n):
                dve.wait_ge(wh_done, n + 1)
                for gain, (a, b), h, l in piece_parts(n):
                    last = dve.scalar_tensor_tensor(l, raw[:, n % 2, a:b], gain, h.bitcast(F32),
                                                    ALU.mult, ALU.subtract)
                last.then_inc(wl_done, 1)

            def norm_latents(t):
                dve.wait_ge(lr_done, t + 1)
                dve.wait_ge(kr_done, t + 1)
                dve.tensor_scalar(lat[:, 0:KV_LORA], kv_ps[t % 2][:, 0:KV_LORA], ls[:, t % 2, 0:1], None, ALU.mult)
                dve.tensor_scalar(lat[:, KV_LORA:KV_LORA + Q_LORA], cq_ps[t % 2][:, 0:Q_LORA], ls[:, t % 2, 1:2], None, ALU.mult)\
                   .then_inc(lat_done, 1)

            def latent_lower(t):
                for i, h, l in ((0, kvh, kvl), (1, cqh, cql)):
                    dve.wait_ge(Th_done, 2 * t + i + 1)
                    dve.tensor_tensor(l[:, :, t * P:(t + 1) * P], T_ps[i][:, 0:3 * P].rearrange("p (k n) -> p k n", k=3),
                                      h[:, :, t * P:(t + 1) * P].bitcast(F32), ALU.subtract).then_inc(Tl_done, 1)

            for t in range(2):
                scale_x(t)
                w_lower(2 * t)
                w_lower(2 * t + 1)
                for half in range(2):
                    x_lower(t, half)
            for n in range(4, KT):
                w_lower(n)
            for t in range(NT):
                if t + 2 < NT:
                    scale_x(t + 2)
                w_lower(KT + t)
                norm_latents(t)
                if t + 2 < NT:
                    for half in range(2):
                        x_lower(t + 2, half)
                if t:
                    latent_lower(t - 1)
            latent_lower(NT - 1)
            for j in range(KT + NEXT):
                w_lower(2 * KT + j)

        @block.tensor
        def _(pe):
            def transpose_x(t):
                pe.wait_ge(xn_done, t + 1)
                for half in range(2):
                    if t:
                        pe.wait_ge(xl_done, 2 * t + half - 1)
                    for k in range(4):
                        last = pe.transpose(x_ps[half][:, k * P:(k + 1) * P],
                                            xin[:, t % 2, (4 * half + k) * P:(4 * half + k + 1) * P], ident[:])
                    last.then_inc(xT_mm, 1)

            def project(t):
                pe.wait_ge(xl_done, 2 * t + 2)
                if t >= 2:
                    pe.wait_ge(lat_done, t - 1)
                for kt in range(KT):
                    if t == 0:
                        pe.wait_ge(wl_done, kt + 1)
                    for out, a, b in ((kv_ps[t % 2][:, 0:KVW], 0, KVW), (cq_ps[t % 2][:, 0:Q_LORA], KVW, WL)):
                        for i, (xx, ww) in enumerate(((xl, wh), (xh, wl), (xh, wh))):
                            last = pe.matmul(out, xx[:, kt, t * P:(t + 1) * P], ww[:, kt, a:b],
                                             start=(kt == 0 and i == 0), stop=(kt == KT - 1 and i == 2))
                last.then_inc(lat_mm, 1)

            def transpose_latents(t):
                pe.wait_ge(lat_done, t + 1)
                pe.wait_ge(krot_done, t + 1)
                if t:
                    pe.wait_ge(Tl_done, 2 * t)
                for k in range(2):
                    pe.transpose(T_ps[0][:, k * P:(k + 1) * P], lat[:, k * P:(k + 1) * P], ident[:])
                pe.transpose(T_ps[0][:, 2 * P:3 * P], krot[:, :, :].rearrange("p a n -> p (a n)"), ident[:]).then_inc(T_mm, 1)
                for k in range(3):
                    last = pe.transpose(T_ps[1][:, k * P:(k + 1) * P], lat[:, (2 + k) * P:(3 + k) * P], ident[:])
                last.then_inc(T_mm, 1)

            transpose_x(0)
            transpose_x(1)
            for t in range(NT):
                project(t)
                if t + 2 < NT:
                    transpose_x(t + 2)
                if t:
                    transpose_latents(t - 1)
            for j in range(GROUPS):
                f, half = divmod(j, 2)
                h, l = ((gh, gl), (wh, wl))[f // 4]
                if j % 8 == 0:
                    pe.wait_ge(wl_done, KT + KT * (f // 4) + KT)
                if j >= 2:
                    pe.wait_ge(silu_done, j - 1)
                for kt in range(KT):
                    for i, (a, b) in enumerate(((l, xh), (h, xl), (h, xh))):
                        last = pe.matmul(x_ps[j % 2][:, :], a[:, kt, f % 4 * P:(f % 4 + 1) * P],
                                         b[:, kt, half * HALF:(half + 1) * HALF],
                                         start=(kt == 0 and i == 0), stop=(kt == KT - 1 and i == 2))
                last.then_inc(gate_mm, 1)
                if j == 0:
                    transpose_latents(NT - 1)
    return sems


def attention(nc, kv, cq, spare, gains, w_head, silu_gate, con, ident, staging, ahead, gated):
    kvh, kvl = kv
    cqh, cql = cq
    SCALE = (NOPE + MROPE) ** -0.5
    FAR = -1e30
    H = MLA_HEADS
    with ExitStack() as ctx:
        def sb(name, shape, dt=F32):
            return ctx.enter_context(nc.sbuf_tensor("at_" + name, shape, dt))

        sems = []

        def sem(name):
            sems.append(ctx.enter_context(nc.semaphore("at_" + name)))
            return sems[-1]

        raw = sb("raw", [P, 5, P])
        wh = sb("wh", [P, 5, P], F32R)
        wl = sb("wl", [P, 5, P], F32R)
        qh = sb("qh", [P, 2, SEQ], F32R)
        ql = sb("ql", [P, 2, SEQ], F32R)
        kh = sb("kh", [P, 2, SEQ], F32R)
        kl = sb("kl", [P, 2, SEQ], F32R)
        rh = sb("rh", [P, SEQ], F32R)
        rl = sb("rl", [P, SEQ], F32R)
        v = sb("v", [P, NT, DM])
        qrT = sb("qrT", [P, MLA_HEADS // 2, SEQ])
        cos = sb("cos", [P, NT, MROPE // 2])
        sin = sb("sin", [P, NT, MROPE // 2])
        RW = MLA_HEADS * MROPE
        qr, rot = (staging[:, i, :].rearrange("p (a n) -> p a n", a=2) for i in range(2))
        tmp = sb("tmp", [P, RW])
        pth, ptl = (w[:, 0:4, :].rearrange("p a (b n) -> p (a b) n", b=2) for w in spare)
        vh, vl = (w[:, 4:8, :].rearrange("p (u a) (b n) -> p u (a b) n", u=2, n=P) for w in spare)
        prob = sb("prob", [P, 2, SEQ])
        sg = sb("sg", [P, 2, SEQ])
        early = sb("early", [1, P], BF16)
        late = sb("late", [1, P // 2], BF16)
        nmax = sb("nmax", [P, 2])
        rsum = sb("rsum", [P, 2])
        rinv = sb("rinv", [P, 2])
        s_ps = [ctx.enter_context(nc.psum_tensor(f"at_s_ps{i}", [P, 2, HALF], F32)) for i in range(2)]
        T_ps = [ctx.enter_context(nc.psum_tensor(f"at_T_ps{i}", [P, HALF], F32)) for i in range(2)]
        j_ps = ctx.enter_context(nc.psum_tensor("at_j_ps", [P, HALF], F32))
        v_ps = ctx.enter_context(nc.psum_tensor("at_v_ps", [P, HALF], F32))
        rope_in, w_in = sem("rope_in"), sem("w_in")
        sg_in = [sem("sg_in0"), sem("sg_in1")]
        g_out = [sem("g_out0"), sem("g_out1")]
        (all_v_mm, v_copied, r_mm, qr_done, rot_part, qrT_mm, qrT_copied) = (
            sem(n) for n in "all_v_mm v_copied r_mm qr_done rot_part qrT_mm qrT_copied".split())
        (mask_done, wh_done, wl_done, vh_done, vl_done, rh_done, rl_done, j_mm, jh_done, jl_done, s_mm, max_done,
         exp_done, inv_done, prob_done, T_mm, Th_done, Tl_done, v_mm, g_done) = (
            sem(n) for n in ("mask_done wh_done wl_done vh_done vl_done rh_done rl_done j_mm jh_done jl_done s_mm max_done "
                             "exp_done inv_done prob_done T_mm Th_done Tl_done v_mm g_done").split())
        block = ctx.enter_context(nc.Block())

        TG = 12

        def groups(i):
            if i < 4:
                return [(i, 0, i + 1)]
            return [(4 + 2 * (i - 4), 0, 4), (5 + 2 * (i - 4), 4, i - 3)]

        def last_group(h, i):
            return TG * h + groups(i)[-1][0]

        def before(h, i, n):
            return (h, i - n) if i >= n else (h - 1, i - n + NT)

        def projection(g):
            return ((2, 3, 4), (0, 1))[g // 2], ((cqh, cql), (kvh, kvl))[g // 2], g % 2

        def project_bank(g, first):
            return v_ps if first and g % 2 else j_ps

        def heads(eng, head):
            head(0, 0, True, 2)
            with eng.Fori(0, (H - 4) // 2) as pair:
                head(2 * pair + 1, 1, False, 2)
                head(2 * pair + 2, 0, False, 2)
            head(H - 3, 1, False, 2)
            head(H - 2, 0, False, 1)
            head(H - 1, 1, False, 0)

        @block.sync
        def _(sp):
            def load_gate(h, slot):
                sp.dma_start(sg[:, slot, :], silu_gate[ds(h * P, P), :]).then_inc(sg_in[slot], 16)

            def store(h, slot):
                sp.wait_ge(g_done, 4 * h + 4)
                sp.dma_start(gated[ds(h * P, P), :], sg[:, slot, :]).then_inc(g_out[slot], 16)

            def load_weights(h):
                sp.wait_ge(wl_done, h)
                sp.dma_start(raw[:], w_head[ds(h, 1), :, :, :].rearrange("a p k n -> p (a k) n")).then_inc(w_in, 16)

            def head(h, u, first, behind):
                if behind > 1:
                    load_weights(h + 2)
                if not first:
                    store(h - 1, 1 - u)
                    if behind:
                        sp.wait_ge(g_out[1 - u], 8 * (h + 1 - (1 - u)))
                if behind:
                    load_gate(h + 1, 1 - u)

            sp.dma_start(cos[:], con["cos_mla"]).then_inc(rope_in, 16)
            sp.dma_start(sin[:], con["sin_mla"]).then_inc(rope_in, 16)
            sp.dma_start(raw[:], w_head[0, :, :, :]).then_inc(w_in, 16)
            load_gate(0, 0)
            load_weights(1)
            heads(sp, head)
            sp.wait_ge(qrT_mm, NT)
            ahead(sp)
            store(H - 1, 1)
            for slot in range(2):
                sp.wait_ge(g_out[slot], 16 * H // 2)

        @block.scalar
        def _(act):
            def w_upper(h, first=False):
                act.wait_ge(w_in, 16 * h + 16)
                if not first:
                    act.wait_ge(j_mm, 4 * h)
                for k in range(5):
                    last = act.activation(wh[:, k, :], raw[:, k, :], ACT.Copy, scale=gains[:, k:k + 1])
                last.then_inc(wh_done, 1)

            def v_upper(h, slot):
                wait_alone(act)
                act.activation(vh[:, slot, :, :], v[:, :, ds(h * MV, MV)], ACT.Copy).then_inc(vh_done, 1)

            def r_upper(h, u):
                rows = slice(u * MROPE, (u + 1) * MROPE)
                wait_alone(act)
                act.activation(rh[rows, :], qrT[rows, ds(h // 2, 1), :].rearrange("p a n -> p (a n)"), ACT.Copy).then_inc(rh_done, 1)

            def project_upper(h, u, g, first=False):
                act.wait_ge(j_mm, 4 * h + g + 1)
                dst, scale = ((qh, SCALE), (kh, 1.0))[g // 2]
                act.activation(dst[:, u, g % 2 * HALF:(g % 2 + 1) * HALF], project_bank(g, first)[:, :], ACT.Copy,
                               scale=scale).then_inc(jh_done, 1)

            def transposed_upper(h, i):
                for g, k0, nk in groups(i):
                    act.wait_ge(T_mm, TG * h + g + 1)
                    if g == groups(i)[0][0] and (i > 1 or type(h) is not int or h):
                        act.wait_ge(v_mm, 4 * h + i // 2)
                    act.activation(pth[:, k0:k0 + nk, i % 2 * P:(i % 2 + 1) * P],
                                   T_ps[g % 2][:, 0:nk * P].rearrange("p (k n) -> p k n", n=P), ACT.Copy).then_inc(Th_done, 1)

            def exponential(h, i, older):
                act.wait_ge(max_done, NT * h + i + 1)
                if older >= 2:
                    act.wait_ge(T_mm, last_group(*before(h, i, 2)) + 1)
                w = (i + 1) * P
                act.activation(prob[:, i % 2, 0:w], s_ps[i % 2][:, :, :].rearrange("p a n -> p (a n)")[:, 0:w], ACT.Exp,
                               bias=nmax[:, i % 2:i % 2 + 1], accum_out=rsum[:, i % 2:i % 2 + 1]).then_inc(exp_done, 1)

            def head(h, u, first, behind):
                for i in range(NT):
                    if i:
                        transposed_upper(h, i - 1)
                    exponential(h, i, i if first else 2)
                    if i == 0 and not first:
                        transposed_upper(h - 1, NT - 1)
                    if not behind:
                        continue
                    if i < 4:
                        project_upper(h + 1, 1 - u, i)
                    if i == 5:
                        if not first:
                            act.wait_ge(v_mm, 4 * h)
                        v_upper(h + 1, 1 - u)
                    if i == 6:
                        r_upper(h + 1, 1 - u)
                    if i == 4 and behind > 1:
                        w_upper(h + 2)

            def r_copy(t):
                act.wait_ge(r_mm, t + 1)
                if t >= 2:
                    act.wait_ge(rot_part, 2 * t - 2)
                act.activation(qr[:, t % 2, :], (j_ps, v_ps)[t % 2][:, :], ACT.Copy, scale=SCALE).then_inc(qr_done, 1)

            r_copy(0)
            r_copy(1)
            r_copy(2)
            w_upper(0, True)
            for t in range(NT):
                act.wait_ge(all_v_mm, t + 1)
                act.activation(v[:, t, :], s_ps[t % 2][:, :, :].rearrange("p a n -> p (a n)"), ACT.Copy).then_inc(v_copied, 1)
                if t + 3 < NT:
                    r_copy(t + 3)
                act.wait_ge(qrT_mm, t + 1)
                act.activation(qrT[:, :, t * P:(t + 1) * P], T_ps[t % 2][:, :].rearrange("p (a n) -> p a n", a=4),
                               ACT.Copy).then_inc(qrT_copied, 1)
            act.wait_ge(qrT_copied, NT)
            r_upper(0, 0)
            for g in range(4):
                project_upper(0, 0, g, True)
            w_upper(1)
            act.wait_ge(v_copied, NT)
            v_upper(0, 0)
            heads(act, head)
            transposed_upper(H - 1, NT - 1)

        @block.gpsimd
        def _(pool):
            pool.memset(early[:, 0:P // 2], 1.0)
            pool.memset(early[:, P // 2:], 0.0)
            pool.memset(late[:, :], FAR).then_inc(mask_done, 1)
            pool.wait_ge(rope_in, 32)
            W = MROPE // 2
            for t in range(NT):
                pool.wait_ge(qr_done, t + 1)
                if t >= 2:
                    pool.wait_ge(qrT_mm, t - 1)
                q = qr[:, t % 2, :].rearrange("p (a u n) -> p a u n", u=2, n=W)
                r = rot[:, t % 2, :].rearrange("p (a u n) -> p a u n", u=2, n=W)
                w = tmp[:, :].rearrange("p (a u n) -> p a u n", u=2, n=W)
                c = cos[:, t:t + 1, :].broadcast_to([P, H, W])
                s = sin[:, t:t + 1, :].broadcast_to([P, H, W])
                pool.tensor_tensor(r[:, :, 0, :], q[:, :, 0, :], c, ALU.mult)
                pool.tensor_tensor(r[:, :, 1, :], q[:, :, 1, :], c, ALU.mult)
                if t:
                    pool.wait_ge(rot_part, 2 * t)
                pool.tensor_tensor(w[:, :, 0, :], q[:, :, 1, :], s, ALU.mult)
                pool.tensor_tensor(w[:, :, 1, :], q[:, :, 0, :], s, ALU.mult).then_inc(rot_part, 1)
                pool.wait_ge(rot_part, 2 * t + 1)
                pool.tensor_tensor(r[:, :, 0, :], r[:, :, 0, :], w[:, :, 0, :], ALU.subtract)
                pool.tensor_tensor(r[:, :, 1, :], r[:, :, 1, :], w[:, :, 1, :], ALU.add).then_inc(rot_part, 1)

        @block.vector
        def _(dve):
            def w_lower(h):
                dve.wait_ge(wh_done, h + 1)
                for k in range(5):
                    last = dve.scalar_tensor_tensor(wl[:, k, :], raw[:, k, :], gains[:, k:k + 1],
                                                    wh[:, k, :].bitcast(F32), ALU.mult, ALU.subtract)
                last.then_inc(wl_done, 1)

            def v_lower(h, slot):
                dve.wait_ge(vh_done, h + 1)
                dve.tensor_tensor(vl[:, slot, :, :], v[:, :, ds(h * MV, MV)], vh[:, slot, :, :].bitcast(F32),
                                  ALU.subtract).then_inc(vl_done, 1)

            def r_lower(h, u):
                rows = slice(u * MROPE, (u + 1) * MROPE)
                dve.wait_ge(rh_done, h + 1)
                dve.tensor_tensor(rl[rows, :], qrT[rows, ds(h // 2, 1), :].rearrange("p a n -> p (a n)"),
                                  rh[rows, :].bitcast(F32), ALU.subtract).then_inc(rl_done, 1)

            def project_lower(h, u, g, first=False):
                dve.wait_ge(jh_done, 4 * h + g + 1)
                at, bank = slice(g % 2 * HALF, (g % 2 + 1) * HALF), project_bank(g, first)
                if g < 2:
                    dve.scalar_tensor_tensor(ql[:, u, at], bank[:, :], SCALE, qh[:, u, at].bitcast(F32),
                                             ALU.mult, ALU.subtract).then_inc(jl_done, 1)
                else:
                    dve.tensor_tensor(kl[:, u, at], bank[:, :], kh[:, u, at].bitcast(F32), ALU.subtract).then_inc(jl_done, 1)

            def maximum(h, i):
                dve.wait_ge(s_mm, NT * h + i + 1)
                w = (i + 1) * P
                dve.tensor_reduce(nmax[:, i % 2:i % 2 + 1], s_ps[i % 2][:, :, :].rearrange("p a n -> p (a n)")[:, 0:w],
                                  AX_X, ALU.max, negate=True).then_inc(max_done, 1)

            def transposed_lower(h, i):
                for g, k0, nk in groups(i):
                    dve.wait_ge(Th_done, TG * h + g + 1)
                    at = (slice(None), slice(k0, k0 + nk), slice(i % 2 * P, (i % 2 + 1) * P))
                    dve.tensor_tensor(ptl[at], T_ps[g % 2][:, 0:nk * P].rearrange("p (k n) -> p k n", n=P),
                                      pth[at].bitcast(F32), ALU.subtract).then_inc(Tl_done, 1)

            def normalise(h, i):
                n = NT * h + i
                dve.wait_ge(exp_done, n + 1)
                dve.reciprocal(rinv[:, i % 2:i % 2 + 1], rsum[:, i % 2:i % 2 + 1]).then_inc(inv_done, 1)
                dve.wait_ge(inv_done, n + 1)
                w = (i + 1) * P
                dve.tensor_scalar(prob[:, i % 2, 0:w], prob[:, i % 2, 0:w], rinv[:, i % 2:i % 2 + 1], None,
                                  ALU.mult).then_inc(prob_done, 1)

            def gate(h, j, slot):
                dve.wait_ge(v_mm, 4 * h + j + 1)
                if j == 0:
                    dve.wait_ge(sg_in[slot], 8 * (h - slot) + 16)
                at = slice(2 * j * P, (2 * j + 2) * P)
                dve.tensor_tensor(sg[:, slot, at], v_ps[:, 0:2 * P], sg[:, slot, at], ALU.mult).then_inc(g_done, 1)

            def head(h, u, first, behind):
                for i in range(NT):
                    if i:
                        maximum(h, i)
                        if i >= 3 and i % 2:
                            gate(h, (i - 3) // 2, u)
                        if i == 1 and not first:
                            gate(h - 1, 3, 1 - u)
                        transposed_lower(h, i - 1)
                    else:
                        maximum(h, 0)
                        if not first:
                            transposed_lower(h - 1, NT - 1)
                    normalise(h, i)
                    if not behind:
                        continue
                    if i < 4:
                        project_lower(h + 1, 1 - u, i)
                    if i == 4 and behind > 1:
                        w_lower(h + 2)
                    if i == 5:
                        v_lower(h + 1, 1 - u)
                    if i == 6:
                        r_lower(h + 1, 1 - u)

            w_lower(0)
            r_lower(0, 0)
            for g in range(4):
                project_lower(0, 0, g, True)
            w_lower(1)
            v_lower(0, 0)
            heads(dve, head)
            transposed_lower(H - 1, NT - 1)
            gate(H - 1, 3, 1)

        @block.tensor
        def _(pe):
            def three(out, pairs, start, stop):
                (ah, al), (bh, bl) = pairs
                pe.matmul(out, al, bh, start=start, stop=False)
                pe.matmul(out, ah, bl, start=False, stop=False)
                return pe.matmul(out, ah, bh, start=False, stop=stop)

            def project(h, g, first=False):
                if g == 0:
                    pe.wait_ge(wl_done, h + 1)
                ks, (sh, sl), half = projection(g)
                if first and g >= 2:
                    pe.wait_ge(jl_done, g - 1)
                if not first:
                    pe.wait_ge(jl_done, 4 * h + g)
                at = slice(half * HALF, (half + 1) * HALF)
                for k in ks:
                    src = k - 2 if g < 2 else k
                    last = three(project_bank(g, first)[:, :], ((wh[:, k, :], wl[:, k, :]), (sh[:, src, at], sl[:, src, at])),
                                 k == ks[0], k == ks[-1])
                last.then_inc(j_mm, 1)

            def scores(h, i, u, older):
                if older >= 2:
                    pe.wait_ge(exp_done, NT * h + i - 1)
                if i == 0:
                    pe.wait_ge(jl_done, 4 * h + 4)
                    pe.wait_ge(rl_done, h + 1)
                q, r = slice(i * P, (i + 1) * P), slice(u * MROPE, (u + 1) * MROPE)
                for c in range(i // 4 + 1):
                    n = min(HALF, (i + 1) * P - c * HALF)
                    ks = slice(c * HALF, c * HALF + n)
                    out = s_ps[i % 2][:, c, 0:n]
                    three(out, ((qh[:, u, q], ql[:, u, q]), (kh[:, u, ks], kl[:, u, ks])), True, False)
                    last = three(out, ((rh[r, q], rl[r, q]), (kvh[r, 2, ks], kvl[r, 2, ks])), False, c < i // 4)
                    if c == i // 4:
                        last = pe.matmul(s_ps[i % 2][:, c, n - P // 2:n], early[:, :], late[:, :], start=False, stop=True)
                last.then_inc(s_mm, 1)

            def transposes(h, i, older):
                pe.wait_ge(prob_done, NT * h + i + 1)
                for g, k0, nk in groups(i):
                    if older >= 2 or g >= 2:
                        pe.wait_ge(Tl_done, TG * h + g - 1)
                    for k in range(nk):
                        last = pe.transpose(T_ps[g % 2][:, k * P:(k + 1) * P],
                                            prob[:, i % 2, (k0 + k) * P:(k0 + k + 1) * P], ident[:])
                    last.then_inc(T_mm, 1)

            def values(h, j, slot):
                pe.wait_ge(Tl_done, last_group(h, 2 * j + 1) + 1)
                if j == 0:
                    pe.wait_ge(vl_done, h + 1)
                else:
                    pe.wait_ge(g_done, 4 * h + j)
                for k in range(2 * j + 2):
                    a = P if k == 2 * j + 1 else 0
                    last = three(v_ps[:, a:2 * P], ((vh[:, slot, k, :], vl[:, slot, k, :]), (pth[:, k, a:], ptl[:, k, a:])),
                                 k == 0, k == 2 * j + 1)
                last.then_inc(v_mm, 1)

            def head(h, u, first, behind):
                for i in range(NT):
                    scores(h, i, u, i if first else 2)
                    if i == 0 and behind:
                        project(h + 1, 0)
                    if i == 0 and not first:
                        transposes(h - 1, NT - 1, 2)
                    if i == 1 and not first:
                        values(h - 1, 3, 1 - u)
                    if i >= 3 and i % 2:
                        values(h, (i - 3) // 2, u)
                    if i:
                        transposes(h, i - 1, i - 1 if first else 2)
                    if 0 < i < 4 and behind:
                        project(h + 1, i)

            def rotary(t):
                if t >= 2:
                    pe.wait_ge(qr_done, t - 1)
                for k in range(3):
                    last = three((j_ps, v_ps)[t % 2][:, :],
                                 ((cqh[:, k, t * P:(t + 1) * P], cql[:, k, t * P:(t + 1) * P]),
                                  (spare[0][:, 4 + k, :], spare[1][:, 4 + k, :])), k == 0, k == 2)
                last.then_inc(r_mm, 1)

            rotary(0)
            rotary(1)
            rotary(2)
            for t in range(NT):
                if t >= 2:
                    pe.wait_ge(v_copied, t - 1)
                for n in range(2):
                    for k in range(2):
                        last = three(s_ps[t % 2][:, n, :],
                                     ((kvh[:, k, t * P:(t + 1) * P], kvl[:, k, t * P:(t + 1) * P]),
                                      (spare[0][:, 2 * k + n, :], spare[1][:, 2 * k + n, :])), k == 0, k == 1)
                last.then_inc(all_v_mm, 1)
                if t + 3 < NT:
                    rotary(t + 3)
                pe.wait_ge(rot_part, 2 * t + 2)
                if t >= 2:
                    pe.wait_ge(qrT_copied, t - 1)
                for k in range(4):
                    last = pe.transpose(T_ps[t % 2][:, k * P:(k + 1) * P], rot[:, t % 2, k * P:(k + 1) * P], ident[:])
                last.then_inc(qrT_mm, 1)
            pe.wait_ge(qr_done, NT)
            for g in range(4):
                project(0, g, True)
            pe.wait_ge(mask_done, 1)
            pe.wait_ge(v_copied, NT)
            pe.wait_ge(qrT_copied, NT)
            heads(pe, head)
            transposes(H - 1, NT - 1, 2)
            values(H - 1, 3, 1)
    return sems


def gla_masks():
    out = np.zeros((P, GLA_LEVELS, P // 2), np.uint32)
    for level in range(GLA_LEVELS):
        size = 1 << level
        for block in range(P // (2 * size)):
            out[2 * block * size:(2 * block + 1) * size, level, block * size:(block + 1) * size] = 1
    return out


def gla_columns(w_in):
    w = w_in.reshape(KT, P, -1)
    k, v = GLA_HEADS * GK, GLA_HEADS * GV
    qk = [w[:, :, i * k:(i + 1) * k].reshape(KT, P, GLA_HEADS, GK) for i in range(2)]
    vr = [w[:, :, 2 * k + i * v:2 * k + (i + 1) * v].reshape(KT, P, GLA_HEADS, GV) for i in range(2)]
    lay = lambda parts: np.ascontiguousarray(np.concatenate(parts, axis=3).transpose(2, 1, 0, 3))
    return lay(qk), lay(vr), np.ascontiguousarray(w[:, :, 2 * k + 2 * v:].transpose(1, 0, 2))


def gla_heads(nc, xT, gain, w_qk, w_vr, w_low, w_up, b_gk, masks, ident, neghalf, staging, arrived, ahead, gated):
    with ExitStack() as ctx:
        def sb(name, shape, dt=F32):
            return ctx.enter_context(nc.sbuf_tensor("gl_" + name, shape, dt))

        def bank(name, shape=(P, HALF)):
            return ctx.enter_context(nc.psum_tensor("gl_" + name, list(shape), F32))

        def sem(name):
            return ctx.enter_context(nc.semaphore("gl_" + name))

        NL = GLA_LEVELS
        KD, QD, QK = NL, NL + 1, NL + 2
        BT = NT // 2
        INV_NORM = 1.0 / 16.0
        xh, xl = xT
        qkh = sb("qkh", [P, KT, 2 * GK], F32R)
        qkl = sb("qkl", [P, KT, 2 * GK], F32R)
        vrh = sb("vrh", [P, KT, 2 * GV], F32R)
        vrl = sb("vrl", [P, KT, 2 * GV], F32R)
        lowh = sb("lowh", [P, KT, GRANK], F32R)
        lowl = sb("lowl", [P, KT, GRANK], F32R)
        raw_low = sb("raw_low", [P, KT, GRANK])
        raw = staging
        bias = sb("bias", [P, GLA_HEADS])
        up = sb("up", [GRANK, GK])
        low = sb("low", [GRANK, SEQ])
        mn = sb("mn", [P, 2, SEQ])
        b = sb("b", [P, SEQ])
        lv = sb("lv", [P, 2, NL + 3, HALF])
        last_decay = sb("last_decay", [P, NT])
        q = sb("q", [P, SEQ])
        k = sb("k", [P, SEQ])
        v = sb("v", [P, 4, GV])
        sr = sb("sr", [P, NT, GV])
        oS = sb("oS", [P, 2, GV])
        osq = sb("osq", [P, GV])
        aT = sb("aT", [P, P])
        aT_parts = [sb("aT_even", [P, P]), sb("aT_odd", [P, P])]
        kt_ = sb("kt_", [P, P])
        R = sb("R", [P, GV])
        ones = sb("ones", [P, P])
        mask = sb("mask", [P, NL, P // 2], U32)
        so = sb("so", [P, 8])
        mo = sb("mo", [P, 2])
        ro = sb("ro", [P, 2])

        j_ps = bank("j_ps", (P, 2, HALF))
        vr_ps = [bank("vr_ps0"), bank("vr_ps1")]
        l_ps, T_ps, o_ps, k_ps = (bank(n) for n in ("l_ps", "T_ps", "o_ps", "k_ps"))

        low_gained, con_in, low_in, up_in = sem("low_gained"), sem("con_in"), sem("low_in"), sem("up_in")
        raw_in = arrived
        g_out = [sem(f"g_out{t}") for t in range(NT)]
        (ones_set, lowh_done, lowl_done, low_mm,
         low_copied, wh_done, wl_done, z_mm, mn_done, d_done, e_done, ln_done, la_done, b_done, sub_done, exp_done,
         mul_done, qk_mm, qk_copied, vr_mm, v_copied, silu_done, score_mm, part_done, mask_done, attend_mm, R_done,
         o_copied, sq_done, mo_done, ro_done, G_done) = (sem(n) for n in (
            "ones_set lowh_done lowl_done low_mm "
            "low_copied wh_done wl_done z_mm mn_done d_done e_done ln_done la_done b_done sub_done exp_done "
            "mul_done qk_mm qk_copied vr_mm v_copied silu_done score_mm part_done mask_done attend_mm R_done "
            "o_copied sq_done mo_done ro_done G_done").split())
        block = ctx.enter_context(nc.Block())
        H = GLA_HEADS
        LAST = H * NT
        PIECES = 6

        def before(h, t, n):
            return (h, t - n) if t >= n else (h - 1, t - n + NT)

        def gate_bank(half, first):
            return vr_ps[half][:, :] if first else j_ps[:, half, :]

        def piece_rows(i):
            if i < 2:
                return qkh, qkl, range(4 * i, 4 * i + 4), 2 * GK
            return vrh, vrl, range(2 * (i - 2), 2 * (i - 2) + 2), 2 * GV

        def heads(eng, head):
            head(0, 0, True)
            with eng.Fori(1, H - 1) as h:
                head(h, 1, True)
            head(H - 1, 1, False)

        @block.sync
        def _(sp):
            def load_piece(h, i):
                sp.wait_ge(wl_done, PIECES * h + i - 1)
                _, _, rows, _ = piece_rows(i)
                src = w_qk if i < 2 else w_vr
                sp.dma_start(raw[:, i % 2, :], src[ds(h, 1), :, rows[0]:rows[-1] + 1, :].rearrange("a p k n -> p (a k n)"))\
                  .then_inc(raw_in[i % 2], 16)

            def load_up(h):
                sp.dma_start(up[:], w_up[:, ds(h * GK, GK)]).then_inc(up_in, 16)

            def store(s, h, t):
                sp.wait_ge(G_done, s + 1)
                sp.dma_start(gated[t * P:(t + 1) * P, ds(h * GV, GV)], sr[:, t, :]).then_inc(g_out[t], 16)

            def head(h, older, more):
                for t in range(NT):
                    if older or t >= 4:
                        store(h * NT + t - 4, *before(h, t, 4))
                    if more:
                        if t == 0:
                            load_piece(h + 1, 0)
                            load_piece(h + 1, 1)
                        if t == 2:
                            load_piece(h + 1, 2)
                            load_piece(h + 1, 3)
                            sp.wait_ge(z_mm, h + 1)
                            load_up(h + 1)
                if more:
                    load_piece(h + 1, 4)
                    load_piece(h + 1, 5)

            sp.dma_start(raw_low[:], w_low).then_inc(low_in, 16)
            load_up(0)
            sp.dma_start(bias[:], b_gk).then_inc(con_in, 16)
            sp.dma_start(mask[:], masks).then_inc(con_in, 16)
            for i in range(2, PIECES):
                load_piece(0, i)
            heads(sp, head)
            sp.wait_ge(wl_done, PIECES * H)
            ahead(sp)
            for t in range(4, NT):
                store(LAST - NT + t, H - 1, t)
            for t in range(NT):
                sp.wait_ge(g_out[t], 16 * H)

        @block.scalar
        def _(act):
            def w_upper(h, i):
                up_, _, rows, n = piece_rows(i)
                act.wait_ge(raw_in[i % 2], 16 * (PIECES // 2 * h + i // 2 + 1))
                for j, r in enumerate(rows):
                    last = act.activation(up_[:, r, :], raw[:, i % 2, j * n:(j + 1) * n], ACT.Copy, scale=gain[:, r:r + 1])
                last.then_inc(wh_done, 1)

            def log_gates(h):
                act.wait_ge(d_done, h + 1)
                act.activation(mn[:, 1, :], mn[:, 1, :], ACT.Exp).then_inc(e_done, 1)
                act.wait_ge(e_done, h + 1)
                act.activation(mn[:, 1, :], mn[:, 1, :], ACT.Ln, bias=1.0).then_inc(ln_done, 1)

            def exponentials(h, c):
                act.wait_ge(sub_done, 2 * h + c + 1)
                act.activation(lv[:, c, 0:QD, :], lv[:, c, 0:QD, :], ACT.Exp, scale=INV_NORM)
                act.activation(lv[:, c, QD, :], b[:, c * HALF:(c + 1) * HALF], ACT.Exp, scale=INV_NORM)
                act.activation(last_decay[:, BT * c:BT * (c + 1)],
                               b[:, c * HALF:(c + 1) * HALF].rearrange("p (t n) -> p t n", n=P)[:, :, P - 1],
                               ACT.Exp, scale=INV_NORM).then_inc(exp_done, 1)

            def qk_copy(h, g):
                act.wait_ge(qk_mm, 4 * h + g + 1)
                dst, scale = ((q, GK ** -0.5), (k, 1.0))[g % 2]
                act.activation(dst[:, g // 2 * HALF:(g // 2 + 1) * HALF], j_ps[:, g % 2, :], ACT.Copy,
                               scale=scale).then_inc(qk_copied, 1)

            def evacuate(s, h, t, older):
                act.wait_ge(vr_mm, s + 1)
                if older or t >= 4:
                    act.wait_ge(attend_mm, s - 3)
                act.activation(v[:, t % 4, :], vr_ps[t % 2][:, 0:GV], ACT.Copy).then_inc(v_copied, 1)
                if older:
                    act.wait_ge(g_out[t], 16 * h)
                act.activation(sr[:, t, :], vr_ps[t % 2][:, GV:], ACT.Silu).then_inc(silu_done, 1)

            def output(s, t, older):
                act.wait_ge(attend_mm, s + 1)
                if older or t >= 2:
                    act.wait_ge(G_done, s - 1)
                act.activation(oS[:, t % 2, :], o_ps[:, 0:GV], ACT.Copy).then_inc(o_copied, 1)
                act.wait_ge(o_copied, s + 1)
                act.activation(osq[:, :], oS[:, t % 2, :], ACT.Square, accum_out=so[:, t % 2:t % 2 + 1]).then_inc(sq_done, 1)

            def head(h, older, more):
                for t in range(NT):
                    s = h * NT + t
                    evacuate(s, h, t, older)
                    if older or t >= 3:
                        _, tt = before(h, t, 3)
                        output(s - 3, tt, older if t >= 3 else older)
                    if more and t < 2:
                        w_upper(h + 1, t)
                    if t == 3:
                        exponentials(h, 1)
                    if more and t == 5:
                        log_gates(h + 1)
                if more:
                    for g in range(4):
                        w_upper(h + 1, 2 + g)
                        qk_copy(h + 1, g)
                        if g == 0:
                            exponentials(h + 1, 0)

            act.wait_ge(low_gained, 1)
            act.activation(lowh[:, :, :], raw_low[:, :, :], ACT.Copy).then_inc(lowh_done, 1)
            w_upper(0, 0)
            w_upper(0, 1)
            for half in range(2):
                act.wait_ge(low_mm, half + 1)
                act.activation(low[:, half * HALF:(half + 1) * HALF], vr_ps[half][0:GRANK, :], ACT.Copy).then_inc(low_copied, 1)
            w_upper(0, 2)
            log_gates(0)
            w_upper(0, 3)
            qk_copy(0, 0)
            w_upper(0, 4)
            qk_copy(0, 1)
            w_upper(0, 5)
            qk_copy(0, 2)
            exponentials(0, 0)
            qk_copy(0, 3)
            heads(act, head)
            for s in range(LAST - 3, LAST):
                output(s, s % NT, 1)

        @block.gpsimd
        def _(pool):
            def rms_o(s, t):
                pool.wait_ge(sq_done, s + 1)
                wait_alone(pool)
                pool.tensor_scalar(mo[:, t % 2:t % 2 + 1], so[:, t % 2:t % 2 + 1], 1.0 / GV, EPS, ALU.mult, ALU.add)\
                    .then_inc(mo_done, 1)
                pool.wait_ge(mo_done, s + 1)
                pool.tensor_tensor(ro[:, t % 2:t % 2 + 1], mo[:, t % 2:t % 2 + 1], neghalf[:], ALU.pow).then_inc(ro_done, 1)

            for part in aT_parts:
                pool.memset(part[:], 0.0)
            pool.memset(ones[:], 1.0).then_inc(ones_set, 1)
            with pool.Fori(0, H) as h:
                for t in range(NT):
                    rms_o(h * NT + t, t)

        @block.vector
        def _(dve):
            def w_lower(h, i):
                up_, lo_, rows, n = piece_rows(i)
                dve.wait_ge(wh_done, PIECES * h + i + 1)
                for j, r in enumerate(rows):
                    last = dve.scalar_tensor_tensor(lo_[:, r, :], raw[:, i % 2, j * n:(j + 1) * n], gain[:, r:r + 1],
                                                    up_[:, r, :].bitcast(F32), ALU.mult, ALU.subtract)
                last.then_inc(wl_done, 1)

            def split_gates(h, first=False):
                dve.wait_ge(z_mm, h + 1)
                for half in range(2):
                    at = slice(half * HALF, (half + 1) * HALF)
                    dve.tensor_scalar(mn[:, 0, at], gate_bank(half, first), bias[:, ds(h, 1)], 0.0, ALU.add, ALU.min)
                    last = dve.tensor_scalar(mn[:, 1, at], gate_bank(half, first), bias[:, ds(h, 1)], 0.0, ALU.add, ALU.max)
                last.then_inc(mn_done, 1)
                dve.wait_ge(mn_done, h + 1)
                dve.tensor_tensor(mn[:, 1, :], mn[:, 0, :], mn[:, 1, :], ALU.subtract).then_inc(d_done, 1)

            def sum_gates(h):
                dve.wait_ge(ln_done, h + 1)
                dve.tensor_tensor(mn[:, 0, :], mn[:, 0, :], mn[:, 1, :], ALU.subtract).then_inc(la_done, 1)
                dve.wait_ge(la_done, h + 1)
                for t in range(NT):
                    at = slice(t * P, (t + 1) * P)
                    last = dve.tensor_tensor_scan(b[:, at], ones[:, :], mn[:, 0, at], 0.0, ALU.mult, ALU.add)
                last.then_inc(b_done, 1)

            def exponents(h, c, older):
                dve.wait_ge(b_done, h + 1)
                if older:
                    dve.wait_ge(attend_mm, (h - 1) * NT + BT * c + BT)
                at = slice(c * HALF, (c + 1) * HALF)
                for level in range(NL):
                    n = 1 << level
                    src = b[:, at].rearrange("p (g u n) -> p g u n", u=2, n=n)
                    dst = lv[:, c, level, :].rearrange("p (g u n) -> p g u n", u=2, n=n)
                    mid = src[:, :, 0, n - 1:n].broadcast_to([P, HALF // (2 * n), n])
                    dve.tensor_tensor(dst[:, :, 0, :], mid, src[:, :, 0, :], ALU.subtract)
                    dve.tensor_tensor(dst[:, :, 1, :], src[:, :, 1, :], mid, ALU.subtract)
                src = b[:, at].rearrange("p (t n) -> p t n", n=P)
                dve.tensor_tensor(lv[:, c, KD, :].rearrange("p (t n) -> p t n", n=P),
                                  src[:, :, P - 1:P].broadcast_to([P, BT, P]), src, ALU.subtract).then_inc(sub_done, 1)

            def products(h, c):
                dve.wait_ge(exp_done, 2 * h + c + 1)
                dve.wait_ge(qk_copied, 4 * h + 2 * c + 2)
                at = slice(c * HALF, (c + 1) * HALF)
                for level in range(NL):
                    n = 1 << level
                    dst = lv[:, c, level, :].rearrange("p (g u n) -> p g u n", u=2, n=n)
                    for u, src in enumerate((k, q)):
                        dve.tensor_tensor(dst[:, :, u, :], dst[:, :, u, :],
                                          src[:, at].rearrange("p (g u n) -> p g u n", u=2, n=n)[:, :, u, :], ALU.mult)
                dve.tensor_tensor(lv[:, c, KD, :], lv[:, c, KD, :], k[:, at], ALU.mult)
                dve.tensor_tensor(lv[:, c, QD, :], lv[:, c, QD, :], q[:, at], ALU.mult)
                dve.tensor_tensor(lv[:, c, QK, :], q[:, at], k[:, at], ALU.mult).then_inc(mul_done, 1)

            def carry_state(s, t, older):
                dve.wait_ge(attend_mm, s + 1)
                if t == 0:
                    dve.tensor_copy(R[:, :], k_ps[:, 0:GV]).then_inc(R_done, 1)
                else:
                    dve.wait_ge(R_done, s)
                    dve.scalar_tensor_tensor(R[:, :], R[:, :], last_decay[:, t:t + 1], k_ps[:, 0:GV],
                                             ALU.mult, ALU.add).then_inc(R_done, 1)

            def gate(s, t):
                dve.wait_ge(ro_done, s + 1)
                dve.wait_ge(silu_done, s + 1)
                dve.scalar_tensor_tensor(sr[:, t, :], oS[:, t % 2, :], ro[:, t % 2:t % 2 + 1], sr[:, t, :],
                                         ALU.mult, ALU.mult).then_inc(G_done, 1)

            def gather_weights(s, older):
                dve.wait_ge(score_mm, s + 1)
                if older:
                    dve.wait_ge(attend_mm, s)
                    wait_alone(dve)
                dve.tensor_copy(kt_[:, :], T_ps[:, P:2 * P])
                for i, level in enumerate((0, None, 2, 1, 4, 3, 6, 5)):
                    dst, n = aT_parts[i % 2], 1 << (level or 0)
                    if i >= 2:
                        dve.wait_ge(part_done, (NL + 1) * s + i - 1)
                        wait_alone(dve)
                    if level is None:
                        last = dve.copy_predicated(dst[:, :], ident[:].bitcast(U32), T_ps[:, 0:P])
                    else:
                        last = dve.copy_predicated(
                            dst[:, :].rearrange("p (g u n) -> p g u n", u=2, n=n)[:, :, 1, :],
                            mask[:, level, :].rearrange("p (g n) -> p g n", n=n),
                            l_ps[:, level * (P // 2):(level + 1) * (P // 2)].rearrange("p (g n) -> p g n", n=n))
                    last.then_inc(part_done, 1)
                dve.wait_ge(part_done, (NL + 1) * s + NL + 1)
                dve.tensor_tensor(aT[:, :], aT_parts[0][:, :], aT_parts[1][:, :], ALU.add).then_inc(mask_done, 1)

            def step(s, h, t, older):
                if older or t >= 3:
                    carry_state(s - 3, (t - 3) % NT, older)
                if older or t >= 4:
                    gate(s - 4, (t - 4) % NT)
                if older or t >= 2:
                    gather_weights(s - 2, older or t >= 3)

            def head(h, older, more):
                for t in range(NT):
                    step(h * NT + t, h, t, older)
                    if more and t < 2:
                        w_lower(h + 1, t)
                    if t == 3:
                        exponents(h, 1, older)
                    if t == 4:
                        products(h, 1)
                    if more and t == 5:
                        split_gates(h + 1)
                    if more and t == 6:
                        dve.wait_ge(exp_done, 2 * h + 2)
                        sum_gates(h + 1)
                    if more and t == 7:
                        exponents(h + 1, 0, 1)
                if more:
                    for i in range(2, PIECES):
                        w_lower(h + 1, i)
                    products(h + 1, 0)

            dve.wait_ge(low_in, 16)
            dve.tensor_tensor(raw_low[:, :, :], raw_low[:, :, :], gain[:, :].unsqueeze(2).broadcast_to([P, KT, GRANK]),
                              ALU.mult).then_inc(low_gained, 1)
            dve.wait_ge(lowh_done, 1)
            dve.tensor_tensor(lowl[:, :, :], raw_low[:, :, :], lowh[:, :, :].bitcast(F32), ALU.subtract).then_inc(lowl_done, 1)
            w_lower(0, 0)
            w_lower(0, 1)
            dve.wait_ge(con_in, 32)
            dve.wait_ge(ones_set, 1)
            split_gates(0, True)
            w_lower(0, 2)
            sum_gates(0)
            w_lower(0, 3)
            exponents(0, 0, 0)
            w_lower(0, 4)
            w_lower(0, 5)
            products(0, 0)
            heads(dve, head)
            for s in range(LAST, LAST + 4):
                if s < LAST + 3:
                    carry_state(s - 3, s % NT + NT - 3, 1)
                gate(s - 4, s % NT + NT - 4)
                if s < LAST + 2:
                    gather_weights(s - 2, 1)

        @block.tensor
        def _(pe):
            def transposed_product(out, wh_, wl_, cols, half):
                at = slice(half * HALF, (half + 1) * HALF)
                for r in range(KT):
                    for i, (w, xx) in enumerate(((wl_, xh), (wh_, xl), (wh_, xh))):
                        last = pe.matmul(out, w[:, r, cols], xx[:, r, at], start=(r == 0 and i == 0),
                                         stop=(r == KT - 1 and i == 2))
                return last

            def gates(h, first=False):
                pe.wait_ge(up_in, 16 * h + 16)
                for half in range(2):
                    last = pe.matmul(gate_bank(half, first), up[:, :], low[:, half * HALF:(half + 1) * HALF], start=True, stop=True)
                last.then_inc(z_mm, 1)

            def project_qk(h, older):
                pe.wait_ge(wl_done, PIECES * h + 2)
                if older:
                    pe.wait_ge(mn_done, h + 1)
                for g in range(4):
                    if g >= 2:
                        pe.wait_ge(qk_copied, 4 * h + g - 1)
                    transposed_product(j_ps[:, g % 2, :], qkh, qkl, slice(g % 2 * GK, (g % 2 + 1) * GK),
                                       g // 2).then_inc(qk_mm, 1)

            def project_vr(s, h, t, older):
                if t == 0:
                    pe.wait_ge(wl_done, PIECES * h + PIECES)
                    if not older:
                        pe.wait_ge(mn_done, 1)
                if older or t >= 2:
                    pe.wait_ge(silu_done, s - 1)
                for r in range(KT):
                    for i, (xx, w) in enumerate(((xl, vrh), (xh, vrl), (xh, vrh))):
                        last = pe.matmul(vr_ps[t % 2][:, :], xx[:, r, t * P:(t + 1) * P], w[:, r, :],
                                         start=(r == 0 and i == 0), stop=(r == KT - 1 and i == 2))
                last.then_inc(vr_mm, 1)

            def attend(s, t, older):
                c, at = t // BT, slice(t % BT * P, (t % BT + 1) * P)
                pe.wait_ge(mask_done, s + 1)
                if older:
                    pe.wait_ge(o_copied, s)
                    pe.wait_ge(R_done, s)
                pe.matmul(o_ps[:, 0:GV], aT[:, :], v[:, t % 4, :], start=True, stop=(t == 0))
                if t:
                    pe.matmul(o_ps[:, 0:GV], lv[:, c, QD, at], R[:, :], start=False, stop=True)
                pe.matmul(k_ps[:, 0:GV], kt_[:, :], v[:, t % 4, :], start=True, stop=True).then_inc(attend_mm, 1)

            def scores(s, h, t, older):
                c, at = t // BT, slice(t % BT * P, (t % BT + 1) * P)
                pe.wait_ge(mul_done, 2 * h + c + 1)
                if older:
                    pe.wait_ge(mask_done, s)
                pe.matmul(T_ps[:, 0:P], ones[:, :], lv[:, c, QK, at], start=True, stop=True)
                pe.transpose(T_ps[:, P:2 * P], lv[:, c, KD, at], ident[:])
                for level in range(NL):
                    n = 1 << level
                    last = pe.matmul(l_ps[:, level * (P // 2):(level + 1) * (P // 2)].rearrange("p (g n) -> p g n", n=n),
                                     lv[:, c, level, at],
                                     lv[:, c, level, at].rearrange("p (g u n) -> p g u n", u=2, n=n)[:, :, 1, :],
                                     start=True, stop=True)
                last.then_inc(score_mm, 1)

            def head(h, older, more):
                for t in range(NT):
                    s = h * NT + t
                    project_vr(s, h, t, older)
                    if older or t >= 3:
                        attend(s - 3, before(h, t, 3)[1], older or t >= 4)
                    if older or t >= 2:
                        hh, tt = before(h, t, 2)
                        scores(s - 2, hh, tt, older or t >= 3)
                    if more and t == 4:
                        pe.wait_ge(qk_copied, 4 * h + 4)
                        gates(h + 1)
                if more:
                    pe.wait_ge(mul_done, 2 * h + 2)
                    project_qk(h + 1, 1)

            pe.wait_ge(ones_set, 1)
            pe.wait_ge(lowl_done, 1)
            for half in range(2):
                transposed_product(vr_ps[half][0:GRANK, :], lowh, lowl, slice(0, GRANK), half).then_inc(low_mm, 1)
            pe.wait_ge(low_copied, 2)
            gates(0, True)
            project_qk(0, 0)
            heads(pe, head)
            for s in range(LAST, LAST + 3):
                attend(s - 3, s % NT + NT - 3, 1)
                if s < LAST + 2:
                    scores(s - 2, H - 1, s % NT + NT - 2, 1)


def feed_forward(nc, x, xT, gain, w1, w2, g_final, ident, neghalf, staging, arrived, out):
    with ExitStack() as ctx:
        def sb(name, shape, dt=F32):
            return ctx.enter_context(nc.sbuf_tensor("ff_" + name, shape, dt))

        def sem(name):
            return ctx.enter_context(nc.semaphore("ff_" + name))

        NC = D_FF // HALF
        FT = HALF // P
        xh, xl = xT
        w1h = sb("w1h", [P, KT, HALF], F32R)
        w1l = sb("w1l", [P, KT, HALF], F32R)
        w2h = sb("w2h", [P, FT, DM], F32R)
        w2l = sb("w2l", [P, FT, DM], F32R)
        hh = sb("hh", [P, FT, SEQ], F32R)
        hl = sb("hl", [P, FT, SEQ], F32R)
        acc = sb("acc", [P, NT, DM])
        raw = staging
        relu = sb("relu", [P, HALF])
        ss = sb("ss", [P, NT])
        ms = sb("ms", [P, NT])
        rms = sb("rms", [P, NT])
        f_ps = [ctx.enter_context(nc.psum_tensor(f"ff_f_ps{i}", [P, HALF], F32)) for i in range(2)]
        y_ps = [ctx.enter_context(nc.psum_tensor(f"ff_y_ps{i}", [P, 2, HALF], F32)) for i in range(2)]

        raw_in = arrived
        x_in = [sem("x_in0"), sem("x_in1")]
        (final_in, out_done, ss_done, ms_done, rms_done, wh_done,
         wl_done, f_mm, relu_done, sq_done, hh_done, hl_done, y_mm, y_added, fin_done) = (
            sem(n) for n in ("final_in out_done ss_done ms_done rms_done "
                             "wh_done wl_done f_mm relu_done sq_done hh_done hl_done y_mm y_added fin_done").split())
        block = ctx.enter_context(nc.Block())

        @block.sync
        def _(sp):
            def load_w(c, n):
                if n < 4:
                    src = w1[ds(c, 1), :, 2 * n:2 * n + 2, :].rearrange("a p k n -> p (a k n)")
                else:
                    src = w2[ds(c * HALF + (n - 4) * P, P), :]
                sp.dma_start(raw[:, n % 2, :], src).then_inc(raw_in[n % 2], 16)

            def load_x(i):
                sp.dma_start(acc[:, 4 * i:4 * i + 4, :], x[i * HALF:(i + 1) * HALF, :].rearrange("(t p) n -> p t n", p=P))\
                  .then_inc(x_in[i], 16)

            for n in range(2, 8):
                sp.wait_ge(wl_done, n - 1)
                load_w(0, n)
                if n >= 6:
                    load_x(n - 6)
            with sp.Fori(1, NC) as c:
                for n in range(8):
                    sp.wait_ge(wl_done, 8 * c + n - 1)
                    load_w(c, n)
            sp.wait_ge(wl_done, 8 * NC)
            sp.dma_start(raw[:, 0, :], g_final.partition_broadcast(P)).then_inc(final_in, 16)
            for t in range(NT):
                sp.wait_ge(fin_done, t + 1)
                sp.dma_start(out[t * P:(t + 1) * P, :], acc[:, t, :]).then_inc(out_done, 16)
            sp.wait_ge(out_done, 16 * NT)

        @block.scalar
        def _(act):
            def square(t):
                act.activation(xl[:, :, t * P:(t + 1) * P], acc[:, t, :].rearrange("p (k n) -> p k n", k=KT), ACT.Square,
                               accum_out=ss[:, t:t + 1]).then_inc(ss_done, 1)

            def w_upper(c, n):
                act.wait_ge(raw_in[n % 2], 64 * c + 16 * (n // 2) + 16)
                if n < 4:
                    for k in range(2):
                        kt = 2 * n + k
                        last = act.activation(w1h[:, kt, :], raw[:, n % 2, k * HALF:(k + 1) * HALF], ACT.Copy,
                                              scale=gain[:, kt:kt + 1])
                else:
                    last = act.activation(w2h[:, n - 4, :], raw[:, n % 2, :], ACT.Copy)
                last.then_inc(wh_done, 1)

            def h_upper(c, j):
                act.wait_ge(sq_done, 8 * c + j + 1)
                act.activation(hh[:, j % 4, j // 4 * HALF:(j // 4 + 1) * HALF], f_ps[j % 2][:, :], ACT.Copy).then_inc(hh_done, 1)

            def groups(c):
                for j in range(8):
                    act.wait_ge(f_mm, 8 * c + j + 1)
                    act.activation(relu[:, :], f_ps[j % 2][:, :], ACT.Relu).then_inc(relu_done, 1)
                    h_upper(c, j)
                    if j % 2 == 0:
                        w_upper(c, 4 + j // 2)

            for n in range(4):
                w_upper(0, n)
            groups(0)
            with act.Fori(1, NC) as c:
                act.wait_ge(f_mm, 8 * c)
                for n in range(4):
                    w_upper(c, n)
                groups(c)
            for t in range(NT):
                act.wait_ge(y_added, NT * (NC - 1) + t + 1)
                square(t)

        @block.gpsimd
        def _(pool):
            for i in range(NT):
                pool.wait_ge(ss_done, i + 1)
                pool.tensor_scalar(ms[:, i:i + 1], ss[:, i:i + 1], 1.0 / DM, EPS, ALU.mult, ALU.add).then_inc(ms_done, 1)
                pool.wait_ge(ms_done, i + 1)
                pool.tensor_tensor(rms[:, i:i + 1], ms[:, i:i + 1], neghalf[:], ALU.pow).then_inc(rms_done, 1)

        @block.vector
        def _(dve):
            def w_lower(c, n):
                dve.wait_ge(wh_done, 8 * c + n + 1)
                if n < 4:
                    for k in range(2):
                        kt = 2 * n + k
                        last = dve.scalar_tensor_tensor(w1l[:, kt, :], raw[:, n % 2, k * HALF:(k + 1) * HALF],
                                                        gain[:, kt:kt + 1], w1h[:, kt, :].bitcast(F32),
                                                        ALU.mult, ALU.subtract)
                else:
                    last = dve.tensor_tensor(w2l[:, n - 4, :], raw[:, n % 2, :], w2h[:, n - 4, :].bitcast(F32), ALU.subtract)
                last.then_inc(wl_done, 1)

            def square_of(c, j):
                dve.wait_ge(relu_done, 8 * c + j + 1)
                dve.scalar_tensor_tensor(f_ps[j % 2][:, :], f_ps[j % 2][:, :], 0.0, relu[:, :], ALU.max,
                                         ALU.mult).then_inc(sq_done, 1)

            def h_lower(c, j):
                dve.wait_ge(hh_done, 8 * c + j + 1)
                at = (j % 4, slice(j // 4 * HALF, (j // 4 + 1) * HALF))
                dve.tensor_tensor(hl[:, at[0], at[1]], f_ps[j % 2][:, :], hh[:, at[0], at[1]].bitcast(F32),
                                  ALU.subtract).then_inc(hl_done, 1)

            def groups(c):
                for j in range(8):
                    square_of(c, j)
                    h_lower(c, j)
                    if j % 2 == 0:
                        w_lower(c, 4 + j // 2)

            def add(c, t):
                dve.wait_ge(y_mm, NT * c + t + 1)
                dve.tensor_tensor(acc[:, t, :], y_ps[t % 2][:, :, :].rearrange("p a n -> p (a n)"), acc[:, t, :],
                                  ALU.add).then_inc(y_added, 1)

            for n in range(4):
                w_lower(0, n)
            groups(0)
            for i in range(2):
                dve.wait_ge(x_in[i], 16)
            with dve.Fori(1, NC) as c:
                for t in range(NT):
                    add(c - 1, t)
                    if t < 4:
                        w_lower(c, t)
                groups(c)
            dve.wait_ge(final_in, 16)
            for t in range(NT):
                add(NC - 1, t)
                if t:
                    dve.wait_ge(rms_done, t)
                    dve.scalar_tensor_tensor(acc[:, t - 1, :], acc[:, t - 1, :], rms[:, t - 1:t], raw[:, 0, :],
                                             ALU.mult, ALU.mult).then_inc(fin_done, 1)
            dve.wait_ge(rms_done, NT)
            dve.scalar_tensor_tensor(acc[:, NT - 1, :], acc[:, NT - 1, :], rms[:, NT - 1:NT], raw[:, 0, :],
                                     ALU.mult, ALU.mult).then_inc(fin_done, 1)

        @block.tensor
        def _(pe):
            def inner(c, j):
                first = type(c) is int and c == 0
                if j >= 2 or not first:
                    pe.wait_ge(hl_done, 8 * c + j - 1)
                f, half = j % 4, j // 4
                for kt in range(KT):
                    if first and j == 0 and kt % 2 == 0:
                        pe.wait_ge(wl_done, kt // 2 + 1)
                    for i, (a, b) in enumerate(((w1l, xh), (w1h, xl), (w1h, xh))):
                        last = pe.matmul(f_ps[j % 2][:, :], a[:, kt, f * P:(f + 1) * P], b[:, kt, half * HALF:(half + 1) * HALF],
                                         start=(kt == 0 and i == 0), stop=(kt == KT - 1 and i == 2))
                last.then_inc(f_mm, 1)

            def outer(c, t):
                if t % 4 == 0:
                    pe.wait_ge(hl_done, 8 * c + t + 4)
                if t >= 2 or type(c) is not int:
                    pe.wait_ge(y_added, NT * c + t - 1)
                for f in range(FT):
                    for n in range(2):
                        for i, (a, b) in enumerate(((hl, w2h), (hh, w2l), (hh, w2h))):
                            last = pe.matmul(y_ps[t % 2][:, n, :], a[:, f, t * P:(t + 1) * P], b[:, f, n * HALF:(n + 1) * HALF],
                                             start=(f == 0 and i == 0), stop=(f == FT - 1 and i == 2))
                last.then_inc(y_mm, 1)

            for j in range(8):
                inner(0, j)
            pe.wait_ge(wl_done, 8)
            for t in range(NT):
                outer(0, t)
            with pe.Fori(1, NC) as c:
                pe.wait_ge(wl_done, 8 * c + 4)
                for j in range(8):
                    inner(c, j)
                pe.wait_ge(wl_done, 8 * c + 8)
                for t in range(NT):
                    outer(c, t)


GAIN_TILES = {"g_pre_a": KT, "gn_gain_a": RET_W // P, "g_kv": KT, "g_pre_b": KT, "g_latents": (KV_LORA + Q_LORA) // P,
              "g_mix": KT, "g_onorm": GV // P, "g_ffn": KT}
GAINS = {name: (sum(list(GAIN_TILES.values())[:n]), sum(list(GAIN_TILES.values())[:n + 1]))
         for n, name in enumerate(GAIN_TILES)}


def build(nc, t, out):
    def scratch(name, shape):
        return nc.dram_tensor(name, shape, F32).ap()

    gated_a = scratch("gated_a", (SEQ, RET_W))
    x1 = scratch("x1", (SEQ, DM))
    silu_gate = scratch("silu_gate", (DM, SEQ))
    gated_b = scratch("gated_b", (DM, SEQ))
    x2 = scratch("x2", (SEQ, DM))
    gated_c = scratch("gated_c", (SEQ, DM))
    x3 = scratch("x3", (SEQ, DM))
    con = {name[4:]: ap for name, ap in t.items() if name.startswith("con_")}

    def rows(w, n):
        return w[n * P:(n + 1) * P, :]

    def pieces(w, n, k):
        return w[0, :, n * k:(n + 1) * k, :].rearrange("p k n -> p (k n)")

    with ExitStack() as whole:
        ident = whole.enter_context(nc.sbuf_tensor("ident", [P, P], F32))
        neghalf = whole.enter_context(nc.sbuf_tensor("neghalf", [P, 1], F32))
        gains = whole.enter_context(nc.sbuf_tensor("gains", [P, t["gains"].shape[1]], F32))
        staging = whole.enter_context(nc.sbuf_tensor("staging", [P, 2, DM], F32))
        arrived = {stage: [whole.enter_context(nc.semaphore(f"{stage}_arrived{i}")) for i in range(2)]
                   for stage in ("close_a", "latents", "close_b", "gla", "close_c", "ffn")}
        const_in = whole.enter_context(nc.semaphore("const_in"))
        neghalf_set = whole.enter_context(nc.semaphore("neghalf_set"))

        def loads(stage, tiles):
            def ahead(sp):
                for i, tile in enumerate(tiles):
                    sp.dma_start(staging[:, i, :], tile).then_inc(arrived[stage][i], 16)
            return ahead

        def gain(name):
            return gains[:, GAINS[name][0]:GAINS[name][1]]

        with nc.Block() as block:
            @block.sync
            def _(sp):
                sp.dma_start(ident[:], con["identity"]).then_inc(const_in, 16)
                sp.dma_start(gains[:], t["gains"]).then_inc(const_in, 16)
                sp.wait_ge(const_in, 32)

            @block.vector
            def _(dve):
                dve.memset(neghalf[:], -0.5).then_inc(neghalf_set, 1)

        used = retention_heads(nc, t["x"], gain("g_pre_a"), t["w_in_a"], con, ident, neghalf, staging,
                               loads("close_a", [rows(t["w_out_a"], i) for i in range(2)]), gated_a)
        used += close_mixer(nc, "wa_", gated_a, t["w_out_a"], gain("gn_gain_a"), t["x"], t["g_post_a"], ident, neghalf,
                            staging, arrived["close_a"], loads("latents", [rows(x1, i) for i in range(2)]), x1)

        with ExitStack() as ctx:
            def sb(name, shape, dt=F32):
                return ctx.enter_context(nc.sbuf_tensor(name, shape, dt))

            kv = sb("kv_upper", [P, 3, SEQ], F32R), sb("kv_lower", [P, 3, SEQ], F32R)
            cq = sb("cq_upper", [P, 3, SEQ], F32R), sb("cq_lower", [P, 3, SEQ], F32R)
            spare = sb("gate_upper", [P, KT, HALF], F32R), sb("gate_lower", [P, KT, HALF], F32R)
            used += latents(nc, x1, gain("g_kv"), gain("g_pre_b"), t["w_latents"], t["w_gate_b"], gain("g_latents"),
                            t["w_units_b"], con, ident, neghalf, kv, cq, spare, staging, arrived["latents"], silu_gate)
            used += attention(nc, kv, cq, spare, gain("g_latents"), t["w_heads_b"], silu_gate, con, ident, staging,
                              loads("close_b", [rows(t["w_out_b"], i) for i in range(2)]), gated_b)
        clear_semaphores(nc, used)

        xT = tuple(whole.enter_context(nc.sbuf_tensor(name, [P, KT, SEQ], F32R)) for name in ("x_upper", "x_lower"))
        close_mixer(nc, "wb_", gated_b, t["w_out_b"], None, x1, t["g_post_b"], ident, neghalf, staging, arrived["close_b"],
                    loads("gla", [pieces(t["w_qk_c"], i, 4) for i in range(2)]), x2, feature_major=True, xT=xT)

        gla_heads(nc, xT, gain("g_mix"), t["w_qk_c"], t["w_vr_c"], t["w_low_c"], t["w_gk_up"], t["b_gk"], con["gla_masks"],
                  ident, neghalf, staging, arrived["gla"], loads("close_c", [rows(t["w_out_c"], i) for i in range(2)]),
                  gated_c)
        close_mixer(nc, "wc_", gated_c, t["w_out_c"], gain("g_onorm"), x2, None, ident, neghalf, staging,
                    arrived["close_c"], loads("ffn", [pieces(t["w_ff1"], i, 2) for i in range(2)]), x3, xT=xT)
        feed_forward(nc, x3, xT, gain("g_ffn"), t["w_ff1"], t["w_ff2"], t["g_final"], ident, neghalf, staging,
                     arrived["ffn"], out)


def lay_out(i):
    w_qk, w_vr, w_low = gla_columns(i["l0_w_in_2"])
    gains = {"g_pre_a": i["g_pre_a"][0], "gn_gain_a": i["gn_gain_a"][0], "g_kv": i["g_kv"], "g_pre_b": i["g_pre_b"][0],
             "g_latents": np.concatenate([i["g_kv_lat"], i["g_q_lat"][0]]), "g_mix": i["l0_norm_mix_2"],
             "g_onorm": i["l0_g_onorm_2"], "g_ffn": i["l0_norm_ffn_2"]}
    arrays = {
        "gains": np.concatenate([columns(gains[name]) for name in GAINS], axis=1),
        "x": i["x"][0], "w_in_a": retention_columns(i["w_in_a"][0]),
        "w_out_a": i["w_out_a"][0], "g_post_a": i["g_post_a"][0],
        "w_latents": latent_columns(i["w_kv_a"], i["w_in_b"][0]), "w_gate_b": gate_units(i["w_in_b"][0]),
        "w_units_b": values_and_rotary_units(i["w_uv"], i["w_uq"][0]),
        "w_heads_b": head_weights(i["w_uk"], i["w_uq"][0]),
        "w_out_b": i["w_out_b"][0], "g_post_b": i["g_post_b"][0],
        "w_qk_c": w_qk, "w_vr_c": w_vr, "w_low_c": w_low,
        "w_gk_up": i["l0_w_gk_up_2"], "b_gk": columns(i["l0_b_gk_2"]),
        "w_out_c": i["l0_w_out_2"], "w_ff1": ff1_chunks(i["l0_w_ff1_2"]),
        "w_ff2": i["l0_w_ff2_2"], "g_final": i["final_norm_2"],
    }
    for name, value in shape_constants().items():
        arrays["con_" + name] = value
    return {name: np.ascontiguousarray(a) for name, a in arrays.items()}


def kernel(**inputs):
    import numpy as _np
    import concourse.bacc as _bacc
    from concourse.bass_utils import run_bass_kernel_spmd as _run

    nc = _bacc.Bacc("TRN2", target_bir_lowering=False, num_devices=1)
    laid = lay_out({name: _np.asarray(a) for name, a in inputs.items()})
    arrays = {"in_" + name: a for name, a in laid.items()}
    tensors = {name: nc.dram_tensor("in_" + name, a.shape, mybir.dt.from_np(a.dtype), kind="ExternalInput").ap()
               for name, a in laid.items()}
    out = nc.dram_tensor("out_0", (SEQ, DM), F32, kind="ExternalOutput").ap()
    build(nc, tensors, out)
    r = _run(nc, [arrays], core_ids=[0])
    return r.results[0]["out_0"].reshape(1, SEQ, DM)
```
